# Optimizing a Trainium2 kernel written in Bass

```python
import jax
import jax.numpy as jnp
from jax import lax
import numpy as np
import math
import jax, jax.numpy as jnp

D_MODEL = 1024
BATCH = 1
SEQ = 512
DEPTH = 2

GLA_HEADS = 4
GLA_DK = 64
GLA_DV = 128
GLA_GATE_RANK = 16
GLA_GATE_TEMP = 16.0
GLA_CHUNK = 64
NSA_HEADS = 8
NSA_KV_GROUPS = 2
NSA_HPG = NSA_HEADS // NSA_KV_GROUPS
NSA_DH = 64
NSA_CMP_BLOCK = 32
NSA_CMP_STRIDE = 16
NSA_CMP_HIDDEN = 128
NSA_SEL_BLOCK = 64
NSA_TOPN = 16
NSA_WINDOW = 512
NSA_QBLOCK = 128
NSA_BRANCHES = 3
SGU_WIDTH = 2 * D_MODEL
SGU_GROUPS = 8
SGU_CHUNK = 128
FFN_HIDDEN = 4 * D_MODEL
NORM_EPS = 1e-6
NEG_BIG = -1e30
POS_BIG = 1e30

EVEN_PROJ_SIZES = (GLA_HEADS * GLA_DK, GLA_HEADS * GLA_DK, GLA_HEADS * GLA_DV, GLA_GATE_RANK, GLA_HEADS * GLA_DV, NSA_HEADS * NSA_DH, NSA_KV_GROUPS * NSA_DH, NSA_KV_GROUPS * NSA_DH, NSA_KV_GROUPS * NSA_DH, NSA_KV_GROUPS * NSA_DH, NSA_KV_GROUPS * NSA_DH, NSA_KV_GROUPS * NSA_DH, NSA_HEADS * NSA_BRANCHES)
EVEN_PROJ_WIDTH = sum(EVEN_PROJ_SIZES)
EVEN_MIX_WIDTH = GLA_HEADS * GLA_DV + NSA_HEADS * NSA_DH


def _rms_norm(x, g):
    xf = x.astype(jnp.float32)
    y = xf * lax.rsqrt(jnp.mean(xf * xf, axis=-1, keepdims=True) + NORM_EPS)
    return (y * g).astype(x.dtype)

def _masked_softmax(s, mask):
    m = mask.astype(jnp.float32)
    s = jnp.where(mask, s, NEG_BIG)
    p = jnp.exp(s - jnp.max(s, axis=-1, keepdims=True)) * m
    return p / jnp.maximum(jnp.sum(p, axis=-1, keepdims=True), 1e-30)

def _squared_relu_mlp(x, w1, w2):
    h = jax.nn.relu(x @ w1)
    return (h * h) @ w2

def _gla(q, k, v, g_lr, r, w_gate, b_gate, norm_g):
    f32 = jnp.float32
    bsz, seq, _ = q.shape
    c = GLA_CHUNK
    nc = seq // c
    glog = jax.nn.log_sigmoid((g_lr @ w_gate + b_gate).astype(f32)) / GLA_GATE_TEMP

    def chunks(t, d):
        return t.astype(f32).reshape(bsz, nc, c, GLA_HEADS, d).transpose(0, 3, 1, 2, 4)

    qc = chunks(q, GLA_DK) * (GLA_DK ** -0.5)
    kc = chunks(k, GLA_DK)
    vc = chunks(v, GLA_DV)
    b = jnp.cumsum(chunks(glog, GLA_DK), axis=3)
    b_last = b[:, :, :, -1:, :]
    q_t = qc * jnp.exp(b)
    k_t = kc * jnp.exp(-b)
    k_end = kc * jnp.exp(b_last - b)
    causal = jnp.tril(jnp.ones((c, c), dtype=bool))
    a = jnp.where(causal, jnp.einsum('bhnid,bhnjd->bhnij', q_t, k_t), 0.0)
    o_intra = jnp.einsum('bhnij,bhnjv->bhniv', a, vc)
    ds = jnp.einsum('bhnjd,bhnjv->bhndv', k_end, vc)
    decay = jnp.exp(b_last[:, :, :, 0, :])

    def step(state, inp):
        dec, d = inp
        return dec[..., None] * state + d, state

    s0 = jnp.zeros((bsz, GLA_HEADS, GLA_DK, GLA_DV), f32)
    _, s_prev = lax.scan(step, s0, (jnp.moveaxis(decay, 2, 0), jnp.moveaxis(ds, 2, 0)))
    s_prev = jnp.moveaxis(s_prev, 0, 2)
    o = o_intra + jnp.einsum('bhnid,bhndv->bhniv', q_t, s_prev)
    o = o.transpose(0, 2, 3, 1, 4).reshape(bsz, seq, GLA_HEADS, GLA_DV)
    o = o * lax.rsqrt(jnp.mean(o * o, axis=-1, keepdims=True) + NORM_EPS) * norm_g
    o = o.reshape(bsz, seq, GLA_HEADS * GLA_DV) * jax.nn.silu(r.astype(f32))
    return o.astype(q.dtype)

def _nsa(q, kc, vc, ks, vs, kw, vw, gate_logits, cmp_pos, cmp_w1, cmp_w2):
    f32 = jnp.float32
    bsz, seq, _ = q.shape
    g_n, hpg, dh, qb_len, w = NSA_KV_GROUPS, NSA_HPG, NSA_DH, NSA_QBLOCK, NSA_WINDOW
    n_qb = seq // qb_len
    n_cmp = (seq - NSA_CMP_BLOCK) // NSA_CMP_STRIDE + 1
    n_sel = seq // NSA_SEL_BLOCK
    topn = min(NSA_TOPN, n_sel)
    scale = dh ** -0.5

    def kv_heads(t):
        return t.reshape(bsz, seq, g_n, dh)

    cmp_idx = jnp.arange(n_cmp)[:, None] * NSA_CMP_STRIDE + jnp.arange(NSA_CMP_BLOCK)[None, :]

    def compress(t, i):
        blocks = kv_heads(t)[:, cmp_idx] + cmp_pos[i][None, None, :, None, :]
        blocks = blocks.transpose(0, 3, 1, 2, 4).reshape(bsz, g_n, n_cmp, NSA_CMP_BLOCK * dh)
        return jax.nn.gelu(blocks @ cmp_w1[i]) @ cmp_w2[i]

    k_cmp = compress(kc, 0)
    v_cmp = compress(vc, 1)
    cmp_start = jnp.arange(n_cmp) * NSA_CMP_STRIDE
    cmp_end = cmp_start + NSA_CMP_BLOCK - 1
    sel_start = jnp.arange(n_sel) * NSA_SEL_BLOCK
    overlap = ((cmp_start[:, None] < sel_start[None, :] + NSA_SEL_BLOCK)
               & (cmp_start[:, None] + NSA_CMP_BLOCK > sel_start[None, :])).astype(f32)

    k_sel = kv_heads(ks).reshape(bsz, n_sel, NSA_SEL_BLOCK, g_n, dh).transpose(0, 3, 1, 2, 4)
    v_sel = kv_heads(vs).reshape(bsz, n_sel, NSA_SEL_BLOCK, g_n, dh).transpose(0, 3, 1, 2, 4)
    pad = ((0, 0), (0, 0), (w, 0), (0, 0))
    k_win = jnp.pad(kv_heads(kw).transpose(0, 2, 1, 3), pad)
    v_win = jnp.pad(kv_heads(vw).transpose(0, 2, 1, 3), pad)

    qb = (q * scale).reshape(bsz, n_qb, qb_len, g_n, hpg, dh).transpose(1, 0, 3, 4, 2, 5)
    gb = jax.nn.sigmoid(gate_logits.astype(f32)).reshape(bsz, n_qb, qb_len, g_n, hpg, NSA_BRANCHES)
    gb = gb.transpose(1, 0, 3, 4, 2, 5)
    b_ix = jnp.arange(bsz)[:, None, None, None]
    g_ix = jnp.arange(g_n)[None, :, None, None]
    within = jnp.arange(NSA_SEL_BLOCK)
    win_off = jnp.arange(qb_len + w)
    sel_j = jnp.arange(n_sel)

    def block(args):
        n, qn, gn = args
        t = n * qb_len + jnp.arange(qb_len)
        s_c = jnp.einsum('bghqd,bgcd->bghqc', qn, k_cmp).astype(f32)
        p_c = _masked_softmax(s_c, cmp_end[None, :] <= t[:, None])
        o_c = jnp.einsum('bghqc,bgcd->bghqd', p_c.astype(v_cmp.dtype), v_cmp)
        imp = jnp.einsum('bgqc,cj->bgqj', jnp.sum(p_c, axis=2), overlap)
        cur = t // NSA_SEL_BLOCK
        forced = (sel_j[None, :] == 0) | (sel_j[None, :] == cur[:, None]) | (sel_j[None, :] == cur[:, None] - 1)
        allowed = sel_start[None, :] <= t[:, None]
        score = jnp.where(forced, POS_BIG, jnp.where(allowed, imp, NEG_BIG))
        top_val, top_idx = lax.top_k(score, topn)
        blk_ok = top_val > 0.5 * NEG_BIG
        k_g = k_sel[b_ix, g_ix, top_idx]
        v_g = v_sel[b_ix, g_ix, top_idx]
        kpos = top_idx[..., None] * NSA_SEL_BLOCK + within
        ok = blk_ok[..., None] & (kpos <= t[None, None, :, None, None])
        s_s = jnp.einsum('bghqd,bgqnkd->bghqnk', qn, k_g).astype(f32)
        s_s = s_s.reshape(bsz, g_n, hpg, qb_len, topn * NSA_SEL_BLOCK)
        p_s = _masked_softmax(s_s, ok.reshape(bsz, g_n, 1, qb_len, topn * NSA_SEL_BLOCK))
        p_s = p_s.reshape(bsz, g_n, hpg, qb_len, topn, NSA_SEL_BLOCK).astype(v_g.dtype)
        o_s = jnp.einsum('bghqnk,bgqnkd->bghqd', p_s, v_g)
        k_w = lax.dynamic_slice_in_dim(k_win, n * qb_len, qb_len + w, axis=2)
        v_w = lax.dynamic_slice_in_dim(v_win, n * qb_len, qb_len + w, axis=2)
        kpos_w = n * qb_len - w + win_off
        ok_w = (kpos_w[None, :] >= 0) & (kpos_w[None, :] <= t[:, None]) & (kpos_w[None, :] > t[:, None] - w)
        s_w = jnp.einsum('bghqd,bgkd->bghqk', qn, k_w).astype(f32)
        p_w = _masked_softmax(s_w, ok_w)
        o_w = jnp.einsum('bghqk,bgkd->bghqd', p_w.astype(v_w.dtype), v_w)
        out = gn[..., 0:1] * o_c + gn[..., 1:2] * o_s + gn[..., 2:3] * o_w
        return out.astype(q.dtype)

    o = lax.map(block, (jnp.arange(n_qb), qb, gb))
    return o.transpose(1, 0, 4, 2, 3, 5).reshape(bsz, seq, NSA_HEADS * dh)

def _even_mixer(x, w_in, w_out, gla_w_gate, gla_b_gate, gla_norm, nsa_gate_b, nsa_cmp_pos, nsa_cmp_w1, nsa_cmp_w2):
    offsets = [int(o) for o in np.cumsum(EVEN_PROJ_SIZES)[:-1]]
    gq, gk, gv, glr, gr, nq, kc, vc, ks, vs, kw, vw, ng = jnp.split(x @ w_in, offsets, axis=-1)
    o_a = _gla(gq, gk, gv, glr, gr, gla_w_gate, gla_b_gate, gla_norm)
    o_b = _nsa(nq, kc, vc, ks, vs, kw, vw, ng + nsa_gate_b, nsa_cmp_pos, nsa_cmp_w1, nsa_cmp_w2)
    return jnp.concatenate([o_a, o_b], axis=-1) @ w_out

def _sgu_mixer(x, w_in, ln_g, ln_b, w_s, b_s, w_out):
    bsz, seq, _ = x.shape
    h = jax.nn.gelu(x @ w_in)
    u, v = jnp.split(h, 2, axis=-1)
    vf = v.astype(jnp.float32)
    mu = jnp.mean(vf, axis=-1, keepdims=True)
    var = jnp.mean((vf - mu) ** 2, axis=-1, keepdims=True)
    v = ((vf - mu) * lax.rsqrt(var + NORM_EPS) * ln_g + ln_b).astype(x.dtype)
    n_ch = seq // SGU_CHUNK
    v = v.reshape(bsz, n_ch, SGU_CHUNK, SGU_GROUPS, SGU_WIDTH // SGU_GROUPS)
    w_causal = jnp.where(jnp.tril(jnp.ones((SGU_CHUNK, SGU_CHUNK), dtype=bool)), w_s, 0.0)
    mixed = jnp.einsum('gts,bnsgc->bntgc', w_causal, v) + b_s.T[:, :, None]
    y = u * mixed.reshape(bsz, seq, SGU_WIDTH)
    return y @ w_out

def first_inputs(seed: int = 0) -> dict:
    key = jax.random.key(seed)
    k = jax.random.split(key, 20)
    ne = (DEPTH + 1) // 2
    no = DEPTH // 2
    f32 = jnp.float32

    def normal(kk, shape):
        return jax.random.normal(kk, shape, f32)

    def dense(kk, shape, fan_in):
        return normal(kk, shape) * (fan_in ** -0.5)

    return {
        'x': normal(k[0], (BATCH, SEQ, D_MODEL)),
        'norm_g': 1.0 + 0.05 * normal(k[1], (DEPTH, 4, D_MODEL)),
        'ffn_w1': dense(k[2], (DEPTH, D_MODEL, FFN_HIDDEN), D_MODEL),
        'ffn_w2': dense(k[3], (DEPTH, FFN_HIDDEN, D_MODEL), FFN_HIDDEN),
        'e_w_in': dense(k[4], (ne, D_MODEL, EVEN_PROJ_WIDTH), D_MODEL),
        'e_w_out': dense(k[5], (ne, EVEN_MIX_WIDTH, D_MODEL), EVEN_MIX_WIDTH),
        'gla_w_gate': dense(k[6], (ne, GLA_GATE_RANK, GLA_HEADS * GLA_DK), GLA_GATE_RANK),
        'gla_b_gate': 0.1 * normal(k[7], (ne, GLA_HEADS * GLA_DK)),
        'gla_norm': 1.0 + 0.05 * normal(k[8], (ne, GLA_HEADS, GLA_DV)),
        'nsa_gate_b': 0.1 * normal(k[9], (ne, NSA_HEADS * NSA_BRANCHES)),
        'nsa_cmp_pos': 0.1 * normal(k[10], (ne, 2, NSA_CMP_BLOCK, NSA_DH)),
        'nsa_cmp_w1': dense(k[11], (ne, 2, NSA_CMP_BLOCK * NSA_DH, NSA_CMP_HIDDEN), NSA_CMP_BLOCK * NSA_DH),
        'nsa_cmp_w2': dense(k[12], (ne, 2, NSA_CMP_HIDDEN, NSA_DH), NSA_CMP_HIDDEN),
        'o_w_in': dense(k[13], (no, D_MODEL, 2 * SGU_WIDTH), D_MODEL),
        'o_ln_g': 1.0 + 0.05 * normal(k[14], (no, SGU_WIDTH)),
        'o_ln_b': 0.02 * normal(k[15], (no, SGU_WIDTH)),
        'o_w_s': dense(k[16], (no, SGU_GROUPS, SGU_CHUNK, SGU_CHUNK), SGU_CHUNK),
        'o_b_s': 1.0 + 0.1 * normal(k[17], (no, SGU_GROUPS, SGU_CHUNK)),
        'o_w_out': dense(k[18], (no, SGU_WIDTH, D_MODEL), SGU_WIDTH),
    }

def first_block(x, norm_g, ffn_w1, ffn_w2, e_w_in, e_w_out, gla_w_gate, gla_b_gate, gla_norm, nsa_gate_b, nsa_cmp_pos, nsa_cmp_w1, nsa_cmp_w2, o_w_in, o_ln_g, o_ln_b, o_w_s, o_b_s, o_w_out):
    h = x
    for layer in range(DEPTH):
        i = layer // 2
        xn = _rms_norm(h, norm_g[layer, 0])
        if layer % 2 == 0:
            m = _even_mixer(xn, e_w_in[i], e_w_out[i], gla_w_gate[i], gla_b_gate[i], gla_norm[i],
                            nsa_gate_b[i], nsa_cmp_pos[i], nsa_cmp_w1[i], nsa_cmp_w2[i])
        else:
            m = _sgu_mixer(xn, o_w_in[i], o_ln_g[i], o_ln_b[i], o_w_s[i], o_b_s[i], o_w_out[i])
        h = h + _rms_norm(m, norm_g[layer, 1])
        f = _squared_relu_mlp(_rms_norm(h, norm_g[layer, 2]), ffn_w1[layer], ffn_w2[layer])
        h = h + _rms_norm(f, norm_g[layer, 3])
    return h


DEPTH_2 = 1

GRID_W = 64
HEAD_DIM = 64
NA_HEADS = 8
NA_KH_MAX = 8
NA_KW = 16
NA_WIDTH = NA_HEADS * HEAD_DIM
SWA_Q_HEADS = 8
SWA_KV_HEADS = 2
SWA_WINDOW = 128
SWA_BLOCK = 128
SWA_Q_WIDTH = SWA_Q_HEADS * HEAD_DIM
SWA_KV_WIDTH = SWA_KV_HEADS * HEAD_DIM
ROPE_THETA = 500000.0
ROPE_DIM = HEAD_DIM // 4
D_FF = 4 * D_MODEL
IN_WIDTH = 3 * NA_WIDTH + SWA_Q_WIDTH + 2 * SWA_KV_WIDTH + 2 * D_MODEL
IN_SPLITS = [
    NA_WIDTH,
    2 * NA_WIDTH,
    3 * NA_WIDTH,
    3 * NA_WIDTH + SWA_Q_WIDTH,
    3 * NA_WIDTH + SWA_Q_WIDTH + SWA_KV_WIDTH,
    3 * NA_WIDTH + SWA_Q_WIDTH + 2 * SWA_KV_WIDTH,
    3 * NA_WIDTH + SWA_Q_WIDTH + 2 * SWA_KV_WIDTH + D_MODEL,
]
DEEPNORM_ALPHA = (2.0 * DEPTH_2) ** 0.25
DEEPNORM_BETA = (8.0 * DEPTH_2) ** -0.25
LN_EPS = 1e-5
MASK_VALUE = -1e30


def layer_norm(x, g, b):
    xf = x.astype(jnp.float32)
    mu = jnp.mean(xf, axis=-1, keepdims=True)
    xc = xf - mu
    var = jnp.mean(xc * xc, axis=-1, keepdims=True)
    y = xc * lax.rsqrt(var + LN_EPS) * g.astype(jnp.float32) + b.astype(jnp.float32)
    return y.astype(x.dtype)

def partial_rotary(x, pos):
    half = ROPE_DIM // 2
    inv_freq = jnp.power(ROPE_THETA, -jnp.arange(0, ROPE_DIM, 2, dtype=jnp.float32) / ROPE_DIM)
    ang = pos.astype(jnp.float32)[:, None] * inv_freq[None, :]
    cos = jnp.cos(ang)[:, None, :]
    sin = jnp.sin(ang)[:, None, :]
    xr = x[..., :ROPE_DIM].astype(jnp.float32)
    x1, x2 = xr[..., :half], xr[..., half:]
    rot = jnp.concatenate([x1 * cos - x2 * sin, x2 * cos + x1 * sin], axis=-1)
    return jnp.concatenate([rot.astype(x.dtype), x[..., ROPE_DIM:]], axis=-1)

def neighbourhood_attention(q, k, v, rpb):
    B, S, H, Dh = q.shape
    rows = S // GRID_W
    kh = min(NA_KH_MAX, rows)
    kw = NA_KW
    qg = q.reshape(B, rows, GRID_W, H, Dh)
    kg = k.reshape(B, rows, GRID_W, H, Dh)
    vg = v.reshape(B, rows, GRID_W, H, Dh)
    cols = jnp.arange(GRID_W)
    col_start = jnp.clip(cols - kw // 2, 0, GRID_W - kw)
    col_idx = col_start[:, None] + jnp.arange(kw)[None, :]
    dc = col_idx - cols[:, None]
    scale = Dh ** -0.5

    def one_row(r):
        rs = jnp.clip(r - kh // 2, 0, rows - kh)
        kr = lax.dynamic_slice_in_dim(kg, rs, kh, axis=1)
        vr = lax.dynamic_slice_in_dim(vg, rs, kh, axis=1)
        kn = kr[:, :, col_idx]
        vn = vr[:, :, col_idx]
        qr = lax.dynamic_index_in_dim(qg, r, axis=1, keepdims=False)
        s = jnp.einsum('bwhd,bkwjhd->bhwkj', qr, kn).astype(jnp.float32) * scale
        dr = rs + jnp.arange(kh) - r
        bias = rpb[:, (dr + NA_KH_MAX - 1)[None, :, None], (dc + kw - 1)[:, None, :]]
        s = s + bias.astype(jnp.float32)[None]
        p = jax.nn.softmax(s.reshape(B, H, GRID_W, kh * kw), axis=-1)
        p = p.reshape(B, H, GRID_W, kh, kw).astype(v.dtype)
        return jnp.einsum('bhwkj,bkwjhd->bwhd', p, vn)

    out = lax.map(one_row, jnp.arange(rows))
    return jnp.moveaxis(out, 0, 1).reshape(B, S, H * Dh)

def windowed_gqa_with_sink(q, k, v, sink):
    B, S, Hq, Dh = q.shape
    G = k.shape[2]
    rep = Hq // G
    blk = SWA_BLOCK
    nb = S // blk
    qb = q.reshape(B, nb, blk, G, rep, Dh)
    pad = ((0, 0), (blk, blk), (0, 0), (0, 0))
    kp = jnp.pad(k, pad).reshape(B, nb + 2, blk, G, Dh)
    vp = jnp.pad(v, pad).reshape(B, nb + 2, blk, G, Dh)
    kb = jnp.concatenate([kp[:, :-2], kp[:, 1:-1], kp[:, 2:]], axis=2)
    vb = jnp.concatenate([vp[:, :-2], vp[:, 1:-1], vp[:, 2:]], axis=2)
    s = jnp.einsum('bnqgrd,bnkgd->bngrqk', qb, kb).astype(jnp.float32) * (Dh ** -0.5)
    qpos = jnp.arange(nb)[:, None] * blk + jnp.arange(blk)[None, :]
    kpos = jnp.arange(nb)[:, None] * blk - blk + jnp.arange(3 * blk)[None, :]
    rel = kpos[:, None, :] - qpos[:, :, None]
    valid = (jnp.abs(rel) <= SWA_WINDOW) & (kpos[:, None, :] >= 0) & (kpos[:, None, :] < S)
    s = jnp.where(valid[None, :, None, None], s, MASK_VALUE)
    sink_l = sink.astype(jnp.float32).reshape(1, 1, G, rep, 1, 1)
    m = jnp.maximum(jnp.max(s, axis=-1, keepdims=True), sink_l)
    e = jnp.exp(s - m)
    p = e / (jnp.sum(e, axis=-1, keepdims=True) + jnp.exp(sink_l - m))
    o = jnp.einsum('bngrqk,bnkgd->bnqgrd', p.astype(v.dtype), vb)
    return o.reshape(B, S, Hq * Dh)

def second_inputs(seed: int = 0) -> dict:
    key = jax.random.key(seed)
    ks = jax.random.split(key, 24)
    f32 = jnp.float32
    beta = DEEPNORM_BETA

    def nrm(k, shape, scale):
        return jax.random.normal(k, shape, f32) * scale

    col_scale = jnp.concatenate([
        jnp.ones((2 * NA_WIDTH,), f32), jnp.full((NA_WIDTH,), beta, f32),
        jnp.ones((SWA_Q_WIDTH + SWA_KV_WIDTH,), f32), jnp.full((SWA_KV_WIDTH,), beta, f32),
        jnp.ones((2 * D_MODEL,), f32)])
    w_in = nrm(ks[1], (DEPTH_2, D_MODEL, IN_WIDTH), D_MODEL ** -0.5) * col_scale
    return {
        "x": jax.random.normal(ks[0], (BATCH, SEQ, D_MODEL), f32),
        "ln0_g": 1.0 + nrm(ks[2], (D_MODEL,), 0.05),
        "ln0_b": nrm(ks[3], (D_MODEL,), 0.02),
        "w_in": w_in,
        "b_in": nrm(ks[4], (DEPTH_2, IN_WIDTH), 0.02),
        "na_rpb": nrm(ks[5], (DEPTH_2, NA_HEADS, 2 * NA_KH_MAX - 1, 2 * NA_KW - 1), 0.1),
        "swa_sink": nrm(ks[6], (DEPTH_2, SWA_Q_HEADS), 0.5),
        "w_branch_na": nrm(ks[7], (DEPTH_2, NA_WIDTH, D_MODEL), NA_WIDTH ** -0.5 * beta),
        "w_branch_swa": nrm(ks[8], (DEPTH_2, SWA_Q_WIDTH, D_MODEL), SWA_Q_WIDTH ** -0.5 * beta),
        "w_out": nrm(ks[9], (DEPTH_2, D_MODEL, D_MODEL), D_MODEL ** -0.5 * beta),
        "b_out": nrm(ks[10], (DEPTH_2, D_MODEL), 0.02),
        "ln1_g": 1.0 + nrm(ks[11], (DEPTH_2, D_MODEL), 0.05),
        "ln1_b": nrm(ks[12], (DEPTH_2, D_MODEL), 0.02),
        "w_ff1": nrm(ks[13], (DEPTH_2, D_MODEL, D_FF), D_MODEL ** -0.5 * beta),
        "b_ff1": nrm(ks[14], (DEPTH_2, D_FF), 0.02),
        "w_ff2": nrm(ks[15], (DEPTH_2, D_FF, D_MODEL), D_FF ** -0.5 * beta),
        "b_ff2": nrm(ks[16], (DEPTH_2, D_MODEL), 0.02),
        "ln2_g": 1.0 + nrm(ks[17], (DEPTH_2, D_MODEL), 0.05),
        "ln2_b": nrm(ks[18], (DEPTH_2, D_MODEL), 0.02),
    }

def second_block(x, ln0_g, ln0_b, w_in, b_in, na_rpb, swa_sink, w_branch_na, w_branch_swa,
              w_out, b_out, ln1_g, ln1_b, w_ff1, b_ff1, w_ff2, b_ff2, ln2_g, ln2_b):
    B, S, _ = x.shape
    pos = jnp.arange(S)
    h = layer_norm(x, ln0_g, ln0_b)
    for l in range(DEPTH_2):
        proj = h @ w_in[l] + b_in[l]
        qa, ka, va, qb, kb, vb, ga, gb = jnp.split(proj, IN_SPLITS, axis=-1)
        qa = qa.reshape(B, S, NA_HEADS, HEAD_DIM)
        ka = ka.reshape(B, S, NA_HEADS, HEAD_DIM)
        va = va.reshape(B, S, NA_HEADS, HEAD_DIM)
        qb = partial_rotary(qb.reshape(B, S, SWA_Q_HEADS, HEAD_DIM), pos)
        kb = partial_rotary(kb.reshape(B, S, SWA_KV_HEADS, HEAD_DIM), pos)
        vb = vb.reshape(B, S, SWA_KV_HEADS, HEAD_DIM)
        y_na = neighbourhood_attention(qa, ka, va, na_rpb[l]) @ w_branch_na[l]
        y_swa = windowed_gqa_with_sink(qb, kb, vb, swa_sink[l]) @ w_branch_swa[l]
        mixed = jax.nn.sigmoid(ga) * y_na + jax.nn.sigmoid(gb) * y_swa
        attn_out = mixed @ w_out[l] + b_out[l]
        h = layer_norm(DEEPNORM_ALPHA * h + attn_out, ln1_g[l], ln1_b[l])
        u = jnp.square(jax.nn.relu(h @ w_ff1[l] + b_ff1[l]))
        ffn_out = u @ w_ff2[l] + b_ff2[l]
        h = layer_norm(DEEPNORM_ALPHA * h + ffn_out, ln2_g[l], ln2_b[l])
    return h


def setup_inputs(seed=0):
    out = dict(first_inputs(seed))
    for name, value in second_inputs(seed + 1).items():
        if name != "x":
            out[name + "_2"] = value
    return out


def reference(
    x, norm_g, ffn_w1, ffn_w2, e_w_in, e_w_out, gla_w_gate, gla_b_gate, gla_norm, nsa_gate_b,
    nsa_cmp_pos, nsa_cmp_w1, nsa_cmp_w2, o_w_in, o_ln_g, o_ln_b, o_w_s, o_b_s, o_w_out, ln0_g_2,
    ln0_b_2, w_in_2, b_in_2, na_rpb_2, swa_sink_2, w_branch_na_2, w_branch_swa_2, w_out_2,
    b_out_2, ln1_g_2, ln1_b_2, w_ff1_2, b_ff1_2, w_ff2_2, b_ff2_2, ln2_g_2, ln2_b_2,
):
    x = first_block(
        x, norm_g, ffn_w1, ffn_w2, e_w_in, e_w_out, gla_w_gate, gla_b_gate, gla_norm,
        nsa_gate_b, nsa_cmp_pos, nsa_cmp_w1, nsa_cmp_w2, o_w_in, o_ln_g, o_ln_b, o_w_s, o_b_s,
        o_w_out,
    )
    return second_block(
        x, ln0_g_2, ln0_b_2, w_in_2, b_in_2, na_rpb_2, swa_sink_2, w_branch_na_2,
        w_branch_swa_2, w_out_2, b_out_2, ln1_g_2, ln1_b_2, w_ff1_2, b_ff1_2, w_ff2_2, b_ff2_2,
        ln2_g_2, ln2_b_2,
    )


_drawn_inputs = setup_inputs


def setup_inputs(seed=0):
    import zlib

    import numpy as np

    out = dict(_drawn_inputs(seed))
    spreads = {}
    factors = {'nsa_gate_b': 4.689,
     'o_ln_g': 3.8,
     'o_ln_b': 22.564,
     'ln0_b_2': 2.8,
     'b_in_2': 8.0,
     'na_rpb_2': 42.814,
     'swa_sink_2': 64.0,
     'b_out_2': 3.355,
     'ln1_b_2': 2.782,
     'b_ff1_2': 6.871,
     'b_ff2_2': 3.332,
     'ln2_b_2': 2.795}
    for name, (base, spread) in spreads.items():
        noise = np.random.default_rng([zlib.crc32(name.encode()), seed]).standard_normal(out[name].shape)
        drawn = base * np.exp(spread * noise) if base else spread * noise
        out[name] = jnp.asarray(drawn.astype(out[name].dtype))
    for name, factor in factors.items():
        out[name] = (out[name] * factor).astype(out[name].dtype)
    return out
```

```python
from contextlib import ExitStack

import numpy as np

import concourse.bass as bass
from concourse import mybir

F32 = mybir.dt.float32
F32R = mybir.dt.float32r
BF16 = mybir.dt.bfloat16
ACT = mybir.ActivationFunctionType
ALU = mybir.AluOpType
AX = mybir.AxisListType

P = 128
T = 512
TB = T // P
D = 1024
KC = D // P
FF = 4 * D
RING = 4
AHEAD = 3
NEG = -1e30
HD = 64
GLA_CHUNK = 64
CMP_BLOCK, CMP_STRIDE, N_CMP = 32, 16, 31
NA_W, NA_ROWS, NA_KW = 64, 8, 16
ROPE_HALF = 8
ALPHA = float(2.0 ** 0.25)

STAGES = [("mix0_in", 23), ("mix0_out", 8), ("ffn0", 64), ("sgu_in", 32), ("sgu_out", 16), ("ffn1", 64),
          ("mix2_in", 18), ("mix2_gate", 16), ("mix2_branch", 8),
          ("mix2_out", 8), ("ffn2", 64)]
BASE, NP = {}, 0
for _name, _n in STAGES:
    BASE[_name] = NP
    NP += _n

VEC, NV = {}, 0
for _name, _n in [("norm_g", 64), ("gla_b", 2), ("gla_norm", 4), ("nsa_gate_b", 1), ("ln0_g", 8), ("ln0_b", 8),
                  ("ln1_g", 8), ("ln1_b", 8), ("ln2_g", 8), ("ln2_b", 8), ("b_in", 34), ("b_out", 8),
                  ("b_ff1", 32), ("b_ff2", 8), ("sink", 8)]:
    VEC[_name] = NV
    NV += _n

CON, NC = {}, 0
for _name, _n in [("ident", P), ("ones", P), ("rot", P), ("low", P), ("up", P), ("scan", T), ("cmpneg", TB * 32),
                  ("cmpone", TB * 32), ("nacol", NA_W), ("eps6", 1), ("eps5", 1), ("one", 1)]:
    CON[_name] = NC
    NC += _n

ITEM, NI = {}, 0
for _name, _n in [("prep0", 8), ("gla", 4), ("nsa", 4), ("prep1", 8), ("prep2", 8), ("sgu", 16), ("prep3", 8),
                  ("ln0", 8), ("na", 4), ("swa", 4), ("mixed", 8), ("ln1", 8)]:
    ITEM[_name] = NI
    NI += _n

UNITS = []
for _t in range(TB):
    for _p in range(4):
        for _g in range(2):
            for _k in ("sel", "win"):
                UNITS.append((_k, _g, _p, _t, 0, (_t + 1) * P, 4 * _g + _p))
U_NA = len(UNITS)
for _t in range(TB):
    for _p in range(4):
        for _g in range(2):
            UNITS.append(("na", _g, _p, _t, 0, T, 2 * _p + _g))
U_SWA = len(UNITS)
for _t in range(TB):
    for _p in range(4):
        for _g in range(2):
            _lo, _hi = max(0, _t - 1) * P, min(TB, _t + 2) * P
            UNITS.append(("swa", _g, _p, _t, _lo, _hi - _lo, 4 * _g + _p))
NU = len(UNITS)
UNITS[U_NA:U_SWA] = sorted(UNITS[U_NA:U_SWA], key=lambda u: (u[6], u[3]))


def panel_reader(n):
    for name, first, count in [(s, BASE[s], c) for s, c in STAGES]:
        if first <= n < first + count:
            i = n - first
            if name.startswith("ffn"):
                return "act" if i % 16 < 8 else "dve"
            if name == "sgu_out":
                return "act" if i < 8 else "dve"
            return "dve" if name in ("mix2_branch", "mix2_out") else "act"
    raise AssertionError(n)


READS = {"act": [0], "dve": [0]}
for _n in range(NP):
    _r = panel_reader(_n)
    for _e in READS:
        READS[_e].append(READS[_e][-1] + (_r == _e))


NA_UNITS = U_SWA - U_NA
BESIDE = set(range(BASE["mix2_in"] + 12, BASE["mix2_branch"]))
BANK = [n % 2 if n in BESIDE else n % 4 for n in range(NP)]


def blocks_beside(i, count, units):
    return range(i * count * KC // units, (i + 1) * count * KC // units)


NA_END = [next(i for i in range(NA_UNITS) if KC * c + KC - 1 in blocks_beside(i, 6, NA_UNITS)) for c in range(6)]


def build(nc, stream, x, vec, con, rope, cmp_pos, cmp_w1, cmp_w2, gate_w, ln_gb, w_s, b_s, rpb, out, stop=None):
    with ExitStack() as ctx:
        sems = {}

        def sem(name):
            if name not in sems:
                sems[name] = ctx.enter_context(nc.semaphore(name))
            return sems[name]

        place = [16512]

        def keep(name, shape, dt=F32):
            size = int(np.prod(shape[1:])) * (2 if dt == BF16 else 4)
            size = -(-size // 32) * 32
            t = nc.alloc_sbuf_tensor_at(name, shape, dt, offset=place[0])
            place[0] += size
            return t

        h = keep("h", [P, KC, T])
        xa = keep("xa", [P, KC, 2, T], F32R)
        raw = keep("raw", [P, RING, KC * P])
        ring = keep("ring", [P, RING, 2, KC * P], F32R)
        xf_at = place[0]
        xf = keep("xf", [P, 4, T])
        sq = keep("sq", [P, 2, T])
        sd = keep("sd", [P, T])
        rs = keep("rs", [P, T])
        misc = keep("misc", [P, T])
        vecs = keep("vecs", [P, NV])
        cons = keep("cons", [P, NC])
        identb = keep("identb", [P, P], BF16)
        lowb = keep("lowb", [P, P], BF16)
        upb = keep("upb", [P, P], BF16)
        stat = keep("stat", [P, 12, 16])
        bn = keep("bn", [P, TB, 4, 6])
        bqa = keep("bqa", [P, 4])
        shared = place[0]

        def at(name, shape, kb, dt=F32):
            assert shared + int(kb * 1024) + int(np.prod(shape[1:])) * 4 <= nc.sbuf_usable_end, name
            return nc.alloc_sbuf_tensor_at(name, shape, dt, offset=shared + int(kb * 1024))

        xb = at("xb", [P, KC, 2, T], 0, F32R)
        acc = at("acc", [P, KC, T], 32)
        relu = at("relu", [P, 2, T], 48)
        ffsq = at("ffsq", [P, 2, T], 52)
        g_at = at("g_at", [P, 4, TB, P], 0)
        g_ke = at("g_ke", [P, 2, TB, 2, P], 8)
        g_v = at("g_v", [P, TB, T], 32)
        g_s = at("g_s", [P, 2 * TB, 2, P], 40)
        g_q = at("g_q", [P, 2, T], 48)
        g_k = at("g_k", [P, 2, T], 52)
        g_b = at("g_b", [P, 2, T], 56)
        g_t = at("g_t", [P, 2, T], 60)
        g_o = at("g_o", [P, TB, T], 56)
        g_r = at("g_r", [P, 4, T], 64)
        n_q = at("n_q", [P, 4, T], 16)
        n_c = at("n_c", [P, 2, T], 72)
        n_k = at("n_k", [P, 2, T], 24)
        n_v = at("n_v", [P, 2, TB, P], 28)
        c_w1 = [at("c_w1k", [P, CMP_BLOCK, P], 32), at("c_w1v", [P, CMP_BLOCK, P], 48)]
        c_bl = at("c_bl", [P, 2, CMP_BLOCK, 32], 64)
        c_s = at("c_s", [P, 2, TB, 4, 32], 32)
        c_e = at("c_e", [P, 2, TB, 4, 32], 36)
        c_pt = at("c_pt", [P, 2, TB, P], 40)
        c_g = at("c_g", [P, 2, 2, 32], 76)
        c_kc = at("c_kc", [P, 32], 76.5)
        c_vbd = at("c_vbd", [P, 2, 4, HD], 76.75)
        c_w2 = at("c_w2", [P, 2, HD], 78.75)
        c_pos = at("c_pos", [P, 2, CMP_BLOCK], 79.25)
        g_wg = at("g_wg", [16, 2 * P], 80)
        n_gate = at("n_gate", [P, TB, 24], 79.5)
        n_p = at("n_p", [P, 2, T], 48)
        n_pt = at("n_pt", [P, 2, T], 52)
        n_o = at("n_o", [P, TB, 8, HD], 56)
        v_tok = at("v_tok", [P, TB, 2 * D], 0)
        gb = at("gb", [P, 2, 2 * D], 32)
        u = at("u", [P, 2 * KC, T], 48)
        wst = at("wst", [P, 8, P], 80)
        bs = nc.alloc_sbuf_tensor_at("bs", [P, 8 * P], F32, offset=xf_at)
        ropes = at("ropes", [P, 2, T], 0)
        rtmp = at("rtmp", [P, 2, T], 4)
        rtmp2 = at("rtmp2", [P, 2, T], 8)
        t2 = at("t2", [P, 2, 14 * NA_W], 16)
        a_o = at("a_o", [P, TB, 8, HD], 24)
        a_q = at("a_q", [P, 4, T], 32)
        a_k = at("a_k", [P, 4, T], 40)
        a_v = at("a_v", [P, TB, T], 48)
        w_q = at("w_q", [P, 4, T], 56)
        w_k = at("w_k", [P, 1, T], 64)
        w_v = at("w_v", [P, TB, P], 66)
        a_p = at("a_p", [P, 2, T], 68)
        a_pt = at("a_pt", [P, 2, T], 72)
        a_s = at("a_s", [P, 2, T], 76)
        w_o = at("w_o", [P, TB, 8, HD], 76)
        sig = at("sig", [P, 2 * KC, T], 32)

        ps = [ctx.enter_context(nc.psum_tensor(f"ps{i}", [P, T], F32)) for i in range(8)]

        ident = cons[:, CON["ident"]:CON["ident"] + P]
        ones = cons[:, CON["ones"]:CON["ones"] + P]

        def col(table, i=0):
            return vecs[:, VEC[table] + i:VEC[table] + i + 1]

        def con_col(name):
            return cons[:, CON[name]:CON[name] + 1]

        landed = [sem(f"landed{s}") for s in range(RING)]
        hi_done, lo_done = sem("hi_done"), sem("lo_done")
        panel_done = sem("panel_done")
        taken = {"act": sem("act_taken"), "dve": sem("dve_taken")}
        setup = sem("setup")

        def act_split(act, n, more=0, panels_more=0):
            m = n + AHEAD
            if m >= NP:
                return
            act.wait_ge(landed[m % RING], 16 * (m // RING + 1) + more)
            if m >= RING:
                act.wait_ge(panel_done, m - RING + 1 + panels_more)
            nc.scalar.activation(ring[:, m % RING, 0], raw[:, m % RING], ACT.Copy).then_inc(hi_done, 1)

        def dve_split(dve, n, more=0):
            m = n + AHEAD
            if m >= NP:
                return
            dve.wait_ge(hi_done, m + 1 + more)
            nc.vector.tensor_tensor(ring[:, m % RING, 1], raw[:, m % RING], ring[:, m % RING, 0].bitcast(F32),
                                    ALU.subtract).then_inc(lo_done, 1)

        def pe_free(pe, n, more=0):
            before = [m for m in range(max(0, n - 8), n) if BANK[m] == BANK[n]]
            if before:
                r = panel_reader(before[-1])
                pe.wait_ge(taken[r], READS[r][before[-1] + 1] + more)

        def pe_panel(pe, n, operand, ready=None, more=0, free_more=0, blocks=range(KC), bank=None, free=True,
                     last=True):
            if free:
                pe_free(pe, n, free_more)
            pe.wait_ge(lo_done, n + 1 + more)
            bank = ps[BANK[n]] if bank is None else bank
            blocks = list(blocks)
            for i, k in enumerate(blocks):
                if ready is not None:
                    pe.wait_ge(ready[0], ready[1] + k + 1)
                for w, xx in ((0, 0), (0, 1), (1, 0)):
                    mm = nc.tensor.matmul(bank[:, :], ring[:, n % RING, w, k * P:(k + 1) * P], operand[:, k, xx],
                                          start=(i == 0 and w == 0 and xx == 0),
                                          stop=(i == len(blocks) - 1 and w == 1))
            if last:
                mm.then_inc(panel_done, 1)

        class Chain:

            def __init__(self, eng, name):
                self.eng, self.sem, self.n = eng, sem(name), 0

            def __call__(self, ins):
                self.n += 1
                ins.then_inc(self.sem, 1)
                self.eng.wait_ge(self.sem, self.n)

        def act_item(act, i, dst, src):
            act.wait_ge(sem("xf_ready"), i + 1)
            nc.scalar.activation(dst[:, 0], src, ACT.Copy).then_inc(sem("xhi_ready"), 1)

        def pool_item(pool, i, dst, src):
            pool.wait_ge(sem("xhi_ready"), i + 1)
            nc.gpsimd.tensor_tensor(dst[:, 1], src, dst[:, 0].bitcast(F32), ALU.subtract).then_inc(sem("xlo_ready"), 1)

        def xf_free(dve, i):
            if i >= 4:
                dve.wait_ge(sem("xlo_ready"), i - 3)

        def item_ready(name):
            return (sem("xlo_ready"), ITEM[name])

        def act_squares(act, i, src, wait=None):
            for k in range(KC):
                if wait is not None:
                    act.wait_ge(wait[0], wait[1] + k + 1)
                if 8 * i + k >= 2:
                    act.wait_ge(sem("sq_summed"), 8 * i + k - 1)
                nc.scalar.activation(sq[:, k % 2], src[:, k], ACT.Square).then_inc(sem("sq_ready"), 1)

        def act_sd(act, i, eps):
            act.wait_ge(sem("sq_summed"), 8 * i + KC)
            nc.scalar.activation(sd[:, :], ps[4][:, :], ACT.Sqrt, scale=1.0 / D, bias=con_col(eps))\
                .then_inc(sem("sd_ready"), 1)

        def pe_squares(pe, i):
            for k in range(KC):
                pe.wait_ge(sem("sq_ready"), 8 * i + k + 1)
                nc.tensor.matmul(ps[4][:, :], ones, sq[:, k % 2], start=(k == 0), stop=(k == KC - 1))\
                    .then_inc(sem("sq_summed"), 1)

        def dve_rs(dve, i):
            dve.wait_ge(sem("sd_ready"), i + 1)
            nc.vector.reciprocal(rs[:, :], sd[:, :]).then_inc(sem("rs_ready"), 1)
            dve.wait_ge(sem("rs_ready"), i + 1)

        def dve_prep(dve, name, g):
            for k in range(KC):
                i = ITEM[name] + k
                xf_free(dve, i)
                nc.vector.scalar_tensor_tensor(out=xf[:, i % 4], in0=h[:, k], scalar=col("norm_g", g * KC + k),
                                               in1=rs[:, :], op0=ALU.mult, op1=ALU.mult)\
                    .then_inc(sem("xf_ready"), 1)

        def dve_post(dve, r, g):
            for k in range(KC):
                nc.vector.scalar_tensor_tensor(out=acc[:, k], in0=acc[:, k], scalar=col("norm_g", g * KC + k),
                                               in1=rs[:, :], op0=ALU.mult, op1=ALU.mult)\
                    .then_inc(sem("post_ready"), 1)

        def pool_residual(pool, r):
            for k in range(KC):
                pool.wait_ge(sem("post_ready"), 8 * r + k + 1)
                nc.gpsimd.tensor_tensor(h[:, k], h[:, k], acc[:, k], ALU.add).then_inc(sem("h_ready"), 1)

        def act_items(act, name, dst, src, n=KC, first=0):
            for k in range(n):
                act_item(act, ITEM[name] + k, dst[:, first + k], src(ITEM[name] + k))

        def pool_items(pool, name, dst, src, n=KC, first=0):
            for k in range(n):
                pool_item(pool, ITEM[name] + k, dst[:, first + k], src(ITEM[name] + k))

        def tile(i):
            return xf[:, i % 4]

        def pe_mean(pe, m, wait):
            for k in range(KC):
                pe.wait_ge(wait[0], wait[1] + k + 1)
                mm = nc.tensor.matmul(ps[5][:, :], ones, h[:, k], start=(k == 0), stop=(k == KC - 1))
            mm.then_inc(sem("mean_summed"), 1)

        def act_mean(act, m):
            act.wait_ge(sem("mean_summed"), m + 1)
            nc.scalar.activation(sd[:, :], ps[5][:, :], ACT.Copy, scale=1.0 / D).then_inc(sem("mean_ready"), 1)
            act_squares(act, 8 + m, h, (sem("centred"), 8 * m))
            act_sd(act, 8 + m, "eps5")

        def dve_ln(dve, m, name, g):
            dve.wait_ge(sem("mean_ready"), m + 1)
            for k in range(KC):
                nc.vector.tensor_tensor(h[:, k], h[:, k], sd[:, :], ALU.subtract).then_inc(sem("centred"), 1)
            dve_rs(dve, 8 + m)
            for k in range(KC):
                i = (ITEM[name] if name else NI) + k
                if name or k < 4:
                    xf_free(dve, i)
                else:
                    dve.wait_ge(sem("y_ready"), k - 3)
                nc.vector.scalar_tensor_tensor(out=xf[:, i % 4], in0=h[:, k], scalar=col(g, k), in1=rs[:, :],
                                               op0=ALU.mult, op1=ALU.mult).then_inc(sem("xf_ready"), 1)

        def act_ln_items(act, name, b):
            for k in range(KC):
                i = ITEM[name] + k
                act.wait_ge(sem("xf_ready"), i + 1)
                nc.scalar.activation(h[:, k], tile(i), ACT.Identity, bias=col(b, k)).then_inc(sem("ln_h"), 1)
                nc.scalar.activation(xa[:, k, 0], tile(i), ACT.Identity, bias=col(b, k))\
                    .then_inc(sem("xhi_ready"), 1)

        def pe_ffn(pe, s, ready):
            base = BASE[s]
            u0 = sum(4 * KC for q in ("ffn0", "ffn1", "ffn2") if BASE[q] < base)
            for j in range(KC):
                pe_panel(pe, base + j, xa, ready if j == 0 else None)
            for j in range(KC, 2 * KC):
                pe_panel(pe, base + j, xb, (sem("ff_lo"), u0) if j == KC else None)
            with pe.Fori(1, 4) as g:
                for j in range(2 * KC):
                    n = base + j
                    if j < 4:
                        pe.wait_ge(taken["dve"], READS["dve"][base] + KC * (g - 1) + 4 + j + 1)
                    else:
                        r = panel_reader(n - 4)
                        pe.wait_ge(taken[r], READS[r][n - 3] + KC * g)
                    pe_panel(pe, n, xa if j < KC else xb,
                             (sem("ff_lo"), u0 + KC * g) if j == KC else None, more=2 * KC * g, free=False)

        def act_ffn(act, s, bias=None):
            base = BASE[s]
            u0 = sum(4 * KC for q in ("ffn0", "ffn1", "ffn2") if BASE[q] < base)

            def turn(g, splits=2 * KC):
                for j in range(2 * KC):
                    if j < splits:
                        act_split(act, base + j, more=64 * g, panels_more=2 * KC * g)
                    if j >= 1 and j <= KC:
                        act.wait_ge(sem("ff_sq"), u0 + j + KC * g)
                        nc.scalar.activation(xb[:, j - 1, 0], ffsq[:, (j - 1) % 2], ACT.Copy)\
                            .then_inc(sem("ff_hi"), 1)
                    if j < KC:
                        act.wait_ge(panel_done, base + j + 1 + 2 * KC * g)
                        b = 0.0 if bias is None else vecs[:, bass.ds(VEC[bias] + j + KC * g, 1)]
                        nc.scalar.activation(relu[:, j % 2], ps[(base + j) % 4][:, :], ACT.Relu, bias=b)\
                            .then_inc(taken["act"], 1)

            with act.Fori(0, 4 - (s == "ffn2")) as g:
                turn(g)
            if s == "ffn2":
                turn(3, 2 * KC - AHEAD)

        def dve_ffn(dve, s):
            base = BASE[s]
            u0 = sum(4 * KC for q in ("ffn0", "ffn1", "ffn2") if BASE[q] < base)

            def turn(g, splits=2 * KC):
                for j in range(2 * KC):
                    if j < splits:
                        dve_split(dve, base + j, more=2 * KC * g)
                    if j < KC:
                        dve.wait_ge(taken["act"], READS["act"][base] + j + 1 + KC * g)
                        nc.vector.tensor_tensor(ffsq[:, j % 2], relu[:, j % 2], relu[:, j % 2], ALU.mult)\
                            .then_inc(sem("ff_sq"), 1)
                        dve.wait_ge(sem("ff_hi"), u0 + j + 1 + KC * g)
                        nc.vector.tensor_tensor(xb[:, j, 1], ffsq[:, j % 2], xb[:, j, 0].bitcast(F32),
                                                ALU.subtract).then_inc(sem("ff_lo"), 1)
                    else:
                        dve.wait_ge(panel_done, base + j + 1 + 2 * KC * g)
                        dve.wait_ge(taken["dve"], READS["dve"][base] + (j - KC) + KC * g)
                        nc.vector.tensor_tensor(acc[:, j - KC], acc[:, j - KC], ps[(base + j) % 4][:, :], ALU.add)\
                            .then_inc(taken["dve"], 1)

            with dve.Fori(0, 4 - (s == "ffn2")) as g:
                turn(g)
            if s == "ffn2":
                turn(3, 2 * KC - AHEAD)

        def operands(u_):
            kind, g, p, t, k0, nk, head = UNITS[u_]
            r = slice(HD * g, HD * g + HD)
            if kind in ("sel", "win"):
                i = int(kind == "win")
                return (n_q[r, p, t * P:(t + 1) * P], n_k[r, i, k0:k0 + nk],
                        [n_v[:, i, j, HD * g:HD * g + HD] for j in range(nk // P)])
            if kind == "na":
                return (a_q[r, p, t * P:(t + 1) * P], a_k[r, p, k0:k0 + nk],
                        [a_v[:, j, HD * head:HD * head + HD] for j in range(nk // P)])
            return (w_q[r, p, t * P:(t + 1) * P], w_k[r, 0, k0:k0 + nk],
                    [w_v[:, k0 // P + j, HD * g:HD * g + HD] for j in range(nk // P)])

        def pe_scores(pe, u_):
            kind, g, p, t, k0, nk, head = UNITS[u_]
            q, k, _ = operands(u_)
            if u_ >= 2:
                pe.wait_ge(sem("at_probs"), u_ - 1)
            masks = []
            if kind in ("sel", "win"):
                masks = [(t * P, lowb)]
            if kind == "swa":
                if t > 0:
                    masks.append((0, upb))
                if t < TB - 1:
                    masks.append((nk - P, lowb))
            bank = ps[4 + u_ % 2]
            mm = nc.tensor.matmul(bank[:, 0:nk], q, k, start=True, stop=not masks)
            for i, (c, m) in enumerate(masks):
                mm = nc.tensor.matmul(bank[:, c:c + P], identb[:, :], m[:, :], start=False, stop=i == len(masks) - 1)
            mm.then_inc(sem("at_scores"), 1)

        def pe_turn(pe, u_, probs):
            nk = UNITS[u_][5]
            pe.wait_ge(sem("at_probs"), u_ + 1)
            if u_ >= 2:
                pe.wait_ge(sem("at_turned"), u_ - 1)
            for j in range(nk // P):
                mm = nc.tensor.transpose(ps[6 + u_ % 2][:, j * P:(j + 1) * P], probs[:, u_ % 2, j * P:(j + 1) * P], ident)
            mm.then_inc(sem("at_turn"), 1)

        def pe_values(pe, u_, turned):
            nk = UNITS[u_][5]
            v = operands(u_)[2]
            pe.wait_ge(sem("at_turned"), u_ + 1)
            if u_ >= 1:
                pe.wait_ge(sem("at_out"), u_)
            for j in range(nk // P):
                mm = nc.tensor.matmul(ps[2][:, 0:HD], turned[:, u_ % 2, j * P:(j + 1) * P], v[j],
                                      start=(j == 0), stop=(j == nk // P - 1))
            mm.then_inc(sem("at_values"), 1)

        def pe_blocks(pe, first, blocks, operand):
            for b in blocks:
                n, k = first + b // KC, b % KC
                if k == 0:
                    pe_free(pe, n)
                    pe.wait_ge(lo_done, n + 1)
                for w, xx in ((0, 0), (0, 1), (1, 0)):
                    mm = nc.tensor.matmul(ps[BANK[n]][:, :], ring[:, n % RING, w, k * P:(k + 1) * P],
                                          operand[:, k, xx], start=(k == 0 and w == 0 and xx == 0),
                                          stop=(k == KC - 1 and w == 1))
                if k == KC - 1:
                    mm.then_inc(panel_done, 1)

        def pe_attention(pe, first, last, probs, turned, beside=None):
            for i in range(first, last + 2):
                if i < last:
                    pe_scores(pe, i)
                if beside is not None:
                    beside(i - first)
                if first <= i - 1 < last:
                    pe_turn(pe, i - 1, probs)
                if i - 2 >= first:
                    pe_values(pe, i - 2, turned)

        NMAX, SUM, SINK, DEN, REC, WGT = range(6)

        def act_attention(act, first, last, probs, turned, beside=None):
            for i in range(first, last + 2):
                if i < last:
                    kind, g, p, t, k0, nk, head = UNITS[i]
                    s = i % 4
                    act.wait_ge(sem("at_max"), i + 1)
                    if i >= 2:
                        act.wait_ge(sem("at_turn"), i - 1)
                    src = a_s[:, i % 2, 0:nk] if kind == "na" else ps[4 + i % 2][:, 0:nk]
                    nc.scalar.activation(probs[:, i % 2, 0:nk], src, ACT.Exp, bias=stat[:, NMAX, s:s + 1],
                                         accum_out=stat[:, SUM, s:s + 1]).then_inc(sem("at_probs"), 1)
                    if kind == "swa":
                        nc.scalar.activation(stat[:, SINK, s:s + 1], col("sink", head), ACT.Exp,
                                             bias=stat[:, NMAX, s:s + 1]).then_inc(sem("at_sink"), 1)
                if first <= i - 1 < last:
                    nk = UNITS[i - 1][5]
                    act.wait_ge(sem("at_turn"), i)
                    if i >= 3:
                        act.wait_ge(sem("at_values"), i - 2)
                    nc.scalar.activation(turned[:, (i - 1) % 2, 0:nk], ps[6 + (i - 1) % 2][:, 0:nk], ACT.Copy)\
                        .then_inc(sem("at_turned"), 1)
                if beside is not None:
                    beside(i - first)

        def dve_attention(dve, chain, first, last, o, beside=None):
            for i in range(first, last + 2):
                if i < last:
                    kind, g, p, t, k0, nk, head = UNITS[i]
                    s = i % 4
                    dve.wait_ge(sem("at_scores"), i + 1)
                    src = ps[4 + i % 2][:, 0:nk]
                    if kind == "na":
                        dve.wait_ge(sem("rpb_masked"), head + 1)
                        if i >= 2:
                            dve.wait_ge(sem("at_probs"), i - 1)
                        c = (7 - 2 * t - 1) * NA_W
                        chain(nc.vector.tensor_tensor(a_s[:, i % 2], src, t2[:, head % 2, c:c + T], ALU.add))
                        src = a_s[:, i % 2]
                        red = nc.vector.tensor_reduce(stat[:, NMAX, s:s + 1], src, AX.X, ALU.max, negate=True)
                        red.then_inc(sem("at_max"), 1)
                    elif kind == "swa":
                        chain(nc.vector.tensor_reduce(stat[:, DEN + 4, s:s + 1], src, AX.X, ALU.max, negate=True))
                        nc.vector.tensor_tensor(stat[:, NMAX, s:s + 1], stat[:, DEN + 4, s:s + 1],
                                                stat[:, 8, 4 + head:5 + head], ALU.min).then_inc(sem("at_max"), 1)
                    else:
                        nc.vector.tensor_reduce(stat[:, NMAX, s:s + 1], src, AX.X, ALU.max, negate=True)\
                            .then_inc(sem("at_max"), 1)
                if i - 2 >= first:
                    w = i - 2
                    kind, g, p, t, k0, nk, head = UNITS[w]
                    s = w % 4
                    dve.wait_ge(sem("at_values"), w + 1)
                    den = stat[:, SUM, s:s + 1]
                    if kind == "swa":
                        dve.wait_ge(sem("at_sink"), w - U_SWA + 1)
                        chain(nc.vector.tensor_tensor(stat[:, DEN, s:s + 1], den, stat[:, SINK, s:s + 1], ALU.add))
                        den = stat[:, DEN, s:s + 1]
                    chain(nc.vector.reciprocal(stat[:, REC, s:s + 1], den))
                    res = ps[2][:, 0:HD]
                    dst = o[:, t, head]
                    if kind in ("sel", "win"):
                        gate = n_gate[:, t, 3 * head + (1 if kind == "sel" else 2):3 * head + (2 if kind == "sel" else 3)]
                        chain(nc.vector.tensor_tensor(stat[:, WGT, s:s + 1], stat[:, REC, s:s + 1], gate, ALU.mult))
                        if w >= 1:
                            dve.wait_ge(sem("at_out"), w)
                        nc.vector.scalar_tensor_tensor(out=dst, in0=res, scalar=stat[:, WGT, s:s + 1], in1=dst,
                                                       op0=ALU.mult, op1=ALU.add).then_inc(sem("at_out"), 1)
                    else:
                        nc.vector.tensor_scalar(dst, res, stat[:, REC, s:s + 1], None, ALU.mult)\
                            .then_inc(sem("at_out"), 1)
                if beside is not None:
                    beside(i - first)

        def pe_outs(pe, o, count, wait):
            pe.wait_ge(*wait)
            for k in range(4):
                i = count + k
                if i >= 2:
                    pe.wait_ge(sem("xf_out"), i - 1)
                for t in range(TB):
                    mm = nc.tensor.transpose(ps[4 + i % 2][:, t * P:(t + 1) * P], o[:, t, k * P:(k + 1) * P], ident)
                mm.then_inc(sem("outs_turned"), 1)

        def dve_outs(dve, name, count, scale=None):
            for k in range(4):
                i = ITEM[name] + k
                xf_free(dve, i)
                dve.wait_ge(sem("outs_turned"), count + k + 1)
                bank = ps[4 + (count + k) % 2][:, :]
                if scale is None:
                    ins = nc.vector.tensor_copy(xf[:, i % 4], bank)
                else:
                    ins = nc.vector.scalar_tensor_tensor(out=xf[:, i % 4], in0=bank, scalar=scale(k)[0],
                                                         in1=scale(k)[1], op0=ALU.mult, op1=ALU.mult)
                ins.then_inc(sem("xf_ready"), 1)
                dve.wait_ge(sem("xf_ready"), i + 1)
                dve.sem_inc(sem("xf_out"), 1)

        VT = {5: 0, 6: 1, 7: 2, 8: 3, 20: 4, 22: 5}
        VT2 = {BASE["mix2_in"] + 8 + i: 6 + i for i in range(4)} | {BASE["mix2_in"] + 17: 10}
        VT.update(VT2)

        def act_value(act, n, bias=0.0):
            v = VT[n]
            if v >= 2:
                act.wait_ge(sem("v_turn"), v - 1)
            act.wait_ge(panel_done, n + 1)
            nc.scalar.activation(sq[:, v % 2], ps[BANK[n]][:, :], ACT.Identity, bias=bias).then_inc(taken["act"], 1)

        def value_bank(v):
            return ps[3] if v == 10 else ps[6 + v % 2]

        def pe_value(pe, n):
            v = VT[n]
            pe.wait_ge(taken["act"], READS["act"][n + 1])
            if v >= 2:
                pe.wait_ge(sem("v_done"), v - 1)
            for t in range(TB):
                mm = nc.tensor.transpose(value_bank(v)[:, t * P:(t + 1) * P], sq[:, v % 2, t * P:(t + 1) * P], ident)
            mm.then_inc(sem("v_turn"), 1)

        def dve_value(dve, n, dst):
            v = VT[n]
            dve.wait_ge(sem("v_turn"), v + 1)
            nc.vector.tensor_copy(dst, value_bank(v)[:, :].rearrange("p (t d) -> p t d", t=TB))\
                .then_inc(sem("v_done"), 1)

        M0, M2 = BASE["mix0_in"], BASE["mix2_in"]

        block = ctx.enter_context(nc.Block())

        @block.sync
        def _(sp):
            sp.dma_start(cons[:, :], con).then_inc(setup, 16)
            sp.dma_start(vecs[:, :], vec).then_inc(setup, 16)
            for k in range(KC):
                sp.dma_start(h[:, k], x[:, k]).then_inc(sem(f"x_in{k % 2}"), 16)
            for n in range(RING):
                sp.dma_start(raw[:, n], stream[n]).then_inc(landed[n], 16)

            def turn(first):
                for s in range(RING):
                    sp.wait_ge(lo_done, first + s - RING + 1)
                    src = stream[bass.ds(first + s, 1)].rearrange("a p n -> p (a n)")
                    sp.dma_start(raw[:, s], src).then_inc(landed[s], 16)

            with sp.Fori(1, NP // RING) as i:
                turn(RING * i)
            for n in range(NP // RING * RING, NP):
                sp.wait_ge(lo_done, n - RING + 1)
                sp.dma_start(raw[:, n % RING], stream[n]).then_inc(landed[n % RING], 16)
            for k in range(KC):
                sp.wait_ge(sem("y_ready"), k + 1)
                sp.dma_start(out[:, k], h[:, k]).then_inc(sem("stored"), 16)
            sp.wait_ge(sem("stored"), 16 * KC)

        @block.gpsimd
        def _(pool):
            chain = Chain(pool, "pool_chain")
            pool.dma_start(g_wg[:, :], gate_w).then_inc(sem("gate_w_in"), 16)
            pool.memset(g_at[:, :, :, :], 0.0)
            pool.memset(g_ke[:, :, :, :, :], 0.0).then_inc(sem("gla_zero"), 1)
            pool_items(pool, "prep0", xa, tile)
            pool.wait_ge(sem("gla_scores_out"), 8)
            for r in (0, HD):
                v = g_at[r:r + HD, :, :, r:r + HD].rearrange("p a t i -> p (a t) i")
                pool.affine_select(out=v, in_=v, compare_op=ALU.is_ge, fill=0.0, base=0,
                                   pattern=[[0, 4 * TB], [1, HD]], channel_multiplier=-1)\
                    .then_inc(sem("gla_masked"), 1)
            pool_items(pool, "gla", xb, tile, 4)
            pool.wait_ge(sem("outs_turned"), 4)
            pool.wait_ge(sem("xf_ready"), ITEM["gla"] + 4)
            for i in range(2):
                pool.dma_start(c_w1[i][:, :, :], cmp_w1[i]).then_inc(sem("cmp_in"), 16)
            pool.dma_start(c_w2[:, :, :], cmp_w2).then_inc(sem("cmp_in"), 16)
            pool.dma_start(c_pos[:, :, :], cmp_pos).then_inc(sem("cmp_in"), 16)
            pool.memset(c_g[:, :, :, :], 0.0).then_inc(sem("cmp_zero"), 1)
            pool.memset(c_vbd[:, :, :, :], 0.0).then_inc(sem("cmp_zero"), 1)
            pool_items(pool, "nsa", xb, tile, 4, 4)
            pool_residual(pool, 0)
            pool_items(pool, "prep1", xa, tile)
            pool.memset(acc[:, :, :], 0.0).then_inc(sem("acc_zero"), 1)
            pool_residual(pool, 1)
            pool_items(pool, "prep2", xa, tile)
            pool.wait_ge(sem("h_ready"), 2 * KC)
            pool.wait_ge(sem("xlo_ready"), ITEM["prep2"] + KC)
            pool.dma_start(gb[:, :, :], ln_gb).then_inc(sem("sgu_in"), 16)
            pool.dma_start(wst[:, :, :], w_s).then_inc(sem("wst_in"), 16)
            pool.dma_start(bs[:, :], b_s).then_inc(sem("sgu_in"), 16)
            pool.wait_ge(sem("wst_in"), 16)
            pool.affine_select(out=wst[:, :, :], in_=wst[:, :, :], compare_op=ALU.is_ge, fill=0.0, base=0,
                               pattern=[[0, 8], [1, P]], channel_multiplier=-1).then_inc(sem("wst_masked"), 1)
            for t in range(TB):
                pool.wait_ge(sem("vn_ready"), t + 1)
                if t == 0:
                    pool.wait_ge(sem("sgu_in"), 32)
                chain(nc.gpsimd.tensor_tensor(v_tok[:, t], v_tok[:, t], gb[:, 0], ALU.mult))
                nc.gpsimd.tensor_tensor(v_tok[:, t], v_tok[:, t], gb[:, 1], ALU.add).then_inc(sem("v_normed"), 1)
            for k in range(2 * KC):
                i = ITEM["sgu"] + k
                if k == KC:
                    pool.wait_ge(panel_done, BASE["sgu_out"] + KC)
                pool_item(pool, i, xa[:, k % KC], u[:, k])
            pool_residual(pool, 2)
            pool_items(pool, "prep3", xa, tile)
            pool.memset(acc[:, :, :], 0.0).then_inc(sem("acc_zero"), 1)
            pool_residual(pool, 3)
            pool.wait_ge(panel_done, BASE["ffn1"] + 64)
            pool.dma_start(ropes[:, :, :], rope).then_inc(sem("rope_in"), 16)

            def load_rpb(hd):
                pool.dma_start(t2[:, hd % 2], rpb[hd]).then_inc(sem(f"rpb_in{hd % 2}"), 16)

            load_rpb(0)
            load_rpb(1)
            for k in range(KC):
                i = ITEM["ln0"] + k
                pool_item(pool, i, xa[:, k], h[:, k])
            for hd in range(8):
                pool.wait_ge(sem(f"rpb_in{hd % 2}"), 16 * (hd // 2 + 1))
                v = t2[:, hd % 2].rearrange("p (s c) -> p s c", c=NA_W)
                m = cons[:, CON["nacol"]:CON["nacol"] + NA_W].unsqueeze(1).to_broadcast([P, 14, NA_W])
                nc.gpsimd.tensor_tensor(v, v, m, ALU.add).then_inc(sem("rpb_masked"), 1)
                if hd >= 1 and hd + 1 < 8:
                    pool.wait_ge(sem("at_max"), U_NA + 4 * hd)
                    load_rpb(hd + 1)
            pool_items(pool, "na", xb, tile, 4)
            pool_items(pool, "swa", xb, tile, 4, 4)
            for c in range(KC):
                i = ITEM["mixed"] + c
                pool_item(pool, i, xa[:, c], tile(i))
            for k in range(KC):
                i = ITEM["ln1"] + k
                pool_item(pool, i, xa[:, k], h[:, k])

        @block.tensor
        def _(pe):
            pe.wait_ge(setup, 32)
            pe_squares(pe, 0)
            for i in range(23):
                n = M0 + i
                pe_panel(pe, n, xa, item_ready("prep0") if i == 0 else None)
                if n - 1 in VT:
                    pe_value(pe, n - 1)
                if n == 22:
                    pe_value(pe, n)
            pe.wait_ge(sem("gate_w_in"), 16)
            for p in range(2):
                mm = nc.tensor.matmul(ps[4 + p][:, :], g_wg[:, p * P:(p + 1) * P], misc[0:16, :], start=True, stop=True)
                mm.then_inc(sem("gla_gate"), 1)
            for p in range(2):
                pe.wait_ge(sem("gla_kend"), p + 1)
                for t in range(TB):
                    mm = nc.tensor.transpose(ps[6 + p][:, t * P:(t + 1) * P], g_t[:, p, t * P:(t + 1) * P], ident)
                mm.then_inc(sem("gla_kturn"), 1)
            pe.wait_ge(taken["act"], READS["act"][M0 + 23])
            for hd in range(4):
                p, r = hd // 2, slice(HD * (hd % 2), HD * (hd % 2) + HD)
                pe.wait_ge(sem("gla_kt"), p + 1)
                for t in range(TB):
                    s = slice(t * P, (t + 1) * P)
                    mm = nc.tensor.matmul(ps[hd][:, s], g_k[r, p, s], g_q[r, p, s], start=True, stop=True)
                mm.then_inc(sem("gla_scores"), 1)
            pe.wait_ge(sem("gla_ke"), 4)
            for c in range(2 * TB - 1):
                if c >= 2:
                    pe.wait_ge(sem("gla_state"), c - 1)
                for p in range(2):
                    mm = nc.tensor.matmul(ps[4 + c % 2][:, p * 256:(p + 1) * 256], g_ke[:, p, c // 2, c % 2],
                                          g_v[:, c // 2, p * 256:(p + 1) * 256], start=True, stop=True)
                mm.then_inc(sem("gla_ds"), 1)
            pe.wait_ge(sem("gla_masked"), 2)
            pe.wait_ge(sem("gla_state"), 2 * TB - 1)
            for t in range(TB):
                for odd in range(2):
                    bank = ps[(6 if t % 2 else 0) + odd]
                    if t >= 2:
                        pe.wait_ge(sem("gla_out_taken"), 2 * (t - 2) + odd + 1)
                    for p in range(2):
                        hd = 2 * p + odd
                        r = slice(HD * odd, HD * odd + HD)
                        dst = bank[:, p * P:(p + 1) * P]
                        mm = nc.tensor.matmul(dst, g_at[:, hd, t], g_v[:, t, hd * P:(hd + 1) * P], start=True,
                                              stop=False)
                        for c2 in range(2):
                            c = 2 * t + c2
                            mm = nc.tensor.matmul(bank[HD * c2:HD * c2 + HD, p * P:(p + 1) * P],
                                                  g_q[r, p, c * HD:(c + 1) * HD], g_s[r, c, p],
                                                  start=False, stop=True)
                    mm.then_inc(sem("gla_out"), 1)
            pe_outs(pe, g_o, 0, (sem("gla_o_ready"), TB))
            pe.wait_ge(sem("cmp_in"), 64)
            pe.wait_ge(sem("xf_out"), 4)
            for i in range(2):
                pe.wait_ge(sem("cmp_blocks"), i + 1)
                for g in range(2):
                    for pos in range(CMP_BLOCK):
                        mm = nc.tensor.matmul(ps[2 * i + g][:, 0:N_CMP], c_w1[i][HD * g:HD * g + HD, pos],
                                              c_bl[HD * g:HD * g + HD, i, pos, 0:N_CMP], start=(pos == 0),
                                              stop=(pos == CMP_BLOCK - 1))
                    mm.then_inc(sem("cmp_hidden"), 1)
            pe.wait_ge(sem("cmp_gelu"), 4)
            for g in range(2):
                mm = nc.tensor.matmul(ps[4][HD * g:HD * g + HD, 0:32], c_w2[:, 0], c_g[:, 0, g], start=True, stop=True)
            mm.then_inc(sem("cmp_kv"), 1)
            for g in range(2):
                for j in range(4):
                    mm = nc.tensor.matmul(ps[5][32 * j:32 * j + 32, g * HD:(g + 1) * HD], c_g[:, 1, g], c_w2[:, 1],
                                          start=True, stop=True)
            mm.then_inc(sem("cmp_kv"), 1)
            pe.wait_ge(sem("cmp_kv_ready"), 2)
            for g in range(2):
                r = slice(HD * g, HD * g + HD)
                for t in range(TB):
                    for j in range(4):
                        mm = nc.tensor.matmul(ps[6 + g][:, (4 * t + j) * 32:(4 * t + j + 1) * 32],
                                              n_q[r, j, t * P:(t + 1) * P], c_kc[r, :], start=True, stop=True)
                mm.then_inc(sem("cmp_scores"), 1)
            for t in range(TB):
                mm = nc.tensor.transpose(ps[t % 2][:, t * P:(t + 1) * P], misc[:, t * P:(t + 1) * P], ident)
            mm.then_inc(sem("gates_turned"), 1)
            for g in range(2):
                pe.wait_ge(sem("cmp_probs"), g + 1)
                for t in range(TB):
                    mm = nc.tensor.transpose(ps[2 + g][:, t * P:(t + 1) * P],
                                             c_e[:, g, t].rearrange("p h c -> p (h c)"), ident)
                mm.then_inc(sem("cmp_turn"), 1)
            for g in range(2):
                pe.wait_ge(sem("cmp_turned"), g + 1)
                for t in range(TB):
                    i = 4 * g + t
                    if i >= 2:
                        pe.wait_ge(sem("cmp_out_taken"), i - 1)
                    nc.tensor.matmul(ps[4 + i % 2][:, 0:256], c_pt[:, g, t],
                                     c_vbd[:, g].rearrange("p h d -> p (h d)"), start=True, stop=True)\
                        .then_inc(sem("cmp_out"), 1)
            pe.wait_ge(sem("cmp_out_taken"), 8)
            pe_attention(pe, 0, U_NA, n_p, n_pt)
            pe_outs(pe, n_o[:, :, :, :].rearrange("p t h d -> p t (h d)"), 4, (sem("at_out"), U_NA))
            for k in range(KC):
                pe_panel(pe, BASE["mix0_out"] + k, xb, item_ready("gla") if k == 0 else None)
            pe_squares(pe, 1)
            pe_squares(pe, 2)
            pe_ffn(pe, "ffn0", item_ready("prep1"))
            pe_squares(pe, 3)
            pe_squares(pe, 4)
            B = BASE["sgu_in"]

            def turn_v(i):
                pe.wait_ge(taken["act"], READS["act"][B] + i + 1)
                if i >= 2:
                    pe.wait_ge(sem("vt_copied"), i - 1)
                for t in range(TB):
                    mm = nc.tensor.transpose(ps[6 + i % 2][:, t * P:(t + 1) * P], sq[:, i % 2, t * P:(t + 1) * P],
                                             ident)
                mm.then_inc(sem("vt_turn"), 1)

            for i in range(2 * KC):
                pe_panel(pe, B + i, xa, item_ready("prep2") if i == 0 else None)
                if i >= 1:
                    turn_v(i - 1)
            pe_panel(pe, B + 2 * KC, xa)
            turn_v(2 * KC - 1)
            for i in range(2 * KC + 1, 2 * KC + RING):
                pe_panel(pe, B + i, xa)
            B += 2 * KC
            with pe.Fori(1, 4) as g:
                for j in range(RING):
                    pe.wait_ge(taken["act"], READS["act"][B] + j + 1 + RING * (g - 1))
                    pe_panel(pe, B + j, xa, more=RING * g, free=False)
            pe.wait_ge(sem("wst_masked"), 1)
            pe.wait_ge(sem("v_normed"), TB)
            pe.wait_ge(taken["act"], READS["act"][B + 16])
            for k in range(2 * KC):
                bank = ps[k % 4] if k < KC else ps[4 + k % 4]
                if k % KC >= 4:
                    pe.wait_ge(sem("y_taken"), k - 3)
                g = k // 2
                for t in range(TB):
                    mm = nc.tensor.matmul(bank[:, t * P:(t + 1) * P], v_tok[:, t, k * P:(k + 1) * P], wst[:, g],
                                          start=True, stop=True)
                mm.then_inc(sem("mixed_v"), 1)
            pe.wait_ge(sem("y_taken"), KC)
            for half in range(2):
                for k in range(KC):
                    pe_panel(pe, BASE["sgu_out"] + KC * half + k, xa,
                             (sem("xlo_ready"), ITEM["sgu"] + KC * half) if k == 0 else None)
            pe_squares(pe, 5)
            pe_squares(pe, 6)
            pe_ffn(pe, "ffn1", item_ready("prep3"))
            pe_squares(pe, 7)
            pe_mean(pe, 0, (sem("h_ready"), 24))
            pe_squares(pe, 8)
            for i in range(12):
                n = M2 + i
                pe_panel(pe, n, xa, item_ready("ln0") if i == 0 else None)
                if n - 1 in VT:
                    pe_value(pe, n - 1)
            pe_blocks(pe, M2 + 12, range(0, 2), xa)
            pe_value(pe, M2 + 11)
            pe.wait_ge(sem("v_done"), 10)

            def beside_na(i):
                if i < NA_UNITS:
                    pe_blocks(pe, M2 + 12, [b for b in blocks_beside(i, 6, NA_UNITS) if b >= 2], xa)
                for c in range(6):
                    if NA_END[c] + 1 != i:
                        continue
                    if c == 5:
                        pe.wait_ge(sem("rope_out"), 5)
                        pe_value(pe, M2 + 17)
                        continue
                    pe.wait_ge(taken["act"], READS["act"][M2 + 13 + c])
                    if c >= 1:
                        pe.wait_ge(sem("rope_out"), c)
                    nc.tensor.matmul(ps[3][:, :], cons[:, CON["rot"]:CON["rot"] + P], rtmp[:, c % 2],
                                     start=True, stop=True).then_inc(sem("rope_turn"), 1)

            pe_attention(pe, U_NA, U_SWA, a_p, a_pt, beside_na)
            pe_outs(pe, a_o[:, :, :, :].rearrange("p t h d -> p t (h d)"), 8, (sem("at_out"), U_SWA))
            pe.wait_ge(sem("xf_out"), 12)
            pe.wait_ge(sem("v_done"), 11)
            G2 = BASE["mix2_gate"]
            pe_attention(pe, U_SWA, NU, a_p, a_pt,
                         lambda i: pe_blocks(pe, G2, blocks_beside(i, 12, NA_UNITS), xa) if i < NA_UNITS else None)
            pe_panel(pe, G2 + 12, xa)
            pe_panel(pe, G2 + 13, xa)
            pe_outs(pe, w_o[:, :, :, :].rearrange("p t h d -> p t (h d)"), 12, (sem("at_out"), NU))
            pe_panel(pe, G2 + 14, xa)
            pe_panel(pe, G2 + 15, xa)
            for c in range(KC):
                n = BASE["mix2_branch"] + c
                pe_panel(pe, n, xb, item_ready("na") if c == 0 else None, blocks=range(4), last=False)
                if c >= 2:
                    pe.wait_ge(sem("branch_taken"), c - 1)
                pe_panel(pe, n, xb, item_ready("na") if c == 0 else None, blocks=range(4, 8), free=False,
                         bank=ps[6 + c % 2])
            for k in range(KC):
                pe_panel(pe, BASE["mix2_out"] + k, xa, item_ready("mixed") if k == 0 else None)
            pe_mean(pe, 1, (taken["dve"], READS["dve"][BASE["mix2_out"]]))
            pe_squares(pe, 9)
            pe_ffn(pe, "ffn2", item_ready("ln1"))
            pe_mean(pe, 2, (sem("h_final"), 0))
            pe_squares(pe, 10)

        @block.scalar
        def _(act):
            chain = Chain(act, "act_chain")
            act.wait_ge(setup, 32)
            act.wait_ge(sem("x_in0"), 64)
            act.wait_ge(sem("x_in1"), 64)
            act_squares(act, 0, h)
            act_sd(act, 0, "eps6")
            for n in range(-AHEAD, 0):
                act_split(act, n)
            act_items(act, "prep0", xa, tile)

            def copy_out(n, dst, func=ACT.Copy, **kw):
                act.wait_ge(panel_done, n + 1)
                return nc.scalar.activation(dst, ps[BANK[n]][:, :], func, **kw).then_inc(taken["act"], 1)

            for i in range(23):
                n = M0 + i
                act_split(act, n)
                if i == 0:
                    act.wait_ge(panel_done, n + 1)
                    chain(nc.scalar.activation(misc[:, :], ps[n % 4][:, :], ACT.Copy))
                    nc.scalar.activation(misc[32:64, :], ps[n % 4][32:64, :], ACT.Sigmoid,
                                         bias=vecs[32:64, VEC["nsa_gate_b"]:VEC["nsa_gate_b"] + 1])\
                        .then_inc(taken["act"], 1)
                elif i < 3:
                    copy_out(n, g_q[:, i - 1], scale=HD ** -0.5)
                elif i < 5:
                    copy_out(n, g_k[:, i - 3])
                elif i < 9:
                    act_value(act, n)
                elif i < 13:
                    copy_out(n, g_r[:, i - 9], ACT.Silu)
                elif i < 17:
                    copy_out(n, n_q[:, i - 13], scale=HD ** -0.5)
                elif i < 19:
                    copy_out(n, n_c[:, i - 17])
                elif i in (19, 21):
                    copy_out(n, n_k[:, (i - 19) // 2])
                else:
                    act_value(act, n)
            for p in range(2):
                act.wait_ge(sem("gla_gate"), p + 1)
                chain(nc.scalar.activation(g_b[:, p], ps[4 + p][:, :], ACT.Identity, bias=col("gla_b", p)))
                chain(nc.scalar.activation(g_t[:, p], g_b[:, p], ACT.Abs))
            for p in range(2):
                chain(nc.scalar.activation(g_t[:, p], g_t[:, p], ACT.Exp, scale=-1.0))
            for p in range(2):
                nc.scalar.activation(g_t[:, p], g_t[:, p], ACT.Ln, bias=con_col("one")).then_inc(sem("gla_ln"), 1)
            for p in range(2):
                act.wait_ge(sem("gla_cum"), p + 1)
                nc.scalar.activation(sq[:, p], g_b[:, p], ACT.Exp)
                nc.scalar.activation(xf[:, p], g_b[:, p], ACT.Exp, scale=-1.0)
                act.wait_ge(sem("gla_diff"), p + 1)
                nc.scalar.activation(g_t[:, p], g_t[:, p], ACT.Exp).then_inc(sem("gla_exp"), 1)
            act.wait_ge(sem("gla_zero"), 1)
            for p in range(2):
                act.wait_ge(sem("gla_kturn"), p + 1)
                for odd in range(2):
                    r = slice(HD * odd, HD * odd + HD)
                    nc.scalar.activation(g_ke[r, p, :, odd], ps[6 + p][r, :].rearrange("p (t d) -> p t d", t=TB),
                                         ACT.Copy).then_inc(sem("gla_ke"), 1)
            for hd in range(4):
                act.wait_ge(sem("gla_scores"), hd + 1)
                for odd in range(2):
                    r = slice(HD * odd, HD * odd + HD)
                    src = ps[hd][r, :].rearrange("p (t d) -> p t d", t=TB)[:, :, HD * odd:HD * odd + HD]
                    nc.scalar.activation(g_at[r, hd, :, HD * odd:HD * odd + HD], src, ACT.Copy)\
                        .then_inc(sem("gla_scores_out"), 1)
            for t in range(TB):
                for odd in range(2):
                    bank = ps[(6 if t % 2 else 0) + odd]
                    act.wait_ge(sem("gla_out"), 2 * t + odd + 1)
                    dst = g_o[:, t].rearrange("p (q o d) -> p q o d", q=2, o=2)[:, :, odd]
                    nc.scalar.activation(dst, bank[:, 0:256].rearrange("p (q d) -> p q d", q=2), ACT.Copy)\
                        .then_inc(sem("gla_out_taken"), 1)
            act.wait_ge(sem("gla_ssq"), TB)
            nc.scalar.activation(stat[:, 1, 0:16], stat[:, 0, 0:16], ACT.Sqrt, scale=1.0 / P, bias=con_col("eps6"))\
                .then_inc(sem("gla_sd"), 1)
            act_items(act, "gla", xb, tile, 4)
            act.wait_ge(sem("cmp_zero"), 2)
            for i in range(2):
                for g in range(2):
                    act.wait_ge(sem("cmp_hidden"), 2 * i + g + 1)
                    nc.scalar.activation(c_g[:, i, g, 0:N_CMP], ps[2 * i + g][:, 0:N_CMP], ACT.Gelu_apprx_tanh)\
                        .then_inc(sem("cmp_gelu"), 1)
            for g in range(2):
                act.wait_ge(sem("cmp_centred"), g + 1)
                nc.scalar.activation(c_e[:, g], c_s[:, g], ACT.Exp).then_inc(sem("cmp_exp"), 1)
            for g in range(2):
                act.wait_ge(sem("cmp_turn"), g + 1)
                nc.scalar.activation(c_pt[:, g], ps[2 + g][:, :].rearrange("p (t q) -> p t q", t=TB), ACT.Copy)\
                    .then_inc(sem("cmp_turned"), 1)
            act_attention(act, 0, U_NA, n_p, n_pt)
            act_items(act, "nsa", xb, tile, 4, 4)
            for k in range(KC):
                act_split(act, BASE["mix0_out"] + k)
                copy_out(BASE["mix0_out"] + k, acc[:, k])
            act_squares(act, 1, acc, (taken["act"], READS["act"][BASE["mix0_out"]]))
            act_sd(act, 1, "eps6")
            act_squares(act, 2, h, (sem("h_ready"), 0))
            act_sd(act, 2, "eps6")
            act_items(act, "prep1", xa, tile)
            act_ffn(act, "ffn0")
            act_squares(act, 3, acc, (taken["dve"], READS["dve"][BASE["ffn0"] + 56]))
            act_sd(act, 3, "eps6")
            act_squares(act, 4, h, (sem("h_ready"), 8))
            act_sd(act, 4, "eps6")
            act_items(act, "prep2", xa, tile)
            B = BASE["sgu_in"]
            for i in range(2 * KC):
                n = B + i
                act_split(act, n)
                act.wait_ge(panel_done, n + 1)
                if i >= 2:
                    act.wait_ge(sem("vt_turn"), i - 1)
                nc.scalar.activation(sq[:, i % 2], ps[n % 4][:, :], ACT.Gelu_apprx_tanh).then_inc(taken["act"], 1)
            for i in range(2 * KC):
                n = B + 2 * KC + i
                act_split(act, n)
                copy_out(n, u[:, i], ACT.Gelu_apprx_tanh)
                if i == 5:
                    act.wait_ge(sem("vn_var"), TB)
                    nc.scalar.activation(stat[:, 1, 0:TB], stat[:, 0, 0:2 * TB:2], ACT.Sqrt, bias=con_col("eps6"))\
                        .then_inc(sem("vn_sd"), 1)
            B = BASE["sgu_out"]
            for k in range(KC):
                act_item(act, ITEM["sgu"] + k, xa[:, k], u[:, k])
            for k in range(KC):
                act_split(act, B + k)
                copy_out(B + k, acc[:, k])
            for k in range(KC):
                act_item(act, ITEM["sgu"] + KC + k, xa[:, k], u[:, KC + k])
            for k in range(KC):
                act_split(act, B + KC + k)
            act_squares(act, 5, acc, (taken["dve"], READS["dve"][B + KC]))
            act_sd(act, 5, "eps6")
            act_squares(act, 6, h, (sem("h_ready"), 16))
            act_sd(act, 6, "eps6")
            act_items(act, "prep3", xa, tile)
            act_ffn(act, "ffn1")
            act_squares(act, 7, acc, (taken["dve"], READS["dve"][BASE["ffn1"] + 56]))
            act_sd(act, 7, "eps6")
            act_mean(act, 0)
            act_ln_items(act, "ln0", "ln0_b")
            for i in range(12):
                n = M2 + i
                act_split(act, n)
                b = col("b_in", i)
                if i < 4:
                    copy_out(n, a_q[:, i], ACT.Identity, bias=bqa[:, i:i + 1], scale=HD ** -0.5)
                elif i < 8:
                    copy_out(n, a_k[:, i - 4], ACT.Identity, bias=b)
                else:
                    act_value(act, n, b)

            def beside(i, first, count, take):
                if i < NA_UNITS:
                    for b in blocks_beside(i, count, NA_UNITS):
                        if b % KC == 0:
                            act_split(act, first + b // KC)
                        if b % KC == KC - 1:
                            take(b // KC)

            def take_swa(c):
                b = col("b_in", 12 + c)
                if c == 5:
                    act_value(act, M2 + 17, b)
                    return
                if c >= 2:
                    act.wait_ge(sem("rope_out"), c - 1)
                copy_out(M2 + 12 + c, rtmp[:, c % 2], ACT.Identity, bias=b)

            def take_gate(j):
                copy_out(BASE["mix2_gate"] + j, sig[:, j], ACT.Sigmoid, bias=col("b_in", 18 + KC * (j % 2) + j // 2))

            act_attention(act, U_NA, U_SWA, a_p, a_pt, lambda i: beside(i, M2 + 12, 6, take_swa))
            act_items(act, "na", xb, tile, 4)
            act_attention(act, U_SWA, NU, a_p, a_pt, lambda i: beside(i, BASE["mix2_gate"], 12, take_gate))
            for j in (12, 13):
                act_split(act, BASE["mix2_gate"] + j)
                take_gate(j)
            act_items(act, "swa", xb, tile, 4, 4)
            for j in (14, 15):
                act_split(act, BASE["mix2_gate"] + j)
                take_gate(j)
            for c in range(KC):
                act_split(act, BASE["mix2_branch"] + c)
                act_item(act, ITEM["mixed"] + c, xa[:, c], tile(ITEM["mixed"] + c))
            for k in range(KC):
                act_split(act, BASE["mix2_out"] + k)
            act_mean(act, 1)
            act_ln_items(act, "ln1", "ln1_b")
            act_ffn(act, "ffn2", "b_ff1")
            act_mean(act, 2)
            for k in range(KC):
                i = NI + k
                act.wait_ge(sem("xf_ready"), i + 1)
                nc.scalar.activation(h[:, k], tile(i), ACT.Identity, bias=col("ln2_b", k)).then_inc(sem("y_ready"), 1)

        @block.vector
        def _(dve):
            chain = Chain(dve, "dve_chain")
            dve.wait_ge(setup, 32)
            for dst, name in ((identb, "ident"), (lowb, "low"), (upb, "up")):
                nc.vector.tensor_copy(dst[:, :], cons[:, CON[name]:CON[name] + P])
            nc.vector.tensor_scalar(stat[:, 8, 4:12], vecs[:, VEC["sink"]:VEC["sink"] + 8], -1.0, None, ALU.mult)
            chain(nc.vector.tensor_scalar(bqa[:, :], vecs[:, VEC["b_in"]:VEC["b_in"] + 4], HD ** -0.5, None,
                                          ALU.mult))
            for n in range(-AHEAD, 0):
                dve_split(dve, n)
            dve_rs(dve, 0)
            dve_prep(dve, "prep0", 0)
            for i in range(23):
                n = M0 + i
                dve_split(dve, n)
                if n - 1 in VT:
                    v = n - 1
                    dve_value(dve, v, g_v[:, :, (v - 5) * P:(v - 4) * P] if v < 10 else n_v[:, (v - 20) // 2])
            dve_value(dve, 22, n_v[:, 1])
            for p in range(2):
                dve.wait_ge(sem("gla_ln"), p + 1)
                chain(nc.vector.scalar_tensor_tensor(out=g_b[:, p], in0=g_b[:, p], scalar=0.0, in1=g_t[:, p],
                                                     op0=ALU.min, op1=ALU.subtract))
                chain(nc.vector.tensor_scalar(g_t[:, p], g_b[:, p], 1.0 / 16.0, None, ALU.mult))
                nc.vector.tensor_tensor_scan(g_b[:, p], cons[:, CON["scan"]:CON["scan"] + T], g_t[:, p], 0.0,
                                             ALU.mult, ALU.add).then_inc(sem("gla_cum"), 1)
                dve.wait_ge(sem("gla_cum"), p + 1)
                bc = g_b[:, p].rearrange("p (c i) -> p c i", i=GLA_CHUNK)
                nc.vector.tensor_tensor(g_t[:, p].rearrange("p (c i) -> p c i", i=GLA_CHUNK),
                                        bc[:, :, GLA_CHUNK - 1:GLA_CHUNK].to_broadcast([P, 2 * TB, GLA_CHUNK]), bc,
                                        ALU.subtract).then_inc(sem("gla_diff"), 1)
            for p in range(2):
                dve.wait_ge(sem("gla_exp"), p + 1)
                nc.vector.tensor_tensor(g_t[:, p], g_t[:, p], g_k[:, p], ALU.mult).then_inc(sem("gla_kend"), 1)
                nc.vector.tensor_copy(stat[:, 2 + p, 0:8], sq[:, p, GLA_CHUNK - 1::GLA_CHUNK])
                dve.wait_ge(sem("gla_kend"), p + 1)
                nc.vector.tensor_tensor(g_q[:, p], g_q[:, p], sq[:, p], ALU.mult)
                nc.vector.tensor_tensor(g_k[:, p], g_k[:, p], xf[:, p], ALU.mult).then_inc(sem("gla_kt"), 1)
            nc.vector.memset(g_s[:, 0], 0.0)
            for c in range(2 * TB - 1):
                dve.wait_ge(sem("gla_ds"), c + 1)
                if c == 0:
                    dve.wait_ge(sem("gla_kt"), 2)
                else:
                    dve.wait_ge(sem("gla_state"), c)
                for p in range(2):
                    for odd in range(2):
                        r = slice(HD * odd, HD * odd + HD)
                        src = ps[4 + c % 2][r, (2 * p + odd) * P:(2 * p + odd + 1) * P]
                        if c == 0:
                            ins = nc.vector.tensor_copy(g_s[r, 1, p], src)
                        else:
                            ins = nc.vector.scalar_tensor_tensor(out=g_s[r, c + 1, p], in0=g_s[r, c, p],
                                                                 scalar=stat[r, 2 + p, c:c + 1], in1=src,
                                                                 op0=ALU.mult, op1=ALU.add)
                ins.then_inc(sem("gla_state"), 1)
            for t in range(TB):
                dve.wait_ge(sem("gla_out_taken"), 2 * t + 2)
                chain(nc.vector.tensor_tensor(xf[:, t % 2], g_o[:, t], g_o[:, t], ALU.mult))
                nc.vector.tensor_reduce(stat[:, 0, 4 * t:4 * t + 4], xf[:, t % 2].rearrange("p (h d) -> p h d", h=4),
                                        AX.X, ALU.add).then_inc(sem("gla_ssq"), 1)
            dve.wait_ge(sem("gla_sd"), 1)
            chain(nc.vector.reciprocal(stat[:, 4, 0:16], stat[:, 1, 0:16]))
            for t in range(TB):
                v = g_o[:, t].rearrange("p (h d) -> p h d", h=4)
                nc.vector.tensor_tensor(v, v, stat[:, 4, 4 * t:4 * t + 4].unsqueeze(2).to_broadcast([P, 4, P]),
                                        ALU.mult).then_inc(sem("gla_o_ready"), 1)
            dve_outs(dve, "gla", 0, lambda k: (col("gla_norm", k), g_r[:, k]))
            dve.wait_ge(sem("cmp_in"), 64)
            for i in range(2):
                src = n_c[:, i].rearrange("p (c s) -> p s c", s=CMP_STRIDE)
                for half in range(2):
                    sl = slice(CMP_STRIDE * half, CMP_STRIDE * half + CMP_STRIDE)
                    ins = nc.vector.tensor_tensor(c_bl[:, i, sl, 0:N_CMP], src[:, :, half:half + N_CMP],
                                                  c_pos[:, i, sl].unsqueeze(2).to_broadcast([P, CMP_STRIDE, N_CMP]),
                                                  ALU.add)
                ins.then_inc(sem("cmp_blocks"), 1)
            dve.wait_ge(sem("cmp_kv"), 1)
            nc.vector.tensor_copy(c_kc[:, :], ps[4][:, 0:32]).then_inc(sem("cmp_kv_ready"), 1)
            dve.wait_ge(sem("cmp_kv"), 2)
            for j in range(4):
                r = slice(32 * j, 32 * j + 32)
                ins = nc.vector.tensor_copy(c_vbd[r, :, j], ps[5][r, 0:2 * HD].rearrange("p (g d) -> p g d", g=2))
            ins.then_inc(sem("cmp_kv_ready"), 1)
            for g in range(2):
                dve.wait_ge(sem("cmp_scores"), g + 1)
                for t in range(TB):
                    neg = cons[:, CON["cmpneg"] + 32 * t:CON["cmpneg"] + 32 * t + 32].unsqueeze(1)
                    ins = nc.vector.tensor_tensor(c_s[:, g, t], ps[6 + g][:, t * P:(t + 1) * P]
                                                  .rearrange("p (h c) -> p h c", h=4), neg.to_broadcast([P, 4, 32]),
                                                  ALU.add)
                chain(ins)
                flat = c_s[:, g].rearrange("p t h c -> p (t h) c")
                chain(nc.vector.tensor_reduce(stat[:, g, 0:16], flat, AX.X, ALU.max))
                nc.vector.tensor_tensor(flat, flat, stat[:, g, 0:16].unsqueeze(2).to_broadcast([P, 16, 32]),
                                        ALU.subtract).then_inc(sem("cmp_centred"), 1)
            dve.wait_ge(sem("gates_turned"), 1)
            for t in range(TB):
                ins = nc.vector.tensor_copy(n_gate[:, t], ps[t % 2][:, t * P + 32:t * P + 56])
            chain(ins)
            for g in range(2):
                dve.wait_ge(sem("cmp_exp"), g + 1)
                for t in range(TB):
                    one = cons[:, CON["cmpone"] + 32 * t:CON["cmpone"] + 32 * t + 32].unsqueeze(1)
                    ins = nc.vector.tensor_tensor(c_e[:, g, t], c_e[:, g, t], one.to_broadcast([P, 4, 32]), ALU.mult)
                chain(ins)
                flat = c_e[:, g].rearrange("p t h c -> p (t h) c")
                chain(nc.vector.tensor_reduce(stat[:, 2 + g, 0:16], flat, AX.X, ALU.add))
                chain(nc.vector.tensor_scalar(stat[:, 4 + g, 0:16], stat[:, 2 + g, 0:16], 1e-30, None, ALU.max))
                chain(nc.vector.reciprocal(stat[:, 6 + g, 0:16] if g == 0 else stat[:, 9, 0:16],
                                           stat[:, 4 + g, 0:16]))
                rec = stat[:, 6, 0:16] if g == 0 else stat[:, 9, 0:16]
                nc.vector.tensor_tensor(flat, flat, rec.unsqueeze(2).to_broadcast([P, 16, 32]), ALU.mult)\
                    .then_inc(sem("cmp_probs"), 1)
            for g in range(2):
                for t in range(TB):
                    i = 4 * g + t
                    dve.wait_ge(sem("cmp_out"), i + 1)
                    gate = n_gate[:, t, 12 * g:12 * g + 12:3].unsqueeze(2).to_broadcast([P, 4, HD])
                    nc.vector.tensor_tensor(n_o[:, t, 4 * g:4 * g + 4],
                                            ps[4 + i % 2][:, 0:256].rearrange("p (h d) -> p h d", h=4), gate,
                                            ALU.mult).then_inc(sem("cmp_out_taken"), 1)
            dve.wait_ge(sem("cmp_out_taken"), 8)
            dve_attention(dve, chain, 0, U_NA, n_o)
            dve_outs(dve, "nsa", 4)
            for k in range(KC):
                dve_split(dve, BASE["mix0_out"] + k)
            dve_rs(dve, 1)
            dve_post(dve, 0, 1)
            dve_rs(dve, 2)
            dve_prep(dve, "prep1", 2)
            dve.wait_ge(sem("acc_zero"), 1)
            dve_ffn(dve, "ffn0")
            dve_rs(dve, 3)
            dve.wait_ge(taken["dve"], READS["dve"][BASE["ffn0"] + 64])
            dve_post(dve, 1, 3)
            dve_rs(dve, 4)
            dve_prep(dve, "prep2", 4)
            B = BASE["sgu_in"]

            def copy_v(i):
                dve.wait_ge(sem("vt_turn"), i + 1)
                nc.vector.tensor_copy(v_tok[:, :, i * P:(i + 1) * P],
                                      ps[6 + i % 2][:, :].rearrange("p (t d) -> p t d", t=TB))\
                    .then_inc(sem("vt_copied"), 1)

            for i in range(2 * KC):
                dve_split(dve, B + i)
                if i >= 1:
                    copy_v(i - 1)
            for i in range(2 * KC):
                dve_split(dve, B + 2 * KC + i)
                if i == 0:
                    copy_v(2 * KC - 1)
                    dve.wait_ge(sem("vt_copied"), 2 * KC)
                if i < TB:
                    for j in range(4):
                        ins = nc.vector.bn_stats(bn[:, i, j], v_tok[:, i, j * T:(j + 1) * T])
                    chain(ins)
                if i == TB:
                    for t in range(TB):
                        chain(nc.vector.bn_aggr(stat[:, 5, 2 * t:2 * t + 2], bn[:, t].rearrange("p j s -> p (j s)")))
                        nc.vector.tensor_copy(stat[:, 0, 2 * t:2 * t + 1], stat[:, 5, 2 * t + 1:2 * t + 2])\
                            .then_inc(sem("vn_var"), 1)
                if i == 7:
                    dve.wait_ge(sem("vn_sd"), 1)
                    chain(nc.vector.reciprocal(stat[:, 2, 0:TB], stat[:, 1, 0:TB]))
                if 7 <= i < 7 + TB:
                    t = i - 7
                    nc.vector.tensor_scalar(v_tok[:, t], v_tok[:, t], stat[:, 5, 2 * t:2 * t + 1],
                                            stat[:, 2, t:t + 1], ALU.subtract, ALU.mult).then_inc(sem("vn_ready"), 1)
            dve.wait_ge(sem("sgu_in"), 32)
            for k in range(2 * KC):
                bank = ps[k % 4] if k < KC else ps[4 + k % 4]
                dve.wait_ge(sem("mixed_v"), k + 1)
                bias = bs[:, (k // 2) * P:(k // 2 + 1) * P].unsqueeze(1).to_broadcast([P, TB, P])
                nc.vector.tensor_tensor(sq[:, k % 2].rearrange("p (t i) -> p t i", t=TB),
                                        bank[:, :].rearrange("p (t i) -> p t i", t=TB), bias, ALU.add)\
                    .then_inc(sem("y_taken"), 1)
                dve.wait_ge(sem("y_taken"), k + 1)
                nc.vector.tensor_tensor(u[:, k], u[:, k], sq[:, k % 2], ALU.mult).then_inc(sem("xf_ready"), 1)
            B = BASE["sgu_out"]
            for k in range(KC):
                dve_split(dve, B + k)
            for k in range(KC):
                dve_split(dve, B + KC + k)
                dve.wait_ge(panel_done, B + KC + k + 1)
                dve.wait_ge(taken["act"], READS["act"][B] + k + 1)
                nc.vector.tensor_tensor(acc[:, k], acc[:, k], ps[(B + KC + k) % 4][:, :], ALU.add)\
                    .then_inc(taken["dve"], 1)
            dve_rs(dve, 5)
            dve.wait_ge(taken["dve"], READS["dve"][B + 16])
            dve_post(dve, 2, 5)
            dve_rs(dve, 6)
            dve_prep(dve, "prep3", 6)
            dve.wait_ge(sem("acc_zero"), 2)
            dve_ffn(dve, "ffn1")
            dve_rs(dve, 7)
            dve.wait_ge(taken["dve"], READS["dve"][BASE["ffn1"] + 64])
            dve_post(dve, 3, 7)
            dve_ln(dve, 0, "ln0", "ln0_g")

            def rope_out(c):
                dve.wait_ge(sem("rope_turn"), c + 1)
                s = HD ** -0.5 if c < 4 else 1.0
                nc.vector.scalar_tensor_tensor(out=rtmp2[:, 0], in0=rtmp[:, c % 2], scalar=s, in1=ropes[:, 0],
                                               op0=ALU.mult, op1=ALU.mult)
                chain(nc.vector.scalar_tensor_tensor(out=rtmp2[:, 1], in0=ps[3][:, :], scalar=s,
                                                     in1=ropes[:, 1], op0=ALU.mult, op1=ALU.mult))
                dst = w_q[:, c] if c < 4 else w_k[:, 0]
                nc.vector.tensor_tensor(dst, rtmp2[:, 0], rtmp2[:, 1], ALU.add).then_inc(sem("rope_out"), 1)
                dve.wait_ge(sem("rope_out"), c + 1)

            for i in range(12):
                n = M2 + i
                dve_split(dve, n)
                if n - 1 in VT:
                    dve_value(dve, n - 1, a_v[:, :, (i - 9) * P:(i - 8) * P])
            dve_value(dve, M2 + 11, a_v[:, :, 3 * P:4 * P])

            def beside(i, first, count):
                if i < NA_UNITS:
                    for b in blocks_beside(i, count, NA_UNITS):
                        if b % KC == 0:
                            dve_split(dve, first + b // KC)

            def beside_na(i):
                beside(i, M2 + 12, 6)
                for c in range(6):
                    if NA_END[c] + 1 != i:
                        continue
                    if c == 0:
                        dve.wait_ge(sem("rope_in"), 16)
                    if c < 5:
                        rope_out(c)
                    else:
                        dve_value(dve, M2 + 17, w_v[:, :, :])

            dve_attention(dve, chain, U_NA, U_SWA, a_o, beside_na)
            dve_outs(dve, "na", 8)
            dve_attention(dve, chain, U_SWA, NU, w_o, lambda i: beside(i, BASE["mix2_gate"], 12))
            for j in (12, 13):
                dve_split(dve, BASE["mix2_gate"] + j)
            dve_outs(dve, "swa", 12)
            for j in (14, 15):
                dve_split(dve, BASE["mix2_gate"] + j)
            for k in range(KC):
                nc.vector.tensor_scalar(h[:, k], h[:, k], ALPHA, col("b_out", k), ALU.mult, ALU.add)\
                    .then_inc(sem("h_scaled"), 1)
            for c in range(KC):
                n = BASE["mix2_branch"] + c
                i = ITEM["mixed"] + c
                dve_split(dve, n)
                dve.wait_ge(panel_done, n + 1)
                dve.wait_ge(taken["act"], READS["act"][n])
                xf_free(dve, i)
                nc.vector.tensor_tensor(sig[:, 2 * c], sig[:, 2 * c], ps[BANK[n]][:, :], ALU.mult)\
                    .then_inc(taken["dve"], 1)
                chain(nc.vector.tensor_tensor(sig[:, 2 * c + 1], sig[:, 2 * c + 1], ps[6 + c % 2][:, :], ALU.mult))
                nc.vector.tensor_tensor(xf[:, i % 4], sig[:, 2 * c], sig[:, 2 * c + 1], ALU.add)\
                    .then_inc(sem("xf_ready"), 1)
                dve.sem_inc(sem("branch_taken"), 1)
            dve.wait_ge(sem("h_scaled"), KC)
            B = BASE["mix2_out"]
            for k in range(KC):
                dve_split(dve, B + k)
                dve.wait_ge(panel_done, B + k + 1)
                nc.vector.tensor_tensor(h[:, k], h[:, k], ps[(B + k) % 4][:, :], ALU.add).then_inc(taken["dve"], 1)
            dve_ln(dve, 1, "ln1", "ln1_g")
            for k in range(KC):
                dve.wait_ge(sem("ln_h"), KC + k + 1)
                ins = nc.vector.tensor_scalar(acc[:, k], h[:, k], ALPHA, col("b_ff2", k), ALU.mult, ALU.add)
            chain(ins)
            dve_ffn(dve, "ffn2")
            dve.wait_ge(taken["dve"], READS["dve"][NP])
            for k in range(KC):
                nc.vector.tensor_copy(h[:, k], acc[:, k]).then_inc(sem("h_final"), 1)
            dve.wait_ge(sem("h_final"), KC)
            dve_ln(dve, 2, None, "ln2_g")


def packed(inputs):
    f = {k: np.asarray(v) for k, v in inputs.items()}

    def panels(w, cols=None):
        w = w if cols is None else w[:, cols]
        n = w.shape[1] // P
        return w.reshape(KC, P, n, P).transpose(2, 1, 0, 3).reshape(n, P, KC * P)

    def paired(first):
        hd = np.arange(8 * HD).reshape(2, 4, HD).transpose(1, 0, 2).reshape(-1)
        return first + hd

    def ffn(w1, w2):
        parts = []
        for g in range(FF // D):
            parts += [panels(w1[:, g * D:(g + 1) * D]), panels(w2[g * D:(g + 1) * D])]
        return parts

    r = np.arange
    w = f["e_w_in"][0]
    misc = np.concatenate([1024 + r(32), 2832 + r(24), 2728 + r(72)])
    even = np.concatenate([misc, r(0, 1024), r(1040, 1552), paired(1552), r(2064, 2832)])
    w2 = f["w_in_2"][0]
    two = np.concatenate([r(0, 1536), paired(1536), r(2048, 2304)])
    gates = np.concatenate([np.concatenate([2304 + c * P + r(P), 3328 + c * P + r(P)]) for c in range(KC)])
    gp = panels(w2, gates)
    branch = panels(np.concatenate([f["w_branch_na_2"][0], f["w_branch_swa_2"][0]], 0))
    ow = f["o_w_out"][0]
    stream = np.concatenate(
        [panels(w, even), panels(f["e_w_out"][0]), *ffn(f["ffn_w1"][0], f["ffn_w2"][0]), panels(f["o_w_in"][0], np.concatenate([2 * D + r(2 * D), r(2 * D)])),
         panels(ow[:D]), panels(ow[D:]), *ffn(f["ffn_w1"][1], f["ffn_w2"][1]), panels(w2, two), gp, branch,
         panels(f["w_out_2"][0]), *ffn(f["w_ff1_2"][0], f["w_ff2_2"][0])])

    def cols(v):
        return v.reshape(-1, P).T

    gate_b = np.zeros((P, 1), np.float32)
    gate_b[32:56, 0] = f["nsa_gate_b"][0]
    b_in = f["b_in_2"][0]
    parts = [f["norm_g"], f["gla_b_gate"], f["gla_norm"], None, f["ln0_g_2"], f["ln0_b_2"], f["ln1_g_2"],
             f["ln1_b_2"], f["ln2_g_2"], f["ln2_b_2"], np.concatenate([b_in[two], b_in[2304:]]), f["b_out_2"],
             f["b_ff1_2"], f["b_ff2_2"]]
    vec = np.concatenate([gate_b if p is None else cols(p) for p in parts]
                         + [np.repeat(f["swa_sink_2"], P, 0)], 1)

    q, k = np.mgrid[0:P, 0:P]
    rot = np.zeros((P, P), np.float32)
    for hd in range(0, P, HD):
        for i in range(ROPE_HALF):
            rot[hd + ROPE_HALF + i, hd + i] = -1.0
            rot[hd + i, hd + ROPE_HALF + i] = 1.0
    scan = (r(T) % GLA_CHUNK != 0).astype(np.float32)[None].repeat(P, 0)
    tok = r(T).reshape(TB, P).T[:, :, None]
    seen = (CMP_STRIDE * r(32) + CMP_BLOCK - 1)[None, None] <= tok
    seen[:, :, N_CMP:] = False
    c = (r(P) % NA_W)[:, None]
    start = np.clip(c - NA_KW // 2, 0, NA_W - NA_KW)
    near = (r(NA_W)[None] >= start) & (r(NA_W)[None] < start + NA_KW)
    one = np.ones((P, 1), np.float32)
    con = np.concatenate([np.eye(P), np.ones((P, P)), rot, np.where(k <= q, 0, NEG), np.where(k >= q, 0, NEG), scan,
                          np.where(seen, 0, NEG).reshape(P, -1), seen.reshape(P, -1), np.where(near, 0, NEG),
                          one * 1e-6, one * 1e-5, one], 1).astype(np.float32)
    inv = np.power(np.float32(500000.0), -np.arange(0, 16, 2, dtype=np.float32) / np.float32(16))
    ang = r(T).astype(np.float32)[:, None] * inv[None]
    rope = np.zeros((P, 2, T), np.float32)
    rope[:, 0] = 1.0
    for hd in range(0, P, HD):
        for half in (0, ROPE_HALF):
            rope[hd + half:hd + half + ROPE_HALF, 0] = np.cos(ang).T
            rope[hd + half:hd + half + ROPE_HALF, 1] = np.sin(ang).T

    pos = np.tile(f["nsa_cmp_pos"][0].transpose(2, 0, 1), (2, 1, 1))
    w1 = f["nsa_cmp_w1"][0].reshape(2, CMP_BLOCK, HD, P).transpose(0, 2, 1, 3)
    w1 = np.tile(w1, (1, 2, 1, 1))
    wide = np.pad(f["na_rpb_2"][0], ((0, 0), (0, 0), (NA_W, NA_W)))
    rpb = np.empty((8, P, 14, NA_W), np.float32)
    for p in range(P):
        row, cc = divmod(p, NA_W)
        a = NA_W + NA_KW - 1 - cc
        rpb[:, p] = wide[:, 1 - row:15 - row, a:a + NA_W]
    return {
        "stream": stream, "x": f["x"][0].T.reshape(KC, P, T).transpose(1, 0, 2), "vec": vec, "con": con, "rope": rope,
        "cmp_pos": pos, "cmp_w1": w1, "cmp_w2": f["nsa_cmp_w2"][0].transpose(1, 0, 2),
        "gate_w": f["gla_w_gate"][0], "ln_gb": np.broadcast_to(np.stack([f["o_ln_g"][0], f["o_ln_b"][0]])[None],
                                                               (P, 2, 2 * D)),
        "w_s": f["o_w_s"][0].transpose(2, 0, 1), "b_s": np.broadcast_to(f["o_b_s"][0].reshape(1, -1), (P, 8 * P)),
        "rpb": rpb.reshape(8, P, 14 * NA_W),
    }


def kernel(**inputs):
    import concourse.bacc as bacc
    from concourse.bass_utils import run_bass_kernel_spmd

    nc = bacc.Bacc("TRN2", target_bir_lowering=False, num_devices=1)
    arrays, args = {}, {}
    for name, a in packed(inputs).items():
        a = np.ascontiguousarray(a)
        arrays[f"in_{name}"] = a
        args[name] = nc.dram_tensor(f"in_{name}", a.shape, F32, kind="ExternalInput").ap()
    out = nc.dram_tensor("out_y", (P, KC, T), F32, kind="ExternalOutput").ap()
    build(nc, out=out, **args)
    r = run_bass_kernel_spmd(nc, [arrays], core_ids=[0])
    y = r.results[0]["out_y"]
    return y.transpose(1, 0, 2).reshape(D, T).T.reshape(1, T, D)
```

```python
from contextlib import ExitStack

import numpy as np

import concourse.bass as bass
from concourse import mybir

F32 = mybir.dt.float32
F32R = mybir.dt.float32r
BF16 = mybir.dt.bfloat16
ACT = mybir.ActivationFunctionType
ALU = mybir.AluOpType
AX = mybir.AxisListType

P = 128
T = 512
TB = T // P
D = 1024
KC = D // P
FF = 4 * D
RING = 4
AHEAD = 3
NEG = -1e30
HD = 64
GLA_CHUNK = 64
CMP_BLOCK, CMP_STRIDE, N_CMP = 32, 16, 31
CMP_STEP = 8
CMP_STEPS = 2 * CMP_BLOCK // CMP_STEP
NA_W, NA_ROWS, NA_KW = 64, 8, 16
ROPE_HALF = 8
ALPHA = float(2.0 ** 0.25)

STAGES = [("mix0_in", 23), ("mix0_gla", 4), ("mix0_nsa", 4), ("ffn0", 64), ("sgu_in", 32), ("sgu_out", 16),
          ("ffn1", 64),
          ("mix2_in", 18), ("mix2_gate", 16), ("mix2_branch", 8),
          ("mix2_out", 8), ("ffn2", 64)]
BASE, NP = {}, 0
for _name, _n in STAGES:
    BASE[_name] = NP
    NP += _n

VEC, NV = {}, 0
for _name, _n in [("norm_g", 64), ("gla_b", 2), ("gla_norm", 4), ("nsa_gate_b", 1), ("ln0_g", 8), ("ln0_b", 8),
                  ("ln1_g", 8), ("ln1_b", 8), ("ln2_g", 8), ("ln2_b", 8), ("b_in", 34), ("b_out", 8),
                  ("b_ff1", 32), ("b_ff2", 8), ("sink", 8)]:
    VEC[_name] = NV
    NV += _n

CON, NC = {}, 0
for _name, _n in [("ident", P), ("ones", P), ("rot", P), ("low", P), ("up", P), ("scan", T), ("cmpneg", TB * 32),
                  ("cmpone", TB * 32), ("nacol", NA_W), ("eps6", 1), ("eps5", 1), ("one", 1)]:
    CON[_name] = NC
    NC += _n

ITEM, NI = {}, 0
for _name, _n in [("gla", 4), ("nsa", 4), ("sgu", 16), ("ln0", 8), ("na", 4), ("swa", 4), ("mixed", 8), ("ln1", 8)]:
    ITEM[_name] = NI
    NI += _n

UNITS = []
for _t in range(TB):
    for _p in range(4):
        for _g in range(2):
            for _k in ("sel", "win"):
                UNITS.append((_k, _g, _p, _t, 0, (_t + 1) * P, 4 * _g + _p))
U_NA = len(UNITS)
for _t in range(TB):
    for _p in range(4):
        for _g in range(2):
            UNITS.append(("na", _g, _p, _t, 0, T, 2 * _p + _g))
U_SWA = len(UNITS)
for _t in range(TB):
    for _p in range(4):
        for _g in range(2):
            _lo, _hi = max(0, _t - 1) * P, min(TB, _t + 2) * P
            UNITS.append(("swa", _g, _p, _t, _lo, _hi - _lo, 4 * _g + _p))
NU = len(UNITS)
UNITS[U_NA:U_SWA] = sorted(UNITS[U_NA:U_SWA], key=lambda u: (u[6], u[3]))


SPREAD = {name: i for i, name in enumerate(["pre0", "post0", "post1", "pre2", "post2", "post3", "mean0", "var0", "mean1",
                                            "var1", "mean2", "var2"])}


def panel_reader(n):
    for name, first, count in [(s, BASE[s], c) for s, c in STAGES]:
        if first <= n < first + count:
            i = n - first
            if name.startswith("ffn"):
                return "act" if i % 16 < 8 else "dve"
            if name == "sgu_in":
                return "dve"
            if name == "sgu_out":
                return "act" if i < 8 else "dve"
            return "dve" if name in ("mix0_in", "mix0_nsa", "mix2_branch", "mix2_out") else "act"
    raise AssertionError(n)


READS = {"act": [0], "dve": [0]}
for _n in range(NP):
    _r = panel_reader(_n)
    for _e in READS:
        READS[_e].append(READS[_e][-1] + (_r == _e))


NA_UNITS = U_SWA - U_NA
BESIDE = set(range(BASE["mix2_in"] + 12, BASE["mix2_branch"]))
BANK = [n % 2 if n in BESIDE else n % 4 for n in range(NP)]
BANKS = [{b} for b in BANK]
for _j in range(4):
    BANKS[BASE["mix0_gla"] + _j] = {0, 1}
    BANKS[BASE["mix0_nsa"] + _j] = {2 * (_j % 2), 2 * (_j % 2) + 1}


def blocks_beside(i, count, units):
    return range(i * count * KC // units, (i + 1) * count * KC // units)


CMP_AT = {"blocks": 4, "hidden": 6, "gelu": 35, "turn": 37, "copy": 38, "kv": 39, "kv_copy": 40}
SCORE_AT = (42, 48)
BLOCK_AT = [3 + b for b in range(KC)] + [11 + 13 * b // 6 for b in range(3 * KC)]
OUT_AT = (54, 57, 60)

NA_END = [next(i for i in range(NA_UNITS) if KC * c + KC - 1 in blocks_beside(i, 6, NA_UNITS)) for c in range(6)]


def build(nc, stream, x, vec, con, rope, cmp_pos, cmp_w1, cmp_w2, gate_w, ln_gb, w_s, b_s, rpb, out):
    with ExitStack() as ctx:
        sems = {}

        def sem(name):
            if name not in sems:
                sems[name] = ctx.enter_context(nc.semaphore(name))
            return sems[name]

        place = [16512]

        def keep(name, shape, dt=F32):
            size = int(np.prod(shape[1:])) * (2 if dt == BF16 else 4)
            size = -(-size // 32) * 32
            t = nc.alloc_sbuf_tensor_at(name, shape, dt, offset=place[0])
            place[0] += size
            return t

        h = keep("h", [P, KC, T])
        xa = keep("xa", [P, KC, 2, T], F32R)
        raw = keep("raw", [P, RING, KC * P])
        ring = keep("ring", [P, RING, 2, KC * P], F32R)
        xf_at = place[0]
        xf = keep("xf", [P, 4, T])
        sq_at = place[0]
        sq = keep("sq", [P, 2, T])
        diag_at = place[0]
        diag = keep("diag", [P, TB, P])
        rs = keep("rs", [P, T])
        misc_at = place[0]
        misc = keep("misc", [P, T])
        part = nc.alloc_sbuf_tensor_at("part", [P, T], F32, offset=misc_at)
        vecs = keep("vecs", [P, NV])
        cons = keep("cons", [P, NC])
        identb = keep("identb", [P, P], BF16)
        lowb = keep("lowb", [P, P], BF16)
        upb = keep("upb", [P, P], BF16)
        stat = keep("stat", [P, 16, 16])
        bn = keep("bn", [P, TB, 4, 6])
        bqa = keep("bqa", [P, 4])
        shared = place[0]

        def at(name, shape, kb, dt=F32):
            assert shared + int(kb * 1024) + int(np.prod(shape[1:])) * 4 <= nc.sbuf_usable_end, name
            return nc.alloc_sbuf_tensor_at(name, shape, dt, offset=shared + int(kb * 1024))

        xb = at("xb", [P, KC, 2, T], 0, F32R)
        acc = at("acc", [P, KC, T], 32)
        relu = at("relu", [P, 2, T], 48)
        ffsq = at("ffsq", [P, 2, T], 52)
        g_at = at("g_at", [P, 4, TB, P], 0)
        g_ke = at("g_ke", [P, 2, TB, 2, P], 8)
        g_v = at("g_v", [P, TB, T], 32)
        g_s = at("g_s", [P, 2 * TB, 2, P], 40)
        g_q = at("g_q", [P, 2, T], 48)
        g_k = at("g_k", [P, 2, T], 52)
        g_b = at("g_b", [P, 2, T], 56)
        g_t = at("g_t", [P, 2, T], 60)
        g_o = at("g_o", [P, TB, T], 56)
        g_r = at("g_r", [P, 4, T], 64)
        n_q = at("n_q", [P, 4, T], 16)
        n_c = at("n_c", [P, 2, T], 72)
        n_k = [[at("n_k00", [P, T], 24), nc.alloc_sbuf_tensor_at("n_k01", [P, T], F32, offset=diag_at)],
               [at("n_k10", [P, T], 26), at("n_k11", [P, T], 82)]]
        n_v = at("n_v", [P, 2, TB, P], 28)
        c_w1 = at("c_w1", [P, 2, CMP_STEP, P], 64)
        c_bl = nc.alloc_sbuf_tensor_at("c_bl", [P, 2, CMP_STEP, 2 * 32], F32, offset=sq_at)
        c_hg = at("c_hg", [HD, 2, P], 81)
        c_s = at("c_s", [P, 2, TB, 4, 32], 64)
        c_e = at("c_e", [P, 2, TB, 4, 32], 68)
        c_pt = at("c_pt", [P, 2, TB, P], 72)
        c_x = at("c_x", [P, 8, HD], 64)
        c_g = at("c_g", [P, 2, 2, 32], 76)
        c_kc = at("c_kc", [P, 32], 76.5)
        c_vbd = at("c_vbd", [P, 2, 4, HD], 76.75)
        c_w2 = at("c_w2", [P, 2, HD], 78.75)
        c_pos = at("c_pos", [P, 2, CMP_BLOCK], 79.25)
        g_wg = at("g_wg", [16, 2 * P], 80)
        n_gate = at("n_gate", [P, TB, 24], 79.5)
        n_p = at("n_p", [P, 2, T], 48)
        n_pt = at("n_pt", [P, 2, T], 52)
        n_o = at("n_o", [P, TB, 8, HD], 56)
        v_tok = at("v_tok", [P, TB, 2 * D], 0)
        gb = at("gb", [P, 2, 2 * D], 32)
        u = at("u", [P, 2 * KC, T], 48)
        wst = at("wst", [P, 8, P], 80)
        bs = nc.alloc_sbuf_tensor_at("bs", [P, 8 * P], F32, offset=xf_at)
        ropes = at("ropes", [P, 2, T], 0)
        rtmp = at("rtmp", [P, 2, T], 4)
        rtmp2 = at("rtmp2", [P, 2, T], 8)
        t2 = at("t2", [P, 2, 14 * NA_W], 16)
        a_o = at("a_o", [P, TB, 8, HD], 24)
        a_q = at("a_q", [P, 4, T], 32)
        a_k = at("a_k", [P, 4, T], 40)
        a_v = at("a_v", [P, TB, T], 48)
        w_q = at("w_q", [P, 4, T], 56)
        w_k = at("w_k", [P, 1, T], 64)
        w_v = at("w_v", [P, TB, P], 66)
        a_p = at("a_p", [P, 2, T], 68)
        a_pt = at("a_pt", [P, 2, T], 72)
        a_s = at("a_s", [P, 2, T], 76)
        w_o = at("w_o", [P, TB, 8, HD], 76)
        sig = at("sig", [P, 2 * KC, T], 32)

        ps = [ctx.enter_context(nc.psum_tensor(f"ps{i}", [P, T], F32)) for i in range(8)]

        ident = cons[:, CON["ident"]:CON["ident"] + P]
        ones = cons[:, CON["ones"]:CON["ones"] + P]

        def col(table, i=0):
            return vecs[:, VEC[table] + i:VEC[table] + i + 1]

        def con_col(name):
            return cons[:, CON[name]:CON[name] + 1]

        landed = [sem(f"landed{s}") for s in range(RING)]
        hi_done, lo_done = sem("hi_done"), sem("lo_done")
        panel_done = sem("panel_done")
        taken = {"act": sem("act_taken"), "dve": sem("dve_taken")}
        setup = sem("setup")

        def act_split(act, n, more=0, panels_more=0):
            m = n + AHEAD
            if m >= NP:
                return
            act.wait_ge(landed[m % RING], 16 * (m // RING + 1) + more)
            if m >= RING:
                act.wait_ge(panel_done, m - RING + 1 + panels_more)
            nc.scalar.activation(ring[:, m % RING, 0], raw[:, m % RING], ACT.Copy).then_inc(hi_done, 1)

        def dve_split(dve, n, more=0):
            m = n + AHEAD
            if m >= NP:
                return
            dve.wait_ge(hi_done, m + 1 + more)
            nc.vector.tensor_tensor(ring[:, m % RING, 1], raw[:, m % RING], ring[:, m % RING, 0].bitcast(F32),
                                    ALU.subtract).then_inc(lo_done, 1)

        def pe_free(pe, n, more=0):
            for bank in sorted(BANKS[n]):
                before = [m for m in range(max(0, n - 8), n) if bank in BANKS[m]]
                if before:
                    r = panel_reader(before[-1])
                    pe.wait_ge(taken[r], READS[r][before[-1] + 1] + more)

        def pe_panel(pe, n, operand, ready=None, more=0, free_more=0, blocks=range(KC), bank=None, free=True,
                     last=True):
            if free:
                pe_free(pe, n, free_more)
            pe.wait_ge(lo_done, n + 1 + more)
            bank = ps[BANK[n]] if bank is None else bank
            blocks = list(blocks)
            for i, k in enumerate(blocks):
                if ready is not None:
                    pe.wait_ge(ready[0], ready[1] + k + 1)
                for w, xx in ((0, 0), (0, 1), (1, 0)):
                    mm = nc.tensor.matmul(bank[:, :], ring[:, n % RING, w, k * P:(k + 1) * P], operand[:, k, xx],
                                          start=(i == 0 and w == 0 and xx == 0),
                                          stop=(i == len(blocks) - 1 and w == 1))
            if last:
                mm.then_inc(panel_done, 1)

        class Chain:

            def __init__(self, eng, name):
                self.eng, self.sem, self.n = eng, sem(name), 0

            def __call__(self, ins):
                self.n += 1
                ins.then_inc(self.sem, 1)
                self.eng.wait_ge(self.sem, self.n)

        def act_item(act, i, dst, src):
            act.wait_ge(sem("xf_ready"), i + 1)
            nc.scalar.activation(dst[:, 0], src, ACT.Copy).then_inc(sem("xhi_ready"), 1)

        def pool_item(pool, i, dst, src):
            pool.wait_ge(sem("xhi_ready"), i + 1)
            nc.gpsimd.tensor_tensor(dst[:, 1], src, dst[:, 0].bitcast(F32), ALU.subtract).then_inc(sem("xlo_ready"), 1)

        def xf_free(dve, i):
            if i >= 4:
                dve.wait_ge(sem("xlo_ready"), i - 3)

        def item_ready(name):
            return (sem("xlo_ready"), ITEM[name])

        def act_square(act, i, k, src):
            if 8 * i + k >= 2:
                act.wait_ge(sem("sq_summed"), 8 * i + k - 1)
            nc.scalar.activation(sq[:, k % 2], src, ACT.Square).then_inc(sem("sq_ready"), 1)

        SD, RC, MEANSQ, R1, R2, R4, RF = 9, 10, 11, 12, 13, 14, 15

        def act_sd(act, i, eps, src=None):
            if src is None:
                act.wait_ge(sem("sq_summed"), 8 * i + KC)
                src = ps[4][:, 0:TB]
            nc.scalar.activation(stat[:, SD, 0:TB], src, ACT.Sqrt, scale=1.0 / D, bias=con_col(eps))\
                .then_inc(sem("sd_ready"), 1)

        def pe_add(pe, src, start=False, stop=False):
            for t in range(TB):
                mm = nc.tensor.matmul(ps[4][:, t:t + 1], src[:, t * P:(t + 1) * P], ones[:, 0:1],
                                      start=(start and t == 0), stop=(stop and t == TB - 1))
            return mm

        def pe_squares(pe, i):
            pe.wait_ge(sem("sq_summed"), 8 * i + 7)
            pe_add(pe, part, start=True)
            pe.wait_ge(sem("sq_ready"), 8 * i + 8)
            pe_add(pe, sq[:, 1], stop=True).then_inc(sem("sq_summed"), 1)

        def pool_squares(pool, i):
            for k in range(1, KC - 1):
                pool.wait_ge(sem("sq_ready"), 8 * i + k + 1)
                pool.wait_ge(sem("sq_summed"), 8 * i + (k if k > 1 else 0))
                nc.gpsimd.tensor_tensor(part[:, :], sq[:, 0] if k == 1 else part[:, :], sq[:, k % 2], ALU.add)\
                    .then_inc(sem("sq_summed"), 2 if k == 1 else 1)

        def pool_variance(pool, m):
            pool.wait_ge(sem("mean_summed"), m + 1)
            for k in range(2, KC, 2):
                pool.wait_ge(sem("var_sq"), 8 * m + k + 1)
                if k > 2:
                    pool.wait_ge(sem("var_even"), 3 * m + k // 2 - 1)
                nc.gpsimd.tensor_tensor(part[:, :], xf[:, 0] if k == 2 else part[:, :], xf[:, k % 4], ALU.add)\
                    .then_inc(sem("var_even"), 1)

        def pool_chunks(pool, m, src, ready):
            for k in range(1, KC - 1):
                pool.wait_ge(*ready(k))
                if k > 1:
                    pool.wait_ge(sem("mean_part"), 6 * m + k - 1)
                nc.gpsimd.tensor_tensor(part[:, :], src[:, 0] if k == 1 else part[:, :], src[:, k], ALU.add)\
                    .then_inc(sem("mean_part"), 1)

        def pe_mean(pe, m, src, ready):
            pe.wait_ge(sem("mean_part"), 6 * (m + 1))
            pe_add(pe, part, start=True)
            pe.wait_ge(*ready(KC - 1))
            pe_add(pe, src[:, KC - 1], stop=True).then_inc(sem("mean_summed"), 1)

        def dve_diag(dve, chain, src):
            for t in range(TB):
                ins = nc.vector.tensor_scalar(diag[:, t], ident, src[:, t:t + 1], None, ALU.mult)
            ins.then_inc(sem("diag_ready"), 1)

        def pe_spread(pe, name):
            pe.wait_ge(sem("diag_ready"), SPREAD[name] + 1)
            for t in range(TB):
                mm = nc.tensor.matmul(ps[5][:, t * P:(t + 1) * P], ones, diag[:, t], start=True, stop=True)
            mm.then_inc(sem("spread"), 1)

        def dve_rms(dve, chain, i, name):
            dve.wait_ge(sem("sd_ready"), i + 1)
            chain(nc.vector.reciprocal(stat[:, RC, 0:TB], stat[:, SD, 0:TB]))
            dve_diag(dve, chain, stat[:, RC, 0:TB])
            dve.wait_ge(sem("spread"), SPREAD[name] + 1)

        def dve_deferred(dve, chain, i):
            dve.wait_ge(sem("sd_ready"), i + 1)
            chain(nc.vector.reciprocal(stat[:, R1, 0:TB], stat[:, SD, 0:TB]))
            chain(nc.vector.tensor_tensor(stat[:, R2, 0:TB], stat[:, R1, 0:TB], stat[:, R1, 0:TB], ALU.mult))
            chain(nc.vector.tensor_tensor(stat[:, R4, 0:TB], stat[:, R2, 0:TB], stat[:, R2, 0:TB], ALU.mult))

        def dve_rms_ffn(dve, chain, i, name):
            dve.wait_ge(sem("sq_summed"), 8 * i + KC)
            nc.vector.tensor_tensor(stat[:, MEANSQ, 0:TB], ps[4][:, 0:TB], stat[:, R4, 0:TB], ALU.mult)\
                .then_inc(sem("corrected"), 1)
            dve.wait_ge(sem("sd_ready"), i + 1)
            chain(nc.vector.reciprocal(stat[:, RF, 0:TB], stat[:, SD, 0:TB]))
            chain(nc.vector.tensor_tensor(stat[:, RC, 0:TB], stat[:, RF, 0:TB], stat[:, R2, 0:TB], ALU.mult))
            dve_diag(dve, chain, stat[:, RC, 0:TB])
            dve.wait_ge(sem("spread"), SPREAD[name] + 1)

        def dve_between(dve, g_post, r, q, g_pre):
            for k in range(KC + 1):
                if k < KC:
                    nc.vector.scalar_tensor_tensor(out=acc[:, k], in0=acc[:, k], scalar=col("norm_g", g_post * KC + k),
                                                   in1=ps[5][:, :], op0=ALU.mult, op1=ALU.mult)\
                        .then_inc(sem("post_ready"), 1)
                if q is not None and k >= 1:
                    dve_pre_lo(dve, q, g_pre, k - 1)
                if k < KC:
                    dve.wait_ge(sem("post_ready"), 8 * r + k + 1)
                    nc.vector.tensor_tensor(h[:, k], h[:, k], acc[:, k], ALU.add).then_inc(sem("h_ready"), 1)

        def dve_pre_lo(dve, q, g, k):
            dve.wait_ge(sem("pre_hi"), 8 * q + k + 1)
            nc.vector.scalar_tensor_tensor(out=xa[:, k, 1], in0=h[:, k], scalar=col("norm_g", g * KC + k),
                                           in1=xa[:, k, 0].bitcast(F32), op0=ALU.mult, op1=ALU.subtract)\
                .then_inc(sem("pre_lo"), 1)

        def act_pre(act, g, k, i):
            nc.scalar.activation(xa[:, k, 0], h[:, k], ACT.Copy, scale=col("norm_g", g * KC + k))\
                .then_inc(sem("pre_hi"), 1)
            act_square(act, i, k, h[:, k])

        def act_between(act, r, g_pre, i):
            for k in range(KC):
                act.wait_ge(sem("h_ready"), 8 * r + k + 1)
                act_pre(act, g_pre, k, i)

        def pe_pair(pe, n, ready):
            pe_free(pe, n)
            pe_free(pe, n + 1)
            pe.wait_ge(lo_done, n + 2)
            for k in range(KC):
                pe.wait_ge(ready[0], ready[1] + k + 1)
                for m in (n, n + 1):
                    for w, xx in ((0, 0), (0, 1), (1, 0)):
                        mm = nc.tensor.matmul(ps[BANK[m]][:, :], ring[:, m % RING, w, k * P:(k + 1) * P],
                                              xa[:, k, xx], start=(k == 0 and w == 0 and xx == 0),
                                              stop=(k == KC - 1 and w == 1))
                    if k == KC - 1:
                        mm.then_inc(panel_done, 1)

        def act_items(act, name, dst, src, n=KC, first=0):
            for k in range(n):
                act_item(act, ITEM[name] + k, dst[:, first + k], src(ITEM[name] + k))

        def pool_items(pool, name, dst, src, n=KC, first=0):
            for k in range(n):
                pool_item(pool, ITEM[name] + k, dst[:, first + k], src(ITEM[name] + k))

        def tile(i):
            return xf[:, i % 4]

        def residual_ready(k):
            return sem("h_ready"), 3 * KC + k + 1

        def mixed_ready(k):
            return taken["dve"], READS["dve"][BASE["mix2_out"]] + k + 1

        def pe_ln(pe, m):
            pe_spread(pe, f"mean{m}")
            for k in range(1, KC, 2):
                pe.wait_ge(sem("var_sq"), 8 * m + k + 1)
                pe_add(pe, xf[:, k % 4], start=k == 1).then_inc(sem("var_odd"), 1)
            pe.wait_ge(sem("var_even"), 3 * (m + 1))
            pe_add(pe, part, stop=True).then_inc(sem("var_summed"), 1)
            pe_spread(pe, f"var{m}")

        def act_ln(act, m):
            for k in range(KC):
                act.wait_ge(sem("centred"), 8 * m + k + 1)
                if k >= 4:
                    act.wait_ge(*((sem("var_odd"), 4 * m + k // 2 - 1) if k % 2 else (sem("var_even"), 3 * m + 1)))
                nc.scalar.activation(xf[:, k % 4], h[:, k], ACT.Square).then_inc(sem("var_sq"), 1)
            act.wait_ge(sem("var_summed"), m + 1)
            act_sd(act, 8 + m, "eps5", ps[4][:, 0:TB])

        def dve_ln(dve, chain, m, name, g, src=h):
            dve.wait_ge(sem("mean_summed"), m + 1)
            chain(nc.vector.tensor_scalar(stat[:, MEANSQ, 0:TB], ps[4][:, 0:TB], 1.0 / D, None, ALU.mult))
            dve_diag(dve, chain, stat[:, MEANSQ, 0:TB])
            dve.wait_ge(sem("spread"), SPREAD[f"mean{m}"] + 1)
            for k in range(KC):
                nc.vector.tensor_tensor(h[:, k], src[:, k], ps[5][:, :], ALU.subtract).then_inc(sem("centred"), 1)
            dve_rms(dve, chain, 8 + m, f"var{m}")
            for k in range(KC):
                i = (ITEM[name] if name else NI) + k
                if name or k < 4:
                    xf_free(dve, i)
                else:
                    dve.wait_ge(sem("y_ready"), k - 3)
                nc.vector.scalar_tensor_tensor(out=xf[:, i % 4], in0=h[:, k], scalar=col(g, k), in1=ps[5][:, :],
                                               op0=ALU.mult, op1=ALU.mult).then_inc(sem("xf_ready"), 1)

        def act_ln_items(act, name, b):
            for k in range(KC):
                i = ITEM[name] + k
                act.wait_ge(sem("xf_ready"), i + 1)
                nc.scalar.activation(h[:, k], tile(i), ACT.Identity, bias=col(b, k)).then_inc(sem("ln_h"), 1)
                nc.scalar.activation(xa[:, k, 0], tile(i), ACT.Identity, bias=col(b, k))\
                    .then_inc(sem("xhi_ready"), 1)

        def ffn_out_ready(s):
            return lambda k: (taken["dve"], READS["dve"][BASE[s]] + 3 * KC + k + 1)

        def pe_ffn(pe, s, ready, norm=None):
            base = BASE[s]
            u0 = sum(4 * KC for q in ("ffn0", "ffn1", "ffn2") if BASE[q] < base)
            pe_pair(pe, base, ready)
            if norm is not None:
                pe_squares(pe, norm)
            for j in range(2, KC):
                pe_panel(pe, base + j, xa)
            for j in range(KC, 2 * KC):
                pe_panel(pe, base + j, xb, (sem("ff_lo"), u0) if j == KC else None)

            def turn(g):
                for j in range(2 * KC):
                    n = base + j
                    if j < 4:
                        pe.wait_ge(taken["dve"], READS["dve"][base] + KC * (g - 1) + 4 + j + 1)
                    else:
                        r = panel_reader(n - 4)
                        pe.wait_ge(taken[r], READS[r][n - 3] + KC * g)
                    pe_panel(pe, n, xa if j < KC else xb,
                             (sem("ff_lo"), u0 + KC * g) if j == KC else None, more=2 * KC * g, free=False)

            with pe.Fori(1, 4) as g:
                turn(g)

        def act_ffn(act, s, bias=None, norm=None):
            base = BASE[s]
            u0 = sum(4 * KC for q in ("ffn0", "ffn1", "ffn2") if BASE[q] < base)

            def turn(g, splits=2 * KC):
                for j in range(2 * KC):
                    if j < splits:
                        act_split(act, base + j, more=64 * g, panels_more=2 * KC * g)
                    if j >= 1 and j <= KC:
                        act.wait_ge(sem("ff_sq"), u0 + j + KC * g)
                        nc.scalar.activation(xb[:, j - 1, 0], ffsq[:, (j - 1) % 2], ACT.Copy)\
                            .then_inc(sem("ff_hi"), 1)
                    if j < KC:
                        act.wait_ge(panel_done, base + j + 1 + 2 * KC * g)
                        b = 0.0 if bias is None else vecs[:, bass.ds(VEC[bias] + j + KC * g, 1)]
                        nc.scalar.activation(relu[:, j % 2], ps[(base + j) % 4][:, :], ACT.Relu, bias=b)\
                            .then_inc(taken["act"], 1)

                    if norm is not None and j > KC and g is last_turn:
                        square(j - KC - 1)

            def square(k):
                act.wait_ge(taken["dve"], READS["dve"][base] + 3 * KC + k + 1)
                act_square(act, norm, k, acc[:, k])

            last_turn = 3
            with act.Fori(0, 3) as g:
                turn(g)
            turn(last_turn, 2 * KC - AHEAD if s == "ffn2" else 2 * KC)
            if norm is not None:
                square(KC - 1)

        def dve_ffn(dve, s):
            base = BASE[s]
            u0 = sum(4 * KC for q in ("ffn0", "ffn1", "ffn2") if BASE[q] < base)

            def turn(g, splits=2 * KC):
                for j in range(2 * KC):
                    if j < splits:
                        dve_split(dve, base + j, more=2 * KC * g)
                    if j < KC:
                        dve.wait_ge(taken["act"], READS["act"][base] + j + 1 + KC * g)
                        nc.vector.tensor_tensor(ffsq[:, j % 2], relu[:, j % 2], relu[:, j % 2], ALU.mult)\
                            .then_inc(sem("ff_sq"), 1)
                        dve.wait_ge(sem("ff_hi"), u0 + j + 1 + KC * g)
                        nc.vector.tensor_tensor(xb[:, j, 1], ffsq[:, j % 2], xb[:, j, 0].bitcast(F32),
                                                ALU.subtract).then_inc(sem("ff_lo"), 1)
                    else:
                        dve.wait_ge(panel_done, base + j + 1 + 2 * KC * g)
                        dve.wait_ge(taken["dve"], READS["dve"][base] + (j - KC) + KC * g)
                        nc.vector.tensor_tensor(acc[:, j - KC], acc[:, j - KC], ps[(base + j) % 4][:, :], ALU.add)\
                            .then_inc(taken["dve"], 1)

            with dve.Fori(0, 4 - (s == "ffn2")) as g:
                turn(g)
            if s == "ffn2":
                turn(3, 2 * KC - AHEAD)

        def operands(u_):
            kind, g, p, t, k0, nk, head = UNITS[u_]
            r = slice(HD * g, HD * g + HD)
            if kind in ("sel", "win"):
                i = int(kind == "win")
                return (n_q[:, p, t * P:(t + 1) * P], n_k[i][g][:, k0:k0 + nk],
                        [n_v[:, i, j, HD * g:HD * g + HD] for j in range(nk // P)])
            if kind == "na":
                return (a_q[r, p, t * P:(t + 1) * P], a_k[r, p, k0:k0 + nk],
                        [a_v[:, j, HD * head:HD * head + HD] for j in range(nk // P)])
            return (w_q[r, p, t * P:(t + 1) * P], w_k[r, 0, k0:k0 + nk],
                    [w_v[:, k0 // P + j, HD * g:HD * g + HD] for j in range(nk // P)])

        def pe_scores(pe, u_):
            kind, g, p, t, k0, nk, head = UNITS[u_]
            q, k, _ = operands(u_)
            if u_ >= 2:
                pe.wait_ge(sem("at_probs"), u_ - 1)
            masks = []
            if kind in ("sel", "win"):
                masks = [(t * P, lowb)]
            if kind == "swa":
                if t > 0:
                    masks.append((0, upb))
                if t < TB - 1:
                    masks.append((nk - P, lowb))
            bank = ps[4 + u_ % 2]
            mm = nc.tensor.matmul(bank[:, 0:nk], q, k, start=True, stop=not masks)
            for i, (c, m) in enumerate(masks):
                mm = nc.tensor.matmul(bank[:, c:c + P], identb[:, :], m[:, :], start=False, stop=i == len(masks) - 1)
            mm.then_inc(sem("at_scores"), 1)

        def pe_turn(pe, u_, probs):
            nk = UNITS[u_][5]
            pe.wait_ge(sem("at_probs"), u_ + 1)
            if u_ >= 2:
                pe.wait_ge(sem("at_turned"), u_ - 1)
            for j in range(nk // P):
                mm = nc.tensor.transpose(ps[6 + u_ % 2][:, j * P:(j + 1) * P], probs[:, u_ % 2, j * P:(j + 1) * P],
                                         ident)
            mm.then_inc(sem("at_turn"), 1)

        def pe_values(pe, u_, turned):
            nk = UNITS[u_][5]
            v = operands(u_)[2]
            pe.wait_ge(sem("at_turned"), u_ + 1)
            if u_ >= 1:
                pe.wait_ge(sem("at_out"), u_)
            for j in range(nk // P):
                mm = nc.tensor.matmul(ps[2][:, 0:HD], turned[:, u_ % 2, j * P:(j + 1) * P], v[j],
                                      start=(j == 0), stop=(j == nk // P - 1))
            mm.then_inc(sem("at_values"), 1)

        def pe_blocks(pe, first, blocks, operand):
            for b in blocks:
                n, k = first + b // KC, b % KC
                if k == 0:
                    pe_free(pe, n)
                    pe.wait_ge(lo_done, n + 1)
                for w, xx in ((0, 0), (0, 1), (1, 0)):
                    mm = nc.tensor.matmul(ps[BANK[n]][:, :], ring[:, n % RING, w, k * P:(k + 1) * P],
                                          operand[:, k, xx], start=(k == 0 and w == 0 and xx == 0),
                                          stop=(k == KC - 1 and w == 1))
                if k == KC - 1:
                    mm.then_inc(panel_done, 1)

        def pe_attention(pe, first, last, probs, turned, beside=None):
            for i in range(first, last + 2):
                if i < last:
                    pe_scores(pe, i)
                if beside is not None:
                    beside(i - first)
                if first <= i - 1 < last:
                    pe_turn(pe, i - 1, probs)
                if i - 2 >= first:
                    pe_values(pe, i - 2, turned)

        NMAX, SUM, SINK, DEN, REC, WGT = range(6)

        def act_attention(act, first, last, probs, turned, beside=None):
            for i in range(first, last + 2):
                if i < last:
                    kind, g, p, t, k0, nk, head = UNITS[i]
                    s = i % 4
                    act.wait_ge(sem("at_max"), i + 1)
                    if i >= 2:
                        act.wait_ge(sem("at_turn"), i - 1)
                    src = a_s[:, i % 2, 0:nk] if kind == "na" else ps[4 + i % 2][:, 0:nk]
                    nc.scalar.activation(probs[:, i % 2, 0:nk], src, ACT.Exp, bias=stat[:, NMAX, s:s + 1],
                                         accum_out=stat[:, SUM, s:s + 1]).then_inc(sem("at_probs"), 1)
                    if kind == "swa":
                        nc.scalar.activation(stat[:, SINK, s:s + 1], col("sink", head), ACT.Exp,
                                             bias=stat[:, NMAX, s:s + 1]).then_inc(sem("at_sink"), 1)
                if first <= i - 1 < last:
                    nk = UNITS[i - 1][5]
                    act.wait_ge(sem("at_turn"), i)
                    if i >= 3:
                        act.wait_ge(sem("at_values"), i - 2)
                    nc.scalar.activation(turned[:, (i - 1) % 2, 0:nk], ps[6 + (i - 1) % 2][:, 0:nk], ACT.Copy)\
                        .then_inc(sem("at_turned"), 1)
                if beside is not None:
                    beside(i - first)

        def dve_attention(dve, chain, first, last, o, beside=None):
            for i in range(first, last + 2):
                if i < last:
                    kind, g, p, t, k0, nk, head = UNITS[i]
                    s = i % 4
                    dve.wait_ge(sem("at_scores"), i + 1)
                    src = ps[4 + i % 2][:, 0:nk]
                    if kind == "na":
                        dve.wait_ge(sem("rpb_masked"), head + 1)
                        if i >= 2:
                            dve.wait_ge(sem("at_probs"), i - 1)
                        c = (7 - 2 * t - 1) * NA_W
                        chain(nc.vector.tensor_tensor(a_s[:, i % 2], src, t2[:, head % 2, c:c + T], ALU.add))
                        src = a_s[:, i % 2]
                        red = nc.vector.tensor_reduce(stat[:, NMAX, s:s + 1], src, AX.X, ALU.max, negate=True)
                        red.then_inc(sem("at_max"), 1)
                    elif kind == "swa":
                        chain(nc.vector.tensor_reduce(stat[:, DEN + 4, s:s + 1], src, AX.X, ALU.max, negate=True))
                        nc.vector.tensor_tensor(stat[:, NMAX, s:s + 1], stat[:, DEN + 4, s:s + 1],
                                                stat[:, 8, 4 + head:5 + head], ALU.min).then_inc(sem("at_max"), 1)
                    else:
                        nc.vector.tensor_reduce(stat[:, NMAX, s:s + 1], src, AX.X, ALU.max, negate=True)\
                            .then_inc(sem("at_max"), 1)
                if i - 2 >= first:
                    w = i - 2
                    kind, g, p, t, k0, nk, head = UNITS[w]
                    s = w % 4
                    dve.wait_ge(sem("at_values"), w + 1)
                    den = stat[:, SUM, s:s + 1]
                    if kind == "swa":
                        dve.wait_ge(sem("at_sink"), w - U_SWA + 1)
                        chain(nc.vector.tensor_tensor(stat[:, DEN, s:s + 1], den, stat[:, SINK, s:s + 1], ALU.add))
                        den = stat[:, DEN, s:s + 1]
                    chain(nc.vector.reciprocal(stat[:, REC, s:s + 1], den))
                    res = ps[2][:, 0:HD]
                    dst = o[:, t, head]
                    if kind in ("sel", "win"):
                        branch = 3 * head + (1 if kind == "sel" else 2)
                        gate = n_gate[:, t, branch:branch + 1]
                        chain(nc.vector.tensor_tensor(stat[:, WGT, s:s + 1], stat[:, REC, s:s + 1], gate, ALU.mult))
                        if kind == "sel":
                            nc.vector.tensor_scalar(dst, res, stat[:, WGT, s:s + 1], None, ALU.mult)\
                                .then_inc(sem("at_out"), 1)
                            if beside is not None:
                                beside(i - first)
                            continue
                        dve.wait_ge(sem("at_out"), w)
                        nc.vector.scalar_tensor_tensor(out=dst, in0=res, scalar=stat[:, WGT, s:s + 1], in1=dst,
                                                       op0=ALU.mult, op1=ALU.add).then_inc(sem("at_out"), 1)
                    else:
                        nc.vector.tensor_scalar(dst, res, stat[:, REC, s:s + 1], None, ALU.mult)\
                            .then_inc(sem("at_out"), 1)
                if beside is not None:
                    beside(i - first)

        def pe_outs(pe, o, count, wait):
            pe.wait_ge(*wait)
            for k in range(4):
                i = count + k
                if i >= 2:
                    pe.wait_ge(sem("xf_out"), i - 1)
                for t in range(TB):
                    mm = nc.tensor.transpose(ps[4 + i % 2][:, t * P:(t + 1) * P], o[:, t, k * P:(k + 1) * P], ident)
                mm.then_inc(sem("outs_turned"), 1)

        def dve_outs(dve, name, count, scale=None):
            for k in range(4):
                i = ITEM[name] + k
                xf_free(dve, i)
                dve.wait_ge(sem("outs_turned"), count + k + 1)
                bank = ps[4 + (count + k) % 2][:, :]
                if scale is None:
                    ins = nc.vector.tensor_copy(xf[:, i % 4], bank)
                else:
                    ins = nc.vector.scalar_tensor_tensor(out=xf[:, i % 4], in0=bank, scalar=scale(k)[0],
                                                         in1=scale(k)[1], op0=ALU.mult, op1=ALU.mult)
                ins.then_inc(sem("xf_ready"), 1)
                dve.wait_ge(sem("xf_ready"), i + 1)
                dve.sem_inc(sem("xf_out"), 1)

        VT = {5: 0, 6: 1, 7: 2, 8: 3, 20: 4, 22: 5}
        VT2 = {BASE["mix2_in"] + 8 + i: 6 + i for i in range(4)} | {BASE["mix2_in"] + 17: 10}
        VT.update(VT2)

        def act_value(act, n, bias=0.0):
            v = VT[n]
            if v >= 2:
                act.wait_ge(sem("v_turn"), v - 1)
            act.wait_ge(panel_done, n + 1)
            nc.scalar.activation(sq[:, v % 2], ps[BANK[n]][:, :], ACT.Identity, bias=bias).then_inc(taken["act"], 1)

        def value_bank(v):
            return ps[3] if v == 10 else ps[6 + v % 2]

        def pe_value(pe, n):
            v = VT[n]
            r = panel_reader(n)
            pe.wait_ge(taken[r], READS[r][n + 1])
            if v >= 2:
                pe.wait_ge(sem("v_done"), v - 1)
            for t in range(TB):
                mm = nc.tensor.transpose(value_bank(v)[:, t * P:(t + 1) * P], sq[:, v % 2, t * P:(t + 1) * P], ident)
            mm.then_inc(sem("v_turn"), 1)

        def dve_value(dve, n, dst):
            v = VT[n]
            dve.wait_ge(sem("v_turn"), v + 1)
            nc.vector.tensor_copy(dst, value_bank(v)[:, :].rearrange("p (t d) -> p t d", t=TB))\
                .then_inc(sem("v_done"), 1)

        M0, M2 = BASE["mix0_in"], BASE["mix2_in"]

        block = ctx.enter_context(nc.Block())

        @block.sync
        def _(sp):
            sp.dma_start(cons[:, :], con).then_inc(setup, 16)
            sp.dma_start(vecs[:, :], vec).then_inc(setup, 16)
            for k in range(KC):
                sp.dma_start(h[:, k], x[:, k]).then_inc(sem(f"x_in{k}"), 16)
                if k in (1, 3):
                    sp.dma_start(raw[:, k // 2], stream[k // 2]).then_inc(landed[k // 2], 16)
            for n in range(2, RING):
                sp.dma_start(raw[:, n], stream[n]).then_inc(landed[n], 16)

            def turn(first):
                for s in range(RING):
                    sp.wait_ge(lo_done, first + s - RING + 1)
                    src = stream[bass.ds(first + s, 1)].rearrange("a p n -> p (a n)")
                    sp.dma_start(raw[:, s], src).then_inc(landed[s], 16)

            with sp.Fori(1, NP // RING) as i:
                turn(RING * i)
            for n in range(NP // RING * RING, NP):
                sp.wait_ge(lo_done, n - RING + 1)
                sp.dma_start(raw[:, n % RING], stream[n]).then_inc(landed[n % RING], 16)
            for k in range(KC):
                sp.wait_ge(sem("y_ready"), k + 1)
                sp.dma_start(out[:, k], h[:, k]).then_inc(sem("stored"), 16)
            sp.wait_ge(sem("stored"), 16 * KC)

        @block.gpsimd
        def _(pool):
            chain = Chain(pool, "pool_chain")
            pool.dma_start(g_wg[:, :], gate_w).then_inc(sem("gate_w_in"), 16)
            pool.dma_start(c_w2[:, :, :], cmp_w2).then_inc(sem("cmp_in"), 16)
            pool.dma_start(c_pos[:, :, :], cmp_pos).then_inc(sem("cmp_in"), 16)
            pool.memset(g_at[:, :, :, :], 0.0)
            pool.memset(g_ke[:, :, :, :, :], 0.0).then_inc(sem("gla_zero"), 1)
            pool_squares(pool, 0)
            pool.memset(c_vbd[:, :, :, :], 0.0).then_inc(sem("cmp_zero"), 1)
            pool.wait_ge(sem("cmp_zero"), 1)
            pool.wait_ge(sem("spread"), SPREAD["pre0"] + 1)
            for i in range(2):
                for g in range(2):
                    if i or g:
                        pool.wait_ge(sem("keys_zero"), 2 * i + g)
                    r = slice(HD * (1 - g), HD * (1 - g) + HD)
                    pool.memset(n_k[i][g][r, :], 0.0).then_inc(sem("keys_zero"), 1)
            pool.wait_ge(sem("gla_scores_out"), 8)
            pool.wait_ge(sem("keys_zero"), 4)
            for r in (0, HD):
                v = g_at[r:r + HD, :, :, r:r + HD].rearrange("p a t i -> p (a t) i")
                pool.affine_select(out=v, in_=v, compare_op=ALU.is_ge, fill=0.0, base=0,
                                   pattern=[[0, 4 * TB], [1, HD]], channel_multiplier=-1)\
                    .then_inc(sem("gla_masked"), 1)

            def load_w1(q):
                i, first = divmod(q * CMP_STEP, CMP_BLOCK)
                pool.dma_start(c_w1[:, q % 2], cmp_w1[i][:, first:first + CMP_STEP])\
                    .then_inc(sem(f"cmp_w1_in{q % 2}"), 16)

            pool_items(pool, "gla", xb, tile, 4)
            load_w1(0)
            load_w1(1)
            pool.wait_ge(sem("v_turn"), 6)
            pool.memset(c_bl[:, :, :, :], 0.0).then_inc(sem("cmp_zero"), 1)
            for q in range(2, CMP_STEPS):
                pool.wait_ge(sem("cmp_hidden"), q - 1)
                load_w1(q)
            pool_items(pool, "nsa", xb, tile, 4, 4)
            pool_squares(pool, 1)
            pool_squares(pool, 2)
            pool.wait_ge(sem("h_ready"), KC)
            pool.memset(acc[:, :, :], 0.0).then_inc(sem("acc_zero"), 1)
            pool_squares(pool, 3)
            pool_squares(pool, 4)
            pool.wait_ge(sem("h_ready"), 2 * KC)
            pool.dma_start(gb[:, :, :], ln_gb).then_inc(sem("sgu_in"), 16)
            pool.dma_start(wst[:, :, :], w_s).then_inc(sem("wst_in"), 16)
            pool.dma_start(bs[:, :], b_s).then_inc(sem("sgu_in"), 16)
            pool.wait_ge(sem("wst_in"), 16)
            pool.affine_select(out=wst[:, :, :], in_=wst[:, :, :], compare_op=ALU.is_ge, fill=0.0, base=0,
                               pattern=[[0, 8], [1, P]], channel_multiplier=-1).then_inc(sem("wst_masked"), 1)
            for t in range(TB):
                pool.wait_ge(sem("vn_ready"), t + 1)
                if t == 0:
                    pool.wait_ge(sem("sgu_in"), 32)
                chain(nc.gpsimd.tensor_tensor(v_tok[:, t], v_tok[:, t], gb[:, 0], ALU.mult))
                nc.gpsimd.tensor_tensor(v_tok[:, t], v_tok[:, t], gb[:, 1], ALU.add).then_inc(sem("v_normed"), 1)
            for k in range(2 * KC):
                i = ITEM["sgu"] + k
                if k == KC:
                    pool.wait_ge(panel_done, BASE["sgu_out"] + KC)
                pool_item(pool, i, xa[:, k % KC], u[:, k])
            pool_squares(pool, 5)
            pool_squares(pool, 6)
            pool.wait_ge(sem("h_ready"), 3 * KC)
            pool.memset(acc[:, :, :], 0.0).then_inc(sem("acc_zero"), 1)
            pool_squares(pool, 7)
            pool_chunks(pool, 0, h, residual_ready)
            pool.wait_ge(panel_done, BASE["ffn1"] + 64)
            pool.dma_start(ropes[:, :, :], rope).then_inc(sem("rope_in"), 16)

            def load_rpb(hd):
                pool.dma_start(t2[:, hd % 2], rpb[hd]).then_inc(sem(f"rpb_in{hd % 2}"), 16)

            load_rpb(0)
            load_rpb(1)
            pool_variance(pool, 0)
            for k in range(KC):
                i = ITEM["ln0"] + k
                pool_item(pool, i, xa[:, k], h[:, k])
            for hd in range(8):
                pool.wait_ge(sem(f"rpb_in{hd % 2}"), 16 * (hd // 2 + 1))
                v = t2[:, hd % 2].rearrange("p (s c) -> p s c", c=NA_W)
                m = cons[:, CON["nacol"]:CON["nacol"] + NA_W].unsqueeze(1).to_broadcast([P, 14, NA_W])
                nc.gpsimd.tensor_tensor(v, v, m, ALU.add).then_inc(sem("rpb_masked"), 1)
                if hd >= 1 and hd + 1 < 8:
                    pool.wait_ge(sem("at_max"), U_NA + 4 * hd)
                    load_rpb(hd + 1)
            pool_items(pool, "na", xb, tile, 4)
            pool_items(pool, "swa", xb, tile, 4, 4)
            for c in range(KC):
                i = ITEM["mixed"] + c
                pool_item(pool, i, xa[:, c], tile(i))
            pool_chunks(pool, 1, h, mixed_ready)
            pool_variance(pool, 1)
            for k in range(KC):
                i = ITEM["ln1"] + k
                pool_item(pool, i, xa[:, k], h[:, k])
            pool_chunks(pool, 2, acc, ffn_out_ready("ffn2"))
            pool_variance(pool, 2)

        @block.tensor
        def _(pe):
            pe.wait_ge(setup, 32)
            pe_pair(pe, M0, (sem("pre_lo"), 0))
            pe_squares(pe, 0)
            def gla_gate_logits():
                pe.wait_ge(sem("gate_w_in"), 16)
                pe.wait_ge(taken["dve"], 1)
                for p in range(2):
                    mm = nc.tensor.matmul(ps[4 + p][:, :], g_wg[:, p * P:(p + 1) * P], misc[0:16, :], start=True,
                                          stop=True)
                    mm.then_inc(sem("gla_gate"), 1)

            def gla_turn_keys(p):
                pe.wait_ge(sem("gla_kend"), p + 1)
                for t in range(TB):
                    mm = nc.tensor.transpose(ps[4 + p][:, t * P:(t + 1) * P], g_t[:, p, t * P:(t + 1) * P], ident)
                mm.then_inc(sem("gla_kturn"), 1)

            def gla_score():
                pe.wait_ge(sem("gla_ke"), 4)
                pe.wait_ge(sem("v_done"), 4)
                for hd in range(4):
                    p, r = hd // 2, slice(HD * (hd % 2), HD * (hd % 2) + HD)
                    pe.wait_ge(sem("gla_kt"), p + 1)
                    for t in range(TB):
                        s = slice(t * P, (t + 1) * P)
                        mm = nc.tensor.matmul(ps[4 + hd][:, s], g_k[r, p, s], g_q[r, p, s], start=True, stop=True)
                    mm.then_inc(sem("gla_scores"), 1)

            def gla_increment(c):
                if c < 2:
                    pe.wait_ge(sem("gla_scores_out"), 2 * c + 2)
                else:
                    pe.wait_ge(sem("gla_state"), c - 1)
                for p in range(2):
                    mm = nc.tensor.matmul(ps[4 + c % 2][:, p * 256:(p + 1) * 256], g_ke[:, p, c // 2, c % 2],
                                          g_v[:, c // 2, p * 256:(p + 1) * 256], start=True, stop=True)
                mm.then_inc(sem("gla_ds"), 1)

            def gla_output(t):
                if t == 0:
                    pe.wait_ge(sem("gla_masked"), 2)
                    pe.wait_ge(sem("gla_state"), 2 * TB - 1)
                for odd in range(2):
                    bank = ps[(6 if t % 2 else 4) + odd]
                    if t >= 2:
                        pe.wait_ge(sem("gla_out_taken"), 2 * (t - 2) + odd + 1)
                    for p in range(2):
                        hd = 2 * p + odd
                        r = slice(HD * odd, HD * odd + HD)
                        dst = bank[:, p * P:(p + 1) * P]
                        mm = nc.tensor.matmul(dst, g_at[:, hd, t], g_v[:, t, hd * P:(hd + 1) * P], start=True,
                                              stop=False)
                        for c2 in range(2):
                            c = 2 * t + c2
                            mm = nc.tensor.matmul(bank[HD * c2:HD * c2 + HD, p * P:(p + 1) * P],
                                                  g_q[r, p, c * HD:(c + 1) * HD], g_s[r, c, p],
                                                  start=False, stop=True)
                    mm.then_inc(sem("gla_out"), 1)

            for i in range(2, 23):
                n = M0 + i
                pe_panel(pe, n, xa)
                if i == 2:
                    pe_spread(pe, "pre0")
                if i == 3:
                    gla_gate_logits()
                if 6 <= i <= 9:
                    pe_value(pe, n - 1)
                if i in (7, 8):
                    gla_turn_keys(i - 7)
                if i == 10:
                    gla_score()
                if 12 <= i <= 15:
                    for c in range(2 * (i - 12), min(2 * (i - 12) + 2, 2 * TB - 1)):
                        gla_increment(c)
                if i in (16, 17):
                    gla_output(2 * (i - 16))
                    gla_output(2 * (i - 16) + 1)
                if i == 19:
                    pe.wait_ge(sem("gla_out_taken"), 2 * TB)
                    pe.wait_ge(sem("gates_ready"), 1)
                    for t in range(TB):
                        mm = nc.tensor.transpose(ps[4][:, t * P:(t + 1) * P], misc[:, t * P:(t + 1) * P], ident)
                    mm.then_inc(sem("gates_turned"), 1)
            pe.wait_ge(sem("gates_out"), 1)
            pe.wait_ge(sem("gla_out_taken"), 2 * TB)
            pe_value(pe, 20)
            pe_outs(pe, g_o, 0, (sem("gla_o_ready"), TB))
            pe_value(pe, 22)

            def gla_out_block(b):
                n, k = BASE["mix0_gla"] + b // KC, b % KC
                if k == 0:
                    pe_free(pe, n)
                    pe.wait_ge(lo_done, n + 1)
                    if b == 0:
                        pe.wait_ge(sem("xlo_ready"), ITEM["gla"] + 4)
                for w, xx in ((0, 0), (0, 1), (1, 0)):
                    mm = nc.tensor.matmul(ps[k // 4][:, :], ring[:, n % RING, w, k * P:(k + 1) * P],
                                          xb[:, k % 4, xx], start=(k % 4 == 0 and w == 0 and xx == 0),
                                          stop=(k % 4 == 3 and w == 1))
                if k == KC - 1:
                    mm.then_inc(panel_done, 1)

            def cmp_hidden(q):
                pe.wait_ge(sem("cmp_blocks"), q + 1)
                pe.wait_ge(sem(f"cmp_w1_in{q % 2}"), 16 * (q // 2 + 1))
                i, first = divmod(q * CMP_STEP, CMP_BLOCK)
                for pos in range(CMP_STEP):
                    mm = nc.tensor.matmul(ps[3][0:HD, i * P:(i + 1) * P], c_bl[:, q % 2, pos], c_w1[:, q % 2, pos],
                                          start=(first + pos == 0), stop=(first + pos == CMP_BLOCK - 1))
                mm.then_inc(sem("cmp_hidden"), 1)

            def cmp_turn():
                pe.wait_ge(sem("cmp_gelu"), 1)
                for i in range(2):
                    mm = nc.tensor.transpose(ps[3][:, i * HD:(i + 1) * HD], c_hg[:, i], ident[0:HD, 0:HD])
                mm.then_inc(sem("cmp_turned"), 1)

            def cmp_kv():
                pe.wait_ge(sem("cmp_copied"), 1)
                for g in range(2):
                    mm = nc.tensor.matmul(ps[3][HD * g:HD * g + HD, 0:32], c_w2[:, 0], c_g[:, 0, g], start=True,
                                          stop=True)
                for g in range(2):
                    for j in range(4):
                        mm = nc.tensor.matmul(ps[3][32 * j:32 * j + 32, P + g * HD:P + (g + 1) * HD], c_g[:, 1, g],
                                              c_w2[:, 1], start=True, stop=True)
                mm.then_inc(sem("cmp_kv"), 1)

            def cmp_score(g):
                if g == 0:
                    pe.wait_ge(sem("cmp_kv_ready"), 1)
                else:
                    pe.wait_ge(sem("cmp_probs_turned"), 1)
                r = slice(HD * g, HD * g + HD)
                for t in range(TB):
                    for j in range(4):
                        mm = nc.tensor.matmul(ps[3][:, (4 * t + j) * 32:(4 * t + j + 1) * 32],
                                              n_q[r, j, t * P:(t + 1) * P], c_kc[r, :], start=True, stop=True)
                mm.then_inc(sem("cmp_scores"), 1)

            def cmp_turn_probs(g):
                pe.wait_ge(sem("cmp_probs"), g + 1)
                for t in range(TB):
                    mm = nc.tensor.transpose(ps[3][:, t * P:(t + 1) * P],
                                             c_e[:, g, t].rearrange("p h c -> p (h c)"), ident)
                mm.then_inc(sem("cmp_probs_turn"), 1)

            def cmp_output(t):
                pe.wait_ge(sem("cmp_probs_turned"), 2)
                if t >= 1:
                    pe.wait_ge(sem("cmp_out_taken"), t)
                for g in range(2):
                    mm = nc.tensor.matmul(ps[3][:, 256 * g:256 * g + 256], c_pt[:, g, t],
                                          c_vbd[:, g].rearrange("p h d -> p (h d)"), start=True, stop=True)
                mm.then_inc(sem("cmp_out"), 1)

            def beside_nsa(i):
                for b in range(4 * KC):
                    if BLOCK_AT[b] == i:
                        gla_out_block(b)
                q, odd = divmod(i - CMP_AT["hidden"], 4)
                if odd == 0 and 0 <= q < CMP_STEPS:
                    cmp_hidden(q)
                if i == CMP_AT["turn"]:
                    cmp_turn()
                if i == CMP_AT["kv"]:
                    cmp_kv()
                for g in range(2):
                    if i == SCORE_AT[g]:
                        cmp_score(g)
                    if i == SCORE_AT[g] + 4:
                        cmp_turn_probs(g)
                if i in OUT_AT:
                    cmp_output(OUT_AT.index(i))

            pe.wait_ge(sem("xf_out"), 4)
            pe.wait_ge(sem("v_done"), 6)
            pe.wait_ge(taken["dve"], READS["dve"][M0 + 23])
            pe_attention(pe, 0, U_NA, n_p, n_pt, beside_nsa)
            cmp_output(TB - 1)
            pe_outs(pe, n_o[:, :, :, :].rearrange("p t h d -> p t (h d)"), 4, (sem("cmp_added"), TB))
            for j in range(4):
                n = BASE["mix0_nsa"] + j
                pe_free(pe, n)
                pe.wait_ge(lo_done, n + 1)
                for k in range(KC):
                    if j == 0 and k < 4:
                        pe.wait_ge(sem("xlo_ready"), ITEM["nsa"] + k + 1)
                    for w, xx in ((0, 0), (0, 1), (1, 0)):
                        mm = nc.tensor.matmul(ps[2 * (j % 2) + k // 4][:, :], ring[:, n % RING, w, k * P:(k + 1) * P],
                                              xb[:, 4 + k % 4, xx], start=(k % 4 == 0 and w == 0 and xx == 0),
                                              stop=(k % 4 == 3 and w == 1))
                mm.then_inc(panel_done, 1)
            pe_squares(pe, 1)
            pe_spread(pe, "post0")
            pe_ffn(pe, "ffn0", (sem("pre_lo"), KC), 2)
            pe_squares(pe, 3)
            pe_spread(pe, "post1")
            B = BASE["sgu_in"]

            def turn_v(i):
                pe.wait_ge(sem("v_gelu"), i + 1)
                if i >= 2:
                    pe.wait_ge(sem("vt_copied"), i - 1)
                for t in range(TB):
                    mm = nc.tensor.transpose(ps[6 + i % 2][:, t * P:(t + 1) * P], sq[:, i % 2, t * P:(t + 1) * P],
                                             ident)
                mm.then_inc(sem("vt_turn"), 1)

            pe_pair(pe, B, (sem("pre_lo"), 2 * KC))
            pe_squares(pe, 4)
            pe_panel(pe, B + 2, xa)
            pe_spread(pe, "pre2")
            for i in range(3, 2 * KC):
                pe_panel(pe, B + i, xa)
                turn_v(i - 3)
            turn_v(2 * KC - 3)
            turn_v(2 * KC - 2)
            pe_panel(pe, B + 2 * KC, xa)
            turn_v(2 * KC - 1)
            for i in range(2 * KC + 1, 2 * KC + RING):
                pe_panel(pe, B + i, xa)
            B += 2 * KC
            with pe.Fori(1, 4) as g:
                for j in range(RING):
                    pe.wait_ge(taken["dve"], READS["dve"][B] + j + 1 + RING * (g - 1))
                    pe_panel(pe, B + j, xa, more=RING * g, free=False)
            pe.wait_ge(sem("wst_masked"), 1)
            pe.wait_ge(sem("v_normed"), TB)
            pe.wait_ge(taken["dve"], READS["dve"][B + 16])
            for k in range(2 * KC):
                bank = ps[k % 4] if k < KC else ps[4 + k % 4]
                if k % KC >= 4:
                    pe.wait_ge(sem("y_taken"), k - 3)
                g = k // 2
                for t in range(TB):
                    mm = nc.tensor.matmul(bank[:, t * P:(t + 1) * P], v_tok[:, t, k * P:(k + 1) * P], wst[:, g],
                                          start=True, stop=True)
                mm.then_inc(sem("mixed_v"), 1)
            pe.wait_ge(sem("y_taken"), KC)
            for half in range(2):
                for k in range(KC):
                    pe_panel(pe, BASE["sgu_out"] + KC * half + k, xa,
                             (sem("xlo_ready"), ITEM["sgu"] + KC * half) if k == 0 else None)
            pe_squares(pe, 5)
            pe_spread(pe, "post2")
            pe_ffn(pe, "ffn1", (sem("pre_lo"), 3 * KC), 6)
            pe_squares(pe, 7)
            pe_spread(pe, "post3")
            pe_mean(pe, 0, h, residual_ready)
            pe_ln(pe, 0)
            pe_pair(pe, M2, item_ready("ln0"))
            for i in range(2, 12):
                n = M2 + i
                pe_panel(pe, n, xa)
                if n - 1 in VT:
                    pe_value(pe, n - 1)
            pe_blocks(pe, M2 + 12, range(0, 2), xa)
            pe_value(pe, M2 + 11)
            pe.wait_ge(sem("v_done"), 10)

            def beside_na(i):
                if i < NA_UNITS:
                    pe_blocks(pe, M2 + 12, [b for b in blocks_beside(i, 6, NA_UNITS) if b >= 2], xa)
                for c in range(6):
                    if NA_END[c] + 1 != i:
                        continue
                    if c == 5:
                        pe.wait_ge(sem("rope_out"), 5)
                        pe_value(pe, M2 + 17)
                        continue
                    pe.wait_ge(taken["act"], READS["act"][M2 + 13 + c])
                    if c >= 1:
                        pe.wait_ge(sem("rope_out"), c)
                    nc.tensor.matmul(ps[3][:, :], cons[:, CON["rot"]:CON["rot"] + P], rtmp[:, c % 2],
                                     start=True, stop=True).then_inc(sem("rope_turn"), 1)

            pe_attention(pe, U_NA, U_SWA, a_p, a_pt, beside_na)
            pe_outs(pe, a_o[:, :, :, :].rearrange("p t h d -> p t (h d)"), 8, (sem("at_out"), U_SWA))
            pe.wait_ge(sem("xf_out"), 12)
            pe.wait_ge(sem("v_done"), 11)
            G2 = BASE["mix2_gate"]
            pe_attention(pe, U_SWA, NU, a_p, a_pt,
                         lambda i: pe_blocks(pe, G2, blocks_beside(i, 12, NA_UNITS), xa) if i < NA_UNITS else None)
            pe_panel(pe, G2 + 12, xa)
            pe_panel(pe, G2 + 13, xa)
            pe_outs(pe, w_o[:, :, :, :].rearrange("p t h d -> p t (h d)"), 12, (sem("at_out"), NU))
            pe_panel(pe, G2 + 14, xa)
            pe_panel(pe, G2 + 15, xa)
            for c in range(KC):
                n = BASE["mix2_branch"] + c
                pe_panel(pe, n, xb, item_ready("na") if c == 0 else None, blocks=range(4), last=False)
                if c >= 2:
                    pe.wait_ge(sem("branch_taken"), c - 1)
                pe_panel(pe, n, xb, item_ready("na") if c == 0 else None, blocks=range(4, 8), free=False,
                         bank=ps[6 + c % 2])
            for k in range(KC):
                pe_panel(pe, BASE["mix2_out"] + k, xa, item_ready("mixed") if k == 0 else None)
            pe_mean(pe, 1, h, mixed_ready)
            pe_ln(pe, 1)
            pe_ffn(pe, "ffn2", item_ready("ln1"))
            pe_mean(pe, 2, acc, ffn_out_ready("ffn2"))
            pe_ln(pe, 2)

        @block.scalar
        def _(act):
            chain = Chain(act, "act_chain")
            act.wait_ge(setup, 32)
            for k in range(KC):
                act.wait_ge(sem(f"x_in{k}"), 16)
                act_pre(act, 0, k, 0)
                if k in (1, 2):
                    act_split(act, k - 1 - AHEAD)
            act_split(act, -1)
            act_sd(act, 0, "eps6")

            def copy_out(n, dst, func=ACT.Copy, **kw):
                act.wait_ge(panel_done, n + 1)
                return nc.scalar.activation(dst, ps[BANK[n]][:, :], func, **kw).then_inc(taken["act"], 1)

            def gla_gates(p):
                act.wait_ge(sem("gla_gate"), p + 1)
                chain(nc.scalar.activation(g_b[:, p], ps[4 + p][:, :], ACT.Identity, bias=col("gla_b", p)))
                chain(nc.scalar.activation(g_t[:, p], g_b[:, p], ACT.Abs))

            def gla_logs():
                for p in range(2):
                    chain(nc.scalar.activation(g_t[:, p], g_t[:, p], ACT.Exp, scale=-1.0))
                for p in range(2):
                    nc.scalar.activation(g_t[:, p], g_t[:, p], ACT.Ln, bias=con_col("one")).then_inc(sem("gla_ln"), 1)

            def gla_exps(p):
                act.wait_ge(sem("gla_cum"), p + 1)
                nc.scalar.activation(xf[:, 2 + p], g_b[:, p], ACT.Exp)
                nc.scalar.activation(xf[:, p], g_b[:, p], ACT.Exp, scale=-1.0)
                act.wait_ge(sem("gla_diff"), p + 1)
                nc.scalar.activation(g_t[:, p], g_t[:, p], ACT.Exp).then_inc(sem("gla_exp"), 1)

            def gla_keys_out(p):
                act.wait_ge(sem("gla_zero"), 1)
                act.wait_ge(sem("gla_kturn"), p + 1)
                for odd in range(2):
                    r = slice(HD * odd, HD * odd + HD)
                    nc.scalar.activation(g_ke[r, p, :, odd], ps[4 + p][r, :].rearrange("p (t d) -> p t d", t=TB),
                                         ACT.Copy).then_inc(sem("gla_ke"), 1)

            def gla_scores_out(hd):
                act.wait_ge(sem("gla_scores"), hd + 1)
                for odd in range(2):
                    r = slice(HD * odd, HD * odd + HD)
                    src = ps[4 + hd][r, :].rearrange("p (t d) -> p t d", t=TB)[:, :, HD * odd:HD * odd + HD]
                    nc.scalar.activation(g_at[r, hd, :, HD * odd:HD * odd + HD], src, ACT.Copy)\
                        .then_inc(sem("gla_scores_out"), 1)

            def gla_out(t):
                for odd in range(2):
                    bank = ps[(6 if t % 2 else 4) + odd]
                    act.wait_ge(sem("gla_out"), 2 * t + odd + 1)
                    dst = g_o[:, t].rearrange("p (q o d) -> p q o d", q=2, o=2)[:, :, odd]
                    nc.scalar.activation(dst, bank[:, 0:256].rearrange("p (q d) -> p q d", q=2), ACT.Copy)\
                        .then_inc(sem("gla_out_taken"), 1)

            for i in range(23):
                n = M0 + i
                act_split(act, n)
                if i == 0:
                    act.wait_ge(taken["dve"], 1)
                    nc.scalar.activation(misc[32:64, :], misc[32:64, :], ACT.Sigmoid,
                                         bias=vecs[32:64, VEC["nsa_gate_b"]:VEC["nsa_gate_b"] + 1])\
                        .then_inc(sem("gates_ready"), 1)
                if 9 <= i < 13:
                    act.wait_ge(taken["dve"], READS["dve"][n + 1])
                    nc.scalar.activation(g_r[:, i - 9], g_r[:, i - 9], ACT.Silu).then_inc(sem("silu_done"), 1)
                if i == 3:
                    gla_gates(0)
                    gla_gates(1)
                if i == 4:
                    gla_logs()
                if i in (5, 6):
                    gla_exps(i - 5)
                if i == 9:
                    gla_keys_out(0)
                    gla_keys_out(1)
                if i in (10, 11):
                    gla_scores_out(2 * (i - 10))
                    gla_scores_out(2 * (i - 10) + 1)
                if i in (16, 17):
                    gla_out(2 * (i - 16))
                    gla_out(2 * (i - 16) + 1)
                if i == 19:
                    act.wait_ge(sem("gla_ssq"), TB)
                    nc.scalar.activation(stat[:, 1, 0:16], stat[:, 0, 0:16], ACT.Sqrt, scale=1.0 / P,
                                         bias=con_col("eps6")).then_inc(sem("gla_sd"), 1)
            act_items(act, "gla", xb, tile, 4)

            def beside_nsa(i):
                for j in range(4):
                    n = BASE["mix0_gla"] + j
                    if BLOCK_AT[KC * j] == i:
                        act_split(act, n)
                    if BLOCK_AT[KC * j + KC - 1] == i:
                        act.wait_ge(panel_done, n + 1)
                        nc.scalar.activation(acc[:, 2 * j], ps[0][:, :], ACT.Copy)
                        nc.scalar.activation(acc[:, 2 * j + 1], ps[1][:, :], ACT.Copy).then_inc(taken["act"], 1)
                if i == CMP_AT["gelu"]:
                    act.wait_ge(sem("cmp_hidden"), CMP_STEPS)
                    nc.scalar.activation(c_hg[:, :, :], ps[3][0:HD, 0:2 * P].rearrange("p (i d) -> p i d", i=2),
                                         ACT.Gelu_apprx_tanh).then_inc(sem("cmp_gelu"), 1)
                for g in range(2):
                    if i == SCORE_AT[g] + 2:
                        act.wait_ge(sem("cmp_centred"), g + 1)
                        nc.scalar.activation(c_e[:, g], c_s[:, g], ACT.Exp).then_inc(sem("cmp_exp"), 1)
                    if i == SCORE_AT[g] + 5:
                        act.wait_ge(sem("cmp_probs_turn"), g + 1)
                        nc.scalar.activation(c_pt[:, g], ps[3][:, :].rearrange("p (t q) -> p t q", t=TB), ACT.Copy)\
                            .then_inc(sem("cmp_probs_turned"), 1)

            act_attention(act, 0, U_NA, n_p, n_pt, beside_nsa)
            act_items(act, "nsa", xb, tile, 4, 4)

            def act_squares_pair(j):
                act.wait_ge(taken["dve"], READS["dve"][BASE["mix0_nsa"] + j + 1])
                act_square(act, 1, 2 * j, acc[:, 2 * j])
                act_square(act, 1, 2 * j + 1, acc[:, 2 * j + 1])

            for j in range(4):
                act_split(act, BASE["mix0_nsa"] + j)
                if j >= 1:
                    act_squares_pair(j - 1)
            act_squares_pair(3)
            act_sd(act, 1, "eps6")
            act_between(act, 0, 2, 2)
            act_sd(act, 2, "eps6")
            act_ffn(act, "ffn0", norm=3)
            act.wait_ge(sem("corrected"), 1)
            act_sd(act, 3, "eps6", stat[:, MEANSQ, 0:TB])
            act_between(act, 1, 4, 4)
            act_sd(act, 4, "eps6")
            B = BASE["sgu_in"]
            for i in range(2 * KC):
                act_split(act, B + i)
                act.wait_ge(taken["dve"], READS["dve"][B + i + 1])
                if i >= 2:
                    act.wait_ge(sem("vt_turn"), i - 1)
                nc.scalar.activation(sq[:, i % 2], xf[:, 2 + i % 2], ACT.Gelu_apprx_tanh).then_inc(sem("v_gelu"), 1)
            for i in range(2 * KC):
                n = B + 2 * KC + i
                act_split(act, n)
                act.wait_ge(taken["dve"], READS["dve"][n + 1])
                nc.scalar.activation(u[:, i], u[:, i], ACT.Gelu_apprx_tanh).then_inc(sem("u_gelu"), 1)
                if i == 5:
                    act.wait_ge(sem("vn_var"), TB)
                    nc.scalar.activation(stat[:, 1, 0:TB], stat[:, 0, 0:2 * TB:2], ACT.Sqrt, bias=con_col("eps6"))\
                        .then_inc(sem("vn_sd"), 1)
            B = BASE["sgu_out"]
            for k in range(KC):
                act_item(act, ITEM["sgu"] + k, xa[:, k], u[:, k])
            for k in range(KC):
                act_split(act, B + k)
                copy_out(B + k, acc[:, k])
            for k in range(KC):
                act_item(act, ITEM["sgu"] + KC + k, xa[:, k], u[:, KC + k])
            for k in range(KC):
                act_split(act, B + KC + k)
                if k >= 1:
                    act.wait_ge(taken["dve"], READS["dve"][B + KC] + k)
                    act_square(act, 5, k - 1, acc[:, k - 1])
            act.wait_ge(taken["dve"], READS["dve"][B + KC] + KC)
            act_square(act, 5, KC - 1, acc[:, KC - 1])
            act_sd(act, 5, "eps6")
            act_between(act, 2, 6, 6)
            act_sd(act, 6, "eps6")
            act_ffn(act, "ffn1", norm=7)
            act.wait_ge(sem("corrected"), 2)
            act_sd(act, 7, "eps6", stat[:, MEANSQ, 0:TB])
            act_ln(act, 0)
            act_ln_items(act, "ln0", "ln0_b")
            for i in range(12):
                n = M2 + i
                act_split(act, n)
                b = col("b_in", i)
                if i < 4:
                    copy_out(n, a_q[:, i], ACT.Identity, bias=bqa[:, i:i + 1], scale=HD ** -0.5)
                elif i < 8:
                    copy_out(n, a_k[:, i - 4], ACT.Identity, bias=b)
                else:
                    act_value(act, n, b)

            def beside(i, first, count, take):
                if i < NA_UNITS:
                    for b in blocks_beside(i, count, NA_UNITS):
                        if b % KC == 0:
                            act_split(act, first + b // KC)
                        if b % KC == KC - 1:
                            take(b // KC)

            def take_swa(c):
                b = col("b_in", 12 + c)
                if c == 5:
                    act_value(act, M2 + 17, b)
                    return
                if c >= 2:
                    act.wait_ge(sem("rope_out"), c - 1)
                copy_out(M2 + 12 + c, rtmp[:, c % 2], ACT.Identity, bias=b)

            def take_gate(j):
                copy_out(BASE["mix2_gate"] + j, sig[:, j], ACT.Sigmoid, bias=col("b_in", 18 + KC * (j % 2) + j // 2))

            act_attention(act, U_NA, U_SWA, a_p, a_pt, lambda i: beside(i, M2 + 12, 6, take_swa))
            act_items(act, "na", xb, tile, 4)
            act_attention(act, U_SWA, NU, a_p, a_pt, lambda i: beside(i, BASE["mix2_gate"], 12, take_gate))
            for j in (12, 13):
                act_split(act, BASE["mix2_gate"] + j)
                take_gate(j)
            act_items(act, "swa", xb, tile, 4, 4)
            for j in (14, 15):
                act_split(act, BASE["mix2_gate"] + j)
                take_gate(j)
            for c in range(KC):
                act_split(act, BASE["mix2_branch"] + c)
                act_item(act, ITEM["mixed"] + c, xa[:, c], tile(ITEM["mixed"] + c))
            for k in range(KC):
                act_split(act, BASE["mix2_out"] + k)
            act_ln(act, 1)
            act_ln_items(act, "ln1", "ln1_b")
            act_ffn(act, "ffn2", "b_ff1")
            act_ln(act, 2)
            for k in range(KC):
                i = NI + k
                act.wait_ge(sem("xf_ready"), i + 1)
                nc.scalar.activation(h[:, k], tile(i), ACT.Identity, bias=col("ln2_b", k)).then_inc(sem("y_ready"), 1)

        @block.vector
        def _(dve):
            chain = Chain(dve, "dve_chain")
            dve.wait_ge(setup, 32)
            for dst, name in ((identb, "ident"), (lowb, "low"), (upb, "up")):
                nc.vector.tensor_copy(dst[:, :], cons[:, CON[name]:CON[name] + P])
            nc.vector.tensor_scalar(stat[:, 8, 4:12], vecs[:, VEC["sink"]:VEC["sink"] + 8], -1.0, None, ALU.mult)
            chain(nc.vector.tensor_scalar(bqa[:, :], vecs[:, VEC["b_in"]:VEC["b_in"] + 4], HD ** -0.5, None,
                                          ALU.mult))
            for k in range(KC):
                dve_pre_lo(dve, 0, 0, k)
                if k in (1, 2):
                    dve_split(dve, k - 1 - AHEAD)
            dve_split(dve, -1)
            dve.wait_ge(sem("sd_ready"), 1)
            chain(nc.vector.reciprocal(stat[:, RC, 0:TB], stat[:, SD, 0:TB]))
            dve_diag(dve, chain, stat[:, RC, 0:TB])
            def gla_decay(p):
                dve.wait_ge(sem("gla_ln"), p + 1)
                chain(nc.vector.scalar_tensor_tensor(out=g_b[:, p], in0=g_b[:, p], scalar=0.0, in1=g_t[:, p],
                                                     op0=ALU.min, op1=ALU.subtract))
                chain(nc.vector.tensor_scalar(g_t[:, p], g_b[:, p], 1.0 / 16.0, None, ALU.mult))
                nc.vector.tensor_tensor_scan(g_b[:, p], cons[:, CON["scan"]:CON["scan"] + T], g_t[:, p], 0.0,
                                             ALU.mult, ALU.add).then_inc(sem("gla_cum"), 1)
                dve.wait_ge(sem("gla_cum"), p + 1)
                bc = g_b[:, p].rearrange("p (c i) -> p c i", i=GLA_CHUNK)
                nc.vector.tensor_tensor(g_t[:, p].rearrange("p (c i) -> p c i", i=GLA_CHUNK),
                                        bc[:, :, GLA_CHUNK - 1:GLA_CHUNK].to_broadcast([P, 2 * TB, GLA_CHUNK]), bc,
                                        ALU.subtract).then_inc(sem("gla_diff"), 1)

            def gla_scale(p):
                dve.wait_ge(sem("gla_exp"), p + 1)
                dve.wait_ge(taken["dve"], 5)
                nc.vector.tensor_tensor(g_t[:, p], g_t[:, p], g_k[:, p], ALU.mult).then_inc(sem("gla_kend"), 1)
                nc.vector.tensor_copy(stat[:, 2 + p, 0:8], xf[:, 2 + p, GLA_CHUNK - 1::GLA_CHUNK])
                dve.wait_ge(sem("gla_kend"), p + 1)
                nc.vector.tensor_tensor(g_q[:, p], g_q[:, p], xf[:, 2 + p], ALU.mult)
                nc.vector.tensor_tensor(g_k[:, p], g_k[:, p], xf[:, p], ALU.mult).then_inc(sem("gla_kt"), 1)

            def gla_step(c):
                dve.wait_ge(sem("gla_ds"), c + 1)
                if c == 0:
                    nc.vector.memset(g_s[:, 0], 0.0)
                    dve.wait_ge(sem("gla_kt"), 2)
                else:
                    dve.wait_ge(sem("gla_state"), c)
                for p in range(2):
                    for odd in range(2):
                        r = slice(HD * odd, HD * odd + HD)
                        src = ps[4 + c % 2][r, (2 * p + odd) * P:(2 * p + odd + 1) * P]
                        if c == 0:
                            ins = nc.vector.tensor_copy(g_s[r, 1, p], src)
                        else:
                            ins = nc.vector.scalar_tensor_tensor(out=g_s[r, c + 1, p], in0=g_s[r, c, p],
                                                                 scalar=stat[r, 2 + p, c:c + 1], in1=src,
                                                                 op0=ALU.mult, op1=ALU.add)
                ins.then_inc(sem("gla_state"), 1)

            def gla_squares(t):
                dve.wait_ge(sem("gla_out_taken"), 2 * t + 2)
                chain(nc.vector.tensor_tensor(xf[:, t % 2], g_o[:, t], g_o[:, t], ALU.mult))
                nc.vector.tensor_reduce(stat[:, 0, 4 * t:4 * t + 4], xf[:, t % 2].rearrange("p (h d) -> p h d", h=4),
                                        AX.X, ALU.add).then_inc(sem("gla_ssq"), 1)

            def gla_norm(t):
                v = g_o[:, t].rearrange("p (h d) -> p h d", h=4)
                nc.vector.tensor_tensor(v, v, stat[:, 4, 4 * t:4 * t + 4].unsqueeze(2).to_broadcast([P, 4, P]),
                                        ALU.mult).then_inc(sem("gla_o_ready"), 1)

            def take(i):
                n = M0 + i
                dve.wait_ge(panel_done, n + 1)
                if n in VT:
                    v = VT[n]
                    if v >= 2:
                        dve.wait_ge(sem("v_turn"), v - 1)
                    dst = sq[:, v % 2]
                elif i == 0:
                    dst = misc[:, :]
                elif i < 5:
                    dst = g_q[:, i - 1] if i < 3 else g_k[:, i - 3]
                elif i < 13:
                    dst = g_r[:, i - 9]
                elif i < 19:
                    dst = n_q[:, i - 13] if i < 17 else n_c[:, i - 17]
                else:
                    for g in range(2):
                        if g == 0 and i == 19:
                            dve.wait_ge(sem("keys_zero"), 4)
                        r = slice(HD * g, HD * g + HD)
                        ins = nc.vector.tensor_tensor(n_k[(i - 19) // 2][g][r, :], ps[BANK[n]][r, :], rs[r, :],
                                                      ALU.mult)
                    ins.then_inc(taken["dve"], 1)
                    return
                if i in (1, 2, 13, 14, 15, 16):
                    ins = nc.vector.scalar_tensor_tensor(out=dst, in0=ps[BANK[n]][:, :], scalar=HD ** -0.5,
                                                         in1=rs[:, :], op0=ALU.mult, op1=ALU.mult)
                else:
                    ins = nc.vector.tensor_tensor(dst, ps[BANK[n]][:, :], rs[:, :], ALU.mult)
                ins.then_inc(taken["dve"], 1)

            for i in range(23):
                n = M0 + i
                dve_split(dve, n)
                if i == 0:
                    dve.wait_ge(sem("spread"), SPREAD["pre0"] + 1)
                    chain(nc.vector.tensor_copy(rs[:, :], ps[5][:, :]))
                take(i)
                if 6 <= i <= 9:
                    dve_value(dve, n - 1, g_v[:, :, (i - 6) * P:(i - 5) * P])
                if i in (4, 5):
                    gla_decay(i - 4)
                if i in (6, 7):
                    gla_scale(i - 6)
                if 12 <= i <= 15:
                    for c in range(2 * (i - 12), min(2 * (i - 12) + 2, 2 * TB - 1)):
                        gla_step(c)
                if i in (17, 18):
                    gla_squares(2 * (i - 17))
                    gla_squares(2 * (i - 17) + 1)
                if i == 19:
                    dve.wait_ge(sem("gates_turned"), 1)
                    for t in range(TB):
                        ins = nc.vector.tensor_copy(n_gate[:, t], ps[4][:, t * P + 32:t * P + 56])
                    chain(ins)
                    dve.sem_inc(sem("gates_out"), 1)
                if i == 20:
                    dve.wait_ge(sem("gla_sd"), 1)
                    chain(nc.vector.reciprocal(stat[:, 4, 0:16], stat[:, 1, 0:16]))
                    for t in range(TB):
                        gla_norm(t)
            dve_value(dve, 20, n_v[:, 0])
            dve.wait_ge(sem("silu_done"), 4)
            dve_outs(dve, "gla", 0, lambda k: (col("gla_norm", k), g_r[:, k]))
            dve_value(dve, 22, n_v[:, 1])

            def cmp_blocks(q):
                if q == 0:
                    dve.wait_ge(sem("cmp_zero"), 2)
                    dve.wait_ge(sem("cmp_in"), 32)
                    dve.wait_ge(taken["dve"], READS["dve"][M0 + 23])
                if q >= 2:
                    dve.wait_ge(sem("cmp_hidden"), q - 1)
                i, first = divmod(q * CMP_STEP, CMP_BLOCK)
                half, at_s = divmod(first, CMP_STRIDE)
                src = n_c[:, i].rearrange("p (c s) -> p s c", s=CMP_STRIDE)
                for g in range(2):
                    r = slice(HD * g, HD * g + HD)
                    ins = nc.vector.tensor_tensor(c_bl[r, q % 2, :, 32 * g:32 * g + N_CMP],
                                                  src[r, at_s:at_s + CMP_STEP, half:half + N_CMP],
                                                  c_pos[r, i, first:first + CMP_STEP].unsqueeze(2)
                                                  .to_broadcast([HD, CMP_STEP, N_CMP]), ALU.add)
                ins.then_inc(sem("cmp_blocks"), 1)

            def cmp_copy():
                dve.wait_ge(sem("cmp_turned"), 1)
                nc.vector.tensor_copy(c_g[:, :, :, :].rearrange("p i g c -> p (i g c)"), ps[3][:, 0:2 * HD])\
                    .then_inc(sem("cmp_copied"), 1)

            def cmp_kv_copy():
                dve.wait_ge(sem("cmp_kv"), 1)
                nc.vector.tensor_copy(c_kc[:, :], ps[3][:, 0:32])
                for j in range(4):
                    r = slice(32 * j, 32 * j + 32)
                    ins = nc.vector.tensor_copy(c_vbd[r, :, j], ps[3][r, P:2 * P].rearrange("p (g d) -> p g d", g=2))
                ins.then_inc(sem("cmp_kv_ready"), 1)

            def cmp_centre(g):
                dve.wait_ge(sem("cmp_scores"), g + 1)
                for t in range(TB):
                    neg = cons[:, CON["cmpneg"] + 32 * t:CON["cmpneg"] + 32 * t + 32].unsqueeze(1)
                    ins = nc.vector.tensor_tensor(c_s[:, g, t], ps[3][:, t * P:(t + 1) * P]
                                                  .rearrange("p (h c) -> p h c", h=4), neg.to_broadcast([P, 4, 32]),
                                                  ALU.add)
                chain(ins)
                flat = c_s[:, g].rearrange("p t h c -> p (t h) c")
                chain(nc.vector.tensor_reduce(stat[:, 7, 0:16], flat, AX.X, ALU.max))
                nc.vector.tensor_tensor(flat, flat, stat[:, 7, 0:16].unsqueeze(2).to_broadcast([P, 16, 32]),
                                        ALU.subtract).then_inc(sem("cmp_centred"), 1)

            def cmp_normalise(g):
                dve.wait_ge(sem("cmp_exp"), g + 1)
                for t in range(TB):
                    one = cons[:, CON["cmpone"] + 32 * t:CON["cmpone"] + 32 * t + 32].unsqueeze(1)
                    ins = nc.vector.tensor_tensor(c_e[:, g, t], c_e[:, g, t], one.to_broadcast([P, 4, 32]), ALU.mult)
                chain(ins)
                flat = c_e[:, g].rearrange("p t h c -> p (t h) c")
                den, kept, rec = (stat[:, row, 0:16] for row in (7, 9, 10))
                chain(nc.vector.tensor_reduce(den, flat, AX.X, ALU.add))
                chain(nc.vector.tensor_scalar(kept, den, 1e-30, None, ALU.max))
                chain(nc.vector.reciprocal(rec, kept))
                nc.vector.tensor_tensor(flat, flat, rec.unsqueeze(2).to_broadcast([P, 16, 32]), ALU.mult)\
                    .then_inc(sem("cmp_probs"), 1)

            def cmp_add(t):
                dve.wait_ge(sem("cmp_out"), t + 1)
                dve.wait_ge(sem("at_out"), 16 * (t + 1))
                if t >= 1:
                    dve.wait_ge(sem("cmp_added"), t)
                gate = n_gate[:, t, 0:24:3].unsqueeze(2).to_broadcast([P, 8, HD])
                nc.vector.tensor_tensor(c_x[:, :, :], ps[3][:, :].rearrange("p (h d) -> p h d", h=8), gate,
                                        ALU.mult).then_inc(sem("cmp_out_taken"), 1)
                dve.wait_ge(sem("cmp_out_taken"), t + 1)
                nc.vector.tensor_tensor(n_o[:, t], n_o[:, t], c_x[:, :, :], ALU.add).then_inc(sem("cmp_added"), 1)

            def beside_nsa(i):
                for j in range(4):
                    if BLOCK_AT[KC * j] == i:
                        dve_split(dve, BASE["mix0_gla"] + j)
                q, odd = divmod(i - CMP_AT["blocks"], 4)
                if odd == 0 and 0 <= q < CMP_STEPS:
                    cmp_blocks(q)
                if i == CMP_AT["copy"]:
                    cmp_copy()
                if i == CMP_AT["kv_copy"]:
                    cmp_kv_copy()
                for g in range(2):
                    if i == SCORE_AT[g] + 1:
                        cmp_centre(g)
                    if i == SCORE_AT[g] + 3:
                        cmp_normalise(g)
                if i - 1 in OUT_AT:
                    cmp_add(OUT_AT.index(i - 1))

            dve_attention(dve, chain, 0, U_NA, n_o, beside_nsa)
            cmp_add(TB - 1)
            dve_outs(dve, "nsa", 4)
            for j in range(4):
                n = BASE["mix0_nsa"] + j
                dve_split(dve, n)
                dve.wait_ge(panel_done, n + 1)
                for k in (2 * j, 2 * j + 1):
                    ins = nc.vector.tensor_tensor(acc[:, k], acc[:, k], ps[2 * (j % 2) + k % 2][:, :], ALU.add)
                ins.then_inc(taken["dve"], 1)
            dve_rms(dve, chain, 1, "post0")
            dve_between(dve, 1, 0, 1, 2)
            dve_deferred(dve, chain, 2)
            dve.wait_ge(sem("acc_zero"), 1)
            dve_ffn(dve, "ffn0")
            dve_rms_ffn(dve, chain, 3, "post1")
            dve_between(dve, 3, 1, 2, 4)
            dve.wait_ge(sem("sd_ready"), 5)
            chain(nc.vector.reciprocal(stat[:, RC, 0:TB], stat[:, SD, 0:TB]))
            dve_diag(dve, chain, stat[:, RC, 0:TB])
            B = BASE["sgu_in"]

            def copy_v(i):
                dve.wait_ge(sem("vt_turn"), i + 1)
                nc.vector.tensor_copy(v_tok[:, :, i * P:(i + 1) * P],
                                      ps[6 + i % 2][:, :].rearrange("p (t d) -> p t d", t=TB))\
                    .then_inc(sem("vt_copied"), 1)

            def take(n, dst):
                dve.wait_ge(panel_done, n + 1)
                nc.vector.tensor_tensor(dst, ps[BANK[n]][:, :], rs[:, :], ALU.mult).then_inc(taken["dve"], 1)

            for i in range(2 * KC):
                dve_split(dve, B + i)
                if i == 0:
                    dve.wait_ge(sem("spread"), SPREAD["pre2"] + 1)
                    chain(nc.vector.tensor_copy(rs[:, :], ps[5][:, :]))
                if i >= 2:
                    dve.wait_ge(sem("v_gelu"), i - 1)
                take(B + i, xf[:, 2 + i % 2])
                if i >= 3:
                    copy_v(i - 3)
            for i in range(2 * KC):
                dve_split(dve, B + 2 * KC + i)
                take(B + 2 * KC + i, u[:, i])
                if i == 0:
                    for j in (3, 2, 1):
                        copy_v(2 * KC - j)
                    dve.wait_ge(sem("vt_copied"), 2 * KC)
                if i < TB:
                    for j in range(4):
                        ins = nc.vector.bn_stats(bn[:, i, j], v_tok[:, i, j * T:(j + 1) * T])
                    chain(ins)
                if i == TB:
                    for t in range(TB):
                        chain(nc.vector.bn_aggr(stat[:, 5, 2 * t:2 * t + 2], bn[:, t].rearrange("p j s -> p (j s)")))
                        nc.vector.tensor_copy(stat[:, 0, 2 * t:2 * t + 1], stat[:, 5, 2 * t + 1:2 * t + 2])\
                            .then_inc(sem("vn_var"), 1)
                if i == 7:
                    dve.wait_ge(sem("vn_sd"), 1)
                    chain(nc.vector.reciprocal(stat[:, 2, 0:TB], stat[:, 1, 0:TB]))
                if 7 <= i < 7 + TB:
                    t = i - 7
                    nc.vector.tensor_scalar(v_tok[:, t], v_tok[:, t], stat[:, 5, 2 * t:2 * t + 1],
                                            stat[:, 2, t:t + 1], ALU.subtract, ALU.mult).then_inc(sem("vn_ready"), 1)
            dve.wait_ge(sem("sgu_in"), 32)
            dve.wait_ge(sem("u_gelu"), 2 * KC)
            for k in range(2 * KC):
                bank = ps[k % 4] if k < KC else ps[4 + k % 4]
                dve.wait_ge(sem("mixed_v"), k + 1)
                bias = bs[:, (k // 2) * P:(k // 2 + 1) * P].unsqueeze(1).to_broadcast([P, TB, P])
                nc.vector.tensor_tensor(sq[:, k % 2].rearrange("p (t i) -> p t i", t=TB),
                                        bank[:, :].rearrange("p (t i) -> p t i", t=TB), bias, ALU.add)\
                    .then_inc(sem("y_taken"), 1)
                dve.wait_ge(sem("y_taken"), k + 1)
                nc.vector.tensor_tensor(u[:, k], u[:, k], sq[:, k % 2], ALU.mult).then_inc(sem("xf_ready"), 1)
            B = BASE["sgu_out"]
            for k in range(KC):
                dve_split(dve, B + k)
            for k in range(KC):
                dve_split(dve, B + KC + k)
                dve.wait_ge(panel_done, B + KC + k + 1)
                dve.wait_ge(taken["act"], READS["act"][B] + k + 1)
                nc.vector.tensor_tensor(acc[:, k], acc[:, k], ps[(B + KC + k) % 4][:, :], ALU.add)\
                    .then_inc(taken["dve"], 1)
            dve_rms(dve, chain, 5, "post2")
            dve_between(dve, 5, 2, 3, 6)
            dve_deferred(dve, chain, 6)
            dve.wait_ge(sem("acc_zero"), 2)
            dve_ffn(dve, "ffn1")
            dve_rms_ffn(dve, chain, 7, "post3")
            dve_between(dve, 7, 3, None, None)
            dve_ln(dve, chain, 0, "ln0", "ln0_g")

            def rope_out(c):
                dve.wait_ge(sem("rope_turn"), c + 1)
                s = HD ** -0.5 if c < 4 else 1.0
                nc.vector.scalar_tensor_tensor(out=rtmp2[:, 0], in0=rtmp[:, c % 2], scalar=s, in1=ropes[:, 0],
                                               op0=ALU.mult, op1=ALU.mult)
                chain(nc.vector.scalar_tensor_tensor(out=rtmp2[:, 1], in0=ps[3][:, :], scalar=s,
                                                     in1=ropes[:, 1], op0=ALU.mult, op1=ALU.mult))
                dst = w_q[:, c] if c < 4 else w_k[:, 0]
                nc.vector.tensor_tensor(dst, rtmp2[:, 0], rtmp2[:, 1], ALU.add).then_inc(sem("rope_out"), 1)
                dve.wait_ge(sem("rope_out"), c + 1)

            for i in range(12):
                n = M2 + i
                dve_split(dve, n)
                if n - 1 in VT:
                    dve_value(dve, n - 1, a_v[:, :, (i - 9) * P:(i - 8) * P])
            dve_value(dve, M2 + 11, a_v[:, :, 3 * P:4 * P])

            def beside(i, first, count):
                if i < NA_UNITS:
                    for b in blocks_beside(i, count, NA_UNITS):
                        if b % KC == 0:
                            dve_split(dve, first + b // KC)

            def beside_na(i):
                beside(i, M2 + 12, 6)
                for c in range(6):
                    if NA_END[c] + 1 != i:
                        continue
                    if c == 0:
                        dve.wait_ge(sem("rope_in"), 16)
                    if c < 5:
                        rope_out(c)
                    else:
                        dve_value(dve, M2 + 17, w_v[:, :, :])

            dve_attention(dve, chain, U_NA, U_SWA, a_o, beside_na)
            dve_outs(dve, "na", 8)
            dve_attention(dve, chain, U_SWA, NU, w_o, lambda i: beside(i, BASE["mix2_gate"], 12))
            for j in (12, 13):
                dve_split(dve, BASE["mix2_gate"] + j)
            dve_outs(dve, "swa", 12)
            for j in (14, 15):
                dve_split(dve, BASE["mix2_gate"] + j)
            for k in range(KC):
                nc.vector.tensor_scalar(h[:, k], h[:, k], ALPHA, col("b_out", k), ALU.mult, ALU.add)\
                    .then_inc(sem("h_scaled"), 1)
            for c in range(KC):
                n = BASE["mix2_branch"] + c
                i = ITEM["mixed"] + c
                dve_split(dve, n)
                dve.wait_ge(panel_done, n + 1)
                dve.wait_ge(taken["act"], READS["act"][n])
                xf_free(dve, i)
                nc.vector.tensor_tensor(sig[:, 2 * c], sig[:, 2 * c], ps[BANK[n]][:, :], ALU.mult)\
                    .then_inc(taken["dve"], 1)
                chain(nc.vector.tensor_tensor(sig[:, 2 * c + 1], sig[:, 2 * c + 1], ps[6 + c % 2][:, :], ALU.mult))
                nc.vector.tensor_tensor(xf[:, i % 4], sig[:, 2 * c], sig[:, 2 * c + 1], ALU.add)\
                    .then_inc(sem("xf_ready"), 1)
                dve.sem_inc(sem("branch_taken"), 1)
            dve.wait_ge(sem("h_scaled"), KC)
            B = BASE["mix2_out"]
            for k in range(KC):
                dve_split(dve, B + k)
                dve.wait_ge(panel_done, B + k + 1)
                nc.vector.tensor_tensor(h[:, k], h[:, k], ps[(B + k) % 4][:, :], ALU.add).then_inc(taken["dve"], 1)
            dve_ln(dve, chain, 1, "ln1", "ln1_g")
            for k in range(KC):
                dve.wait_ge(sem("ln_h"), KC + k + 1)
                ins = nc.vector.tensor_scalar(acc[:, k], h[:, k], ALPHA, col("b_ff2", k), ALU.mult, ALU.add)
            chain(ins)
            dve_ffn(dve, "ffn2")
            dve_ln(dve, chain, 2, None, "ln2_g", acc)


def packed(inputs):
    f = {k: np.asarray(v) for k, v in inputs.items()}

    def panels(w, cols=None):
        w = w if cols is None else w[:, cols]
        n = w.shape[1] // P
        return w.reshape(KC, P, n, P).transpose(2, 1, 0, 3).reshape(n, P, KC * P)

    def halves(w):
        return w.reshape(4, P, 4, 2, P).transpose(2, 1, 3, 0, 4).reshape(4, P, KC * P)

    def paired(first):
        hd = np.arange(8 * HD).reshape(2, 4, HD).transpose(1, 0, 2).reshape(-1)
        return first + hd

    def ffn(w1, w2):
        parts = []
        for g in range(FF // D):
            parts += [panels(w1[:, g * D:(g + 1) * D]), panels(w2[g * D:(g + 1) * D])]
        return parts

    r = np.arange
    w = f["e_w_in"][0]
    misc = np.concatenate([1024 + r(32), 2832 + r(24), 2728 + r(72)])
    even = np.concatenate([misc, r(0, 1024), r(1040, 1552), paired(1552), r(2064, 2832)])
    w2 = f["w_in_2"][0]
    two = np.concatenate([r(0, 1536), paired(1536), r(2048, 2304)])
    gates = np.concatenate([np.concatenate([2304 + c * P + r(P), 3328 + c * P + r(P)]) for c in range(KC)])
    gp = panels(w2, gates)
    branch = panels(np.concatenate([f["w_branch_na_2"][0], f["w_branch_swa_2"][0]], 0))
    ow = f["o_w_out"][0]
    stream = np.concatenate(
        [panels(w, even), halves(f["e_w_out"][0][:512]), halves(f["e_w_out"][0][512:]),
         *ffn(f["ffn_w1"][0], f["ffn_w2"][0]), panels(f["o_w_in"][0], np.concatenate([2 * D + r(2 * D), r(2 * D)])),
         panels(ow[:D]), panels(ow[D:]), *ffn(f["ffn_w1"][1], f["ffn_w2"][1]), panels(w2, two), gp, branch,
         panels(f["w_out_2"][0]), *ffn(f["w_ff1_2"][0], f["w_ff2_2"][0])])

    def cols(v):
        return v.reshape(-1, P).T

    gate_b = np.zeros((P, 1), np.float32)
    gate_b[32:56, 0] = f["nsa_gate_b"][0]
    b_in = f["b_in_2"][0]
    parts = [f["norm_g"], f["gla_b_gate"], f["gla_norm"], None, f["ln0_g_2"], f["ln0_b_2"], f["ln1_g_2"],
             f["ln1_b_2"], f["ln2_g_2"], f["ln2_b_2"], np.concatenate([b_in[two], b_in[2304:]]), f["b_out_2"],
             f["b_ff1_2"], f["b_ff2_2"]]
    vec = np.concatenate([gate_b if p is None else cols(p) for p in parts]
                         + [np.repeat(f["swa_sink_2"], P, 0)], 1)

    q, k = np.mgrid[0:P, 0:P]
    rot = np.zeros((P, P), np.float32)
    for hd in range(0, P, HD):
        for i in range(ROPE_HALF):
            rot[hd + ROPE_HALF + i, hd + i] = -1.0
            rot[hd + i, hd + ROPE_HALF + i] = 1.0
    scan = (r(T) % GLA_CHUNK != 0).astype(np.float32)[None].repeat(P, 0)
    tok = r(T).reshape(TB, P).T[:, :, None]
    seen = (CMP_STRIDE * r(32) + CMP_BLOCK - 1)[None, None] <= tok
    seen[:, :, N_CMP:] = False
    c = (r(P) % NA_W)[:, None]
    start = np.clip(c - NA_KW // 2, 0, NA_W - NA_KW)
    near = (r(NA_W)[None] >= start) & (r(NA_W)[None] < start + NA_KW)
    one = np.ones((P, 1), np.float32)
    con = np.concatenate([np.eye(P), np.ones((P, P)), rot, np.where(k <= q, 0, NEG), np.where(k >= q, 0, NEG), scan,
                          np.where(seen, 0, NEG).reshape(P, -1), seen.reshape(P, -1), np.where(near, 0, NEG),
                          one * 1e-6, one * 1e-5, one], 1).astype(np.float32)
    inv = np.power(np.float32(500000.0), -np.arange(0, 16, 2, dtype=np.float32) / np.float32(16))
    ang = r(T).astype(np.float32)[:, None] * inv[None]
    rope = np.zeros((P, 2, T), np.float32)
    rope[:, 0] = 1.0
    for hd in range(0, P, HD):
        for half in (0, ROPE_HALF):
            rope[hd + half:hd + half + ROPE_HALF, 0] = np.cos(ang).T
            rope[hd + half:hd + half + ROPE_HALF, 1] = np.sin(ang).T

    pos = np.tile(f["nsa_cmp_pos"][0].transpose(2, 0, 1), (2, 1, 1))
    w1 = f["nsa_cmp_w1"][0].reshape(2, CMP_BLOCK, HD, P).transpose(0, 2, 1, 3)
    w1 = np.tile(w1, (1, 2, 1, 1))
    wide = np.pad(f["na_rpb_2"][0], ((0, 0), (0, 0), (NA_W, NA_W)))
    rpb = np.empty((8, P, 14, NA_W), np.float32)
    for p in range(P):
        row, cc = divmod(p, NA_W)
        a = NA_W + NA_KW - 1 - cc
        rpb[:, p] = wide[:, 1 - row:15 - row, a:a + NA_W]
    return {
        "stream": stream, "x": f["x"][0].T.reshape(KC, P, T).transpose(1, 0, 2), "vec": vec, "con": con, "rope": rope,
        "cmp_pos": pos, "cmp_w1": w1, "cmp_w2": f["nsa_cmp_w2"][0].transpose(1, 0, 2),
        "gate_w": f["gla_w_gate"][0], "ln_gb": np.broadcast_to(np.stack([f["o_ln_g"][0], f["o_ln_b"][0]])[None],
                                                               (P, 2, 2 * D)),
        "w_s": f["o_w_s"][0].transpose(2, 0, 1), "b_s": np.broadcast_to(f["o_b_s"][0].reshape(1, -1), (P, 8 * P)),
        "rpb": rpb.reshape(8, P, 14 * NA_W),
    }


def kernel(**inputs):
    import concourse.bacc as bacc
    from concourse.bass_utils import run_bass_kernel_spmd

    nc = bacc.Bacc("TRN2", target_bir_lowering=False, num_devices=1)
    arrays, args = {}, {}
    for name, a in packed(inputs).items():
        a = np.ascontiguousarray(a)
        arrays[f"in_{name}"] = a
        args[name] = nc.dram_tensor(f"in_{name}", a.shape, F32, kind="ExternalInput").ap()
    out = nc.dram_tensor("out_y", (P, KC, T), F32, kind="ExternalOutput").ap()
    build(nc, out=out, **args)
    r = run_bass_kernel_spmd(nc, [arrays], core_ids=[0])
    y = r.results[0]["out_y"]
    return y.transpose(1, 0, 2).reshape(D, T).T.reshape(1, T, D)
```
